# Optimizing a Trainium2 kernel written in Bass

```python
import math
import jax, jax.numpy as jnp
from jax import lax
import numpy as np

D_MODEL = 1024
BATCH = 1
SEQ = 256
DEPTH = 2

N_BRANCH = 4
A_HEADS = 4
A_HEAD_DIM = 128
A_WIDTH = A_HEADS * A_HEAD_DIM
IDX_HEADS = 4
IDX_DIM = 64
TOPK_MAX = 256
CB_WIDTH = 512
CB_CONV = 31
CC_WIDTH = 512
CC_CONV = 3
SB_HEADS = 4
SB_HEAD_DIM = 128
SB_WIDTH = SB_HEADS * SB_HEAD_DIM
D_FF = 2816
FFN_CONV = 3
ROPE_THETA = 500000.0
ROT_FRACTION_DIV = 4
BLOCK_Q = 128
NORM_EPS = 1e-6

SPLIT_SIZES = (A_WIDTH, A_WIDTH, A_WIDTH, IDX_HEADS * IDX_DIM, IDX_DIM, IDX_HEADS,
               2 * CB_WIDTH, 3 * CC_WIDTH, 3 * SB_WIDTH, N_BRANCH * D_MODEL)
N_IN = sum(SPLIT_SIZES)


def _split_offsets(sizes):
    offs, acc = [], 0
    for s in sizes[:-1]:
        acc += s
        offs.append(acc)
    return offs

def rms_norm(x, g):
    xf = x.astype(jnp.float32)
    y = xf * lax.rsqrt(jnp.mean(xf * xf, axis=-1, keepdims=True) + NORM_EPS)
    return (y * g.astype(jnp.float32)).astype(x.dtype)

def layer_norm(x, g, b):
    xf = x.astype(jnp.float32)
    mu = jnp.mean(xf, axis=-1, keepdims=True)
    xc = xf - mu
    y = xc * lax.rsqrt(jnp.mean(xc * xc, axis=-1, keepdims=True) + NORM_EPS)
    return (y * g.astype(jnp.float32) + b.astype(jnp.float32)).astype(x.dtype)

def partial_rope(x, pos):
    d = x.shape[-1]
    rot = d // ROT_FRACTION_DIV
    half = rot // 2
    inv_freq = ROPE_THETA ** (-(jnp.arange(half, dtype=jnp.float32) * 2.0) / rot)
    ang = pos.astype(jnp.float32)[..., None] * inv_freq
    cos = jnp.cos(ang)[:, :, None, :]
    sin = jnp.sin(ang)[:, :, None, :]
    xf = x.astype(jnp.float32)
    x1, x2 = xf[..., :half], xf[..., half:rot]
    out = jnp.concatenate([x1 * cos - x2 * sin, x2 * cos + x1 * sin, xf[..., rot:]], axis=-1)
    return out.astype(x.dtype)

def causal_dwconv(x, w, b=None):
    width = w.shape[0]
    y = lax.conv_general_dilated(
        x, w.astype(x.dtype)[:, None, :], window_strides=(1,), padding=[(width - 1, 0)],
        dimension_numbers=('NWC', 'WIO', 'NWC'), feature_group_count=x.shape[-1])
    if b is not None:
        y = y + b.astype(x.dtype)
    return y

def _to_blocks(a, nb):
    return jnp.moveaxis(a.reshape((a.shape[0], nb, BLOCK_Q) + a.shape[2:]), 1, 0)

def _from_blocks(a):
    a = jnp.moveaxis(a, 0, 1)
    return a.reshape(a.shape[0], -1, a.shape[-2] * a.shape[-1])

def dsa_attention(q, k, v, q_idx, k_idx, w_idx):
    bsz, seq = q.shape[0], q.shape[1]
    nb = seq // BLOCK_Q
    k_sel = min(TOPK_MAX, seq // 4)
    kv = jnp.stack([k, v], axis=2)
    s_idx = jnp.arange(seq)
    k_idx_f = k_idx.astype(jnp.float32)

    def block(args):
        qb, qib, wb, tb = args
        rel = jax.nn.relu(jnp.einsum('bthd,bsd->bths', qib.astype(jnp.float32), k_idx_f) * IDX_DIM ** -0.5)
        score = jnp.einsum('bths,bth->bts', rel, wb.astype(jnp.float32)) * IDX_HEADS ** -0.5
        causal = s_idx[None, :] <= tb[:, None]
        score = jnp.where(causal[None], score, -jnp.inf)
        _, sel = lax.top_k(score, k_sel)
        valid = sel <= tb[None, :, None]
        kv_sel = jax.vmap(lambda a, i: a[i])(kv, sel)
        logits = jnp.einsum('bthd,btkhd->bthk', qb.astype(jnp.float32),
                            kv_sel[:, :, :, 0].astype(jnp.float32)) * A_HEAD_DIM ** -0.5
        logits = jnp.where(valid[:, :, None, :], logits, -jnp.inf)
        p = jax.nn.softmax(logits, axis=-1)
        out = jnp.einsum('bthk,btkhd->bthd', p, kv_sel[:, :, :, 1].astype(jnp.float32))
        return out.astype(qb.dtype)

    t_blocks = jnp.arange(seq).reshape(nb, BLOCK_Q)
    out = lax.map(block, (_to_blocks(q, nb), _to_blocks(q_idx, nb), _to_blocks(w_idx, nb), t_blocks))
    return _from_blocks(out)

def stick_breaking_attention(q, k, v):
    seq = q.shape[1]
    nb = seq // BLOCK_Q
    s_idx = jnp.arange(seq)
    k_f = k.astype(jnp.float32)
    v_f = v.astype(jnp.float32)

    def block(args):
        qb, tb = args
        z = jnp.einsum('bthd,bshd->bhts', qb.astype(jnp.float32), k_f) * SB_HEAD_DIM ** -0.5
        mask = (s_idx[None, :] < tb[:, None])[None, None]
        log_keep = jnp.where(mask, jax.nn.log_sigmoid(-z), 0.0)
        between = lax.cumsum(log_keep, axis=3, reverse=True) - log_keep
        a = jnp.where(mask, jnp.exp(jax.nn.log_sigmoid(z) + between), 0.0)
        return jnp.einsum('bhts,bshd->bthd', a, v_f).astype(qb.dtype)

    t_blocks = jnp.arange(seq).reshape(nb, BLOCK_Q)
    out = lax.map(block, (_to_blocks(q, nb), t_blocks))
    return _from_blocks(out)

def first_inputs(seed: int = 0) -> dict:
    key = jax.random.key(seed)
    ks = jax.random.split(key, 24)
    f32 = jnp.float32

    def nrm(k, shape, scale):
        return jax.random.normal(k, shape, f32) * scale

    def gain(k, shape):
        return 1.0 + 0.05 * jax.random.normal(k, shape, f32)

    L, D = DEPTH, D_MODEL
    return {
        "x": jax.random.normal(ks[0], (BATCH, SEQ, D), f32),
        "positions": jnp.broadcast_to(jnp.arange(SEQ, dtype=jnp.int32), (BATCH, SEQ)),
        "g_mix": gain(ks[1], (L, D)),
        "w_in": nrm(ks[2], (L, D, N_IN), D ** -0.5),
        "b_gate": nrm(ks[3], (L, N_BRANCH * D), 0.1),
        "g_qa": gain(ks[4], (L, A_HEAD_DIM)),
        "g_ka": gain(ks[5], (L, A_HEAD_DIM)),
        "g_kidx": gain(ks[6], (L, IDX_DIM)),
        "w_oa": nrm(ks[7], (L, A_WIDTH, D), A_WIDTH ** -0.5),
        "cb_conv_w": nrm(ks[8], (L, CB_CONV, CB_WIDTH), CB_CONV ** -0.5),
        "cb_conv_b": nrm(ks[9], (L, CB_WIDTH), 0.02),
        "cb_ln_g": gain(ks[10], (L, CB_WIDTH)),
        "cb_ln_b": nrm(ks[11], (L, CB_WIDTH), 0.02),
        "w_ob": nrm(ks[12], (L, CB_WIDTH, D), CB_WIDTH ** -0.5),
        "cc_conv_w": nrm(ks[13], (L, CC_CONV, CC_WIDTH), CC_CONV ** -0.5),
        "w_oc": nrm(ks[14], (L, CC_WIDTH, D), CC_WIDTH ** -0.5),
        "w_od": nrm(ks[15], (L, SB_WIDTH, D), SB_WIDTH ** -0.5),
        "w_merge": nrm(ks[16], (L, D, D), D ** -0.5),
        "g_ffn": gain(ks[17], (L, D)),
        "w_ffn_gate": nrm(ks[18], (L, D, D_FF), D ** -0.5),
        "w_ffn_up": nrm(ks[19], (L, D, D_FF), D ** -0.5),
        "ffn_conv_w": nrm(ks[20], (L, FFN_CONV, D_FF), FFN_CONV ** -0.5),
        "w_ffn_down": nrm(ks[21], (L, D_FF, D), D_FF ** -0.5),
    }

def first_block(x, positions, g_mix, w_in, b_gate, g_qa, g_ka, g_kidx, w_oa,
              cb_conv_w, cb_conv_b, cb_ln_g, cb_ln_b, w_ob, cc_conv_w, w_oc, w_od,
              w_merge, g_ffn, w_ffn_gate, w_ffn_up, ffn_conv_w, w_ffn_down):
    bsz, seq, dm = x.shape
    offs = _split_offsets(SPLIT_SIZES)
    for l in range(DEPTH):
        h = rms_norm(x, g_mix[l])
        proj = h @ w_in[l]
        aq, ak, av, iq, ik, iw, glu_in, cc_in, sb_in, gate_in = jnp.split(proj, offs, axis=-1)

        qa = partial_rope(rms_norm(aq.reshape(bsz, seq, A_HEADS, A_HEAD_DIM), g_qa[l]), positions)
        ka = partial_rope(rms_norm(ak.reshape(bsz, seq, A_HEADS, A_HEAD_DIM), g_ka[l]), positions)
        va = av.reshape(bsz, seq, A_HEADS, A_HEAD_DIM)
        qi = partial_rope(iq.reshape(bsz, seq, IDX_HEADS, IDX_DIM), positions)
        ki = partial_rope(rms_norm(ik, g_kidx[l])[:, :, None, :], positions)[:, :, 0]
        y_a = dsa_attention(qa, ka, va, qi, ki, iw) @ w_oa[l]

        glu_a, glu_b = jnp.split(glu_in, 2, axis=-1)
        u = causal_dwconv(glu_a * jax.nn.sigmoid(glu_b), cb_conv_w[l], cb_conv_b[l])
        y_b = jax.nn.silu(layer_norm(u, cb_ln_g[l], cb_ln_b[l])) @ w_ob[l]

        gb, gc, xc = jnp.split(cc_in, 3, axis=-1)
        y_c = (gb * causal_dwconv(gc * xc, cc_conv_w[l])) @ w_oc[l]

        sq, sk, sv = jnp.split(sb_in, 3, axis=-1)
        shp = (bsz, seq, SB_HEADS, SB_HEAD_DIM)
        y_d = stick_breaking_attention(sq.reshape(shp), sk.reshape(shp), sv.reshape(shp)) @ w_od[l]

        gates = jax.nn.sigmoid(gate_in + b_gate[l]).reshape(bsz, seq, N_BRANCH, dm)
        merged = (gates[:, :, 0] * y_a + gates[:, :, 1] * y_b
                  + gates[:, :, 2] * y_c + gates[:, :, 3] * y_d)
        x = x + merged @ w_merge[l]

        h2 = rms_norm(x, g_ffn[l])
        gt = causal_dwconv(h2 @ w_ffn_gate[l], ffn_conv_w[l])
        x = x + (jax.nn.silu(gt) * (h2 @ w_ffn_up[l])) @ w_ffn_down[l]
    return x


N_A_LAYERS = (DEPTH + 1) // 2
N_B_LAYERS = DEPTH - N_A_LAYERS
HEAD_DIM = 64
N_HEADS = D_MODEL // HEAD_DIM
N_KV = 4
GQA_R = N_HEADS // N_KV
KV_DIM = N_KV * HEAD_DIM
NUM_BUCKETS = 32
MAX_DISTANCE = 2048
CMP_BLOCK = 32
CMP_STRIDE = 16
CMP_HIDDEN = 256
SEL_BLOCK = 64
SEL_TOPN = 8
SEL_Q_CHUNK = 16
FORCE_BONUS = 100.0
WIN = 256
BAND_BLOCK = 128
DILATIONS = ((128, 1), (512, 4), (2048, 16))
N_DIL = len(DILATIONS)
FFN_HIDDEN = -(-8 * D_MODEL // (3 * 256)) * 256
RMS_EPS = 1e-6
NEG_INF = -1e30
A_IN_DIM = D_MODEL + 6 * KV_DIM + 3 * N_HEADS
B_Q_DIM = N_DIL * D_MODEL
SHARED_KV_DIM = N_DIL * 2 * KV_DIM


def rmsnorm(x, g):
    x32 = x.astype(jnp.float32)
    y = x32 * lax.rsqrt(jnp.mean(x32 * x32, axis=-1, keepdims=True) + RMS_EPS)
    return (y * g.astype(jnp.float32)).astype(x.dtype)

def t5_bucket(dist):
    max_exact = NUM_BUCKETS // 2
    d = jnp.maximum(dist, 0)
    log_ratio = jnp.log(jnp.maximum(d, max_exact).astype(jnp.float32) / max_exact) / math.log(MAX_DISTANCE / max_exact)
    large = max_exact + (log_ratio * (NUM_BUCKETS - max_exact)).astype(jnp.int32)
    return jnp.where(d < max_exact, d, jnp.minimum(large, NUM_BUCKETS - 1))

def masked_softmax(s, mask):
    s = jnp.where(mask, s.astype(jnp.float32), NEG_INF)
    m = jnp.max(s, axis=-1, keepdims=True)
    p = jnp.where(mask, jnp.exp(s - m), 0.0)
    return p, jnp.sum(p, axis=-1, keepdims=True), m

def banded_attention(q, k, v, max_dist, dist_scale, rel_bias):
    n, L, G, R, dh = q.shape
    nb = L // BAND_BLOCK
    n_prev = -(-max_dist // BAND_BLOCK)
    pad = n_prev * BAND_BLOCK
    kw_len = (n_prev + 1) * BAND_BLOCK

    def windows(t):
        tp = jnp.pad(t, ((0, 0), (pad, 0), (0, 0), (0, 0))).reshape(n, nb + n_prev, BAND_BLOCK, G, dh)
        return jnp.concatenate([tp[:, j:j + nb] for j in range(n_prev + 1)], axis=2)

    kw, vw = windows(k), windows(v)
    qb = q.reshape(n, nb, BAND_BLOCK, G, R, dh)
    s = jnp.einsum('nbqgrd,nbkgd->nbgrqk', qb, kw).astype(jnp.float32) * dh ** -0.5
    qi = jnp.arange(BAND_BLOCK)[:, None]
    ki = jnp.arange(kw_len)[None, :]
    dist = pad + qi - ki
    key_pos = jnp.arange(nb)[:, None, None] * BAND_BLOCK - pad + ki[None]
    mask = (dist >= 0) & (dist <= max_dist) & (key_pos >= 0)
    bias = rel_bias[t5_bucket(dist * dist_scale)].reshape(BAND_BLOCK, kw_len, G, R).transpose(2, 3, 0, 1)
    p, denom, m = masked_softmax(s + bias, mask[None, :, None, None])
    o = jnp.einsum('nbgrqk,nbkgd->nbqgrd', p, vw.astype(jnp.float32))
    o = o / denom[..., 0].transpose(0, 1, 4, 2, 3)[..., None]
    lse = (jnp.log(denom) + m)[..., 0].transpose(0, 1, 4, 2, 3).reshape(n, L, G, R)
    return o.reshape(n, L, G, R, dh), lse

def dilated_group_attention(q, k, v, dilation, window, rel_bias):
    B, S = q.shape[:2]
    L = S // dilation
    Lp = -(-L // BAND_BLOCK) * BAND_BLOCK

    def to_sub(t):
        rest = t.shape[2:]
        t = t.reshape((B, L, dilation) + rest)
        t = jnp.moveaxis(t, 2, 1).reshape((B * dilation, L) + rest)
        return jnp.pad(t, ((0, 0), (0, Lp - L)) + ((0, 0),) * len(rest))

    def from_sub(t):
        rest = t.shape[2:]
        t = t[:, :L].reshape((B, dilation, L) + rest)
        return jnp.moveaxis(t, 1, 2).reshape((B, S) + rest)

    o, lse = banded_attention(to_sub(q), to_sub(k), to_sub(v), window // dilation, dilation, rel_bias)
    return from_sub(o), from_sub(lse)

def nsa_attention(h, w_in, b_gate, pe_k, w1_k, w2_k, pe_v, w1_v, w2_v, w_out, rel_bias):
    B, S, _ = h.shape
    proj = h @ w_in
    splits = [D_MODEL + i * KV_DIM for i in range(7)]
    q, kc, vc, ks, vs, kwn, vwn, gl = jnp.split(proj, splits, axis=-1)
    q = q.reshape(B, S, N_KV, GQA_R, HEAD_DIM)
    kvh = lambda t: t.reshape(B, S, N_KV, HEAD_DIM)
    scale = HEAD_DIM ** -0.5
    t_pos = jnp.arange(S)

    n_c = (S - CMP_BLOCK) // CMP_STRIDE + 1
    starts = jnp.arange(n_c) * CMP_STRIDE
    tok_idx = starts[:, None] + jnp.arange(CMP_BLOCK)[None, :]

    def compress(t, pe, w1, w2):
        blk = t[:, tok_idx] + pe[:, None, :]
        blk = jnp.moveaxis(blk, 3, 2).reshape(B, n_c, N_KV, CMP_BLOCK * HEAD_DIM)
        return jax.nn.gelu(blk @ w1) @ w2

    k_cmp = compress(kvh(kc), pe_k, w1_k, w2_k)
    v_cmp = compress(kvh(vc), pe_v, w1_v, w2_v)
    dist_c = t_pos[:, None] - (starts + CMP_BLOCK - 1)[None, :]
    bias_c = rel_bias[t5_bucket(dist_c)].reshape(S, n_c, N_KV, GQA_R).transpose(2, 3, 0, 1)
    s = jnp.einsum('bsgrd,bngd->bgrsn', q, k_cmp).astype(jnp.float32) * scale
    p, denom, _ = masked_softmax(s + bias_c, dist_c >= 0)
    p_cmp = p / jnp.maximum(denom, 1e-30)
    o_cmp = jnp.einsum('bgrsn,bngd->bsgrd', p_cmp, v_cmp.astype(jnp.float32))

    n_sel = S // SEL_BLOCK
    top_n = min(SEL_TOPN, n_sel)
    ci = jnp.arange(n_c)[:, None] * CMP_STRIDE
    sj = jnp.arange(n_sel)[None, :] * SEL_BLOCK
    overlap = ((ci < sj + SEL_BLOCK) & (ci + CMP_BLOCK > sj)).astype(jnp.float32)
    imp = jnp.einsum('bgrsn,nj->bgsj', p_cmp, overlap)
    blk_j = jnp.arange(n_sel)[None, :]
    cur = (t_pos // SEL_BLOCK)[:, None]
    forced = (blk_j == 0) | (blk_j == cur) | (blk_j == cur - 1)
    score = jnp.where(forced, imp + FORCE_BONUS, jnp.where(blk_j <= cur, imp, -1.0))
    _, sel_idx = lax.top_k(score, top_n)

    k_blocks = kvh(ks).reshape(B, n_sel, SEL_BLOCK, N_KV, HEAD_DIM).transpose(0, 3, 1, 2, 4)
    v_blocks = kvh(vs).reshape(B, n_sel, SEL_BLOCK, N_KV, HEAD_DIM).transpose(0, 3, 1, 2, 4)
    n_chunk = S // SEL_Q_CHUNK
    q_ch = jnp.moveaxis(q.reshape(B, n_chunk, SEL_Q_CHUNK, N_KV, GQA_R, HEAD_DIM), 1, 0)
    idx_ch = jnp.moveaxis(sel_idx.reshape(B, N_KV, n_chunk, SEL_Q_CHUNK, top_n), 2, 0)
    c0 = jnp.arange(n_chunk) * SEL_Q_CHUNK
    b_ix = jnp.arange(B)[:, None, None, None]
    g_ix = jnp.arange(N_KV)[None, :, None, None]
    rb_g = rel_bias.reshape(NUM_BUCKETS, N_KV, GQA_R).transpose(1, 0, 2)
    n_keys = top_n * SEL_BLOCK

    def sel_chunk(args):
        qc, ic, start = args
        kg = k_blocks[b_ix, g_ix, ic].reshape(B, N_KV, SEL_Q_CHUNK, n_keys, HEAD_DIM)
        vg = v_blocks[b_ix, g_ix, ic].reshape(B, N_KV, SEL_Q_CHUNK, n_keys, HEAD_DIM)
        kpos = (ic[..., None] * SEL_BLOCK + jnp.arange(SEL_BLOCK)).reshape(B, N_KV, SEL_Q_CHUNK, n_keys)
        dist = (start + jnp.arange(SEL_Q_CHUNK))[:, None] - kpos
        bias = jnp.moveaxis(rb_g[g_ix, t5_bucket(dist)], -1, 3)
        s_sel = jnp.einsum('bcgrd,bgckd->bgcrk', qc, kg).astype(jnp.float32) * scale + bias
        p_sel, den, _ = masked_softmax(s_sel, (dist >= 0)[:, :, :, None, :])
        return jnp.einsum('bgcrk,bgckd->bcgrd', p_sel / jnp.maximum(den, 1e-30), vg.astype(jnp.float32))

    o_sel = jnp.moveaxis(lax.map(sel_chunk, (q_ch, idx_ch, c0)), 0, 1).reshape(B, S, N_KV, GQA_R, HEAD_DIM)

    o_win, _ = banded_attention(q, kvh(kwn), kvh(vwn), WIN - 1, 1, rel_bias)

    g = jax.nn.sigmoid((gl + b_gate).astype(jnp.float32)).reshape(B, S, N_KV, GQA_R, 3)
    o = g[..., 0:1] * o_cmp + g[..., 1:2] * o_sel + g[..., 2:3] * o_win
    return o.reshape(B, S, D_MODEL).astype(h.dtype) @ w_out

def dilated_attention(h, w_q, k_shared, v_shared, w_out, rel_bias):
    B, S, _ = h.shape
    q = (h @ w_q).reshape(B, S, N_DIL, N_KV, GQA_R, HEAD_DIM)
    outs, lses = [], []
    for gi, (window, dilation) in enumerate(DILATIONS):
        o, lse = dilated_group_attention(q[:, :, gi], k_shared[:, :, gi], v_shared[:, :, gi], dilation, window, rel_bias)
        outs.append(o)
        lses.append(lse)
    alpha = jax.nn.softmax(jnp.stack(lses, axis=-1), axis=-1)
    o = jnp.einsum('bsgrdi,bsgri->bsgrd', jnp.stack(outs, axis=-1), alpha)
    return o.reshape(B, S, D_MODEL).astype(h.dtype) @ w_out

def swiglu(h, w_up, w_down):
    a, b = jnp.split(h @ w_up, 2, axis=-1)
    return (jax.nn.silu(a) * b) @ w_down

def second_inputs(seed: int = 0) -> dict:
    key = jax.random.key(seed)
    ks = jax.random.split(key, 20)
    f32 = jnp.float32
    nrm = lambda k, shape, s: s * jax.random.normal(k, shape, f32)
    w = lambda k, shape, fan_in: jax.random.normal(k, shape, f32) * fan_in ** -0.5
    gain = lambda k, shape: 1.0 + 0.05 * jax.random.normal(k, shape, f32)
    cmp_in = CMP_BLOCK * HEAD_DIM
    return {
        "x": jax.random.normal(ks[0], (BATCH, SEQ, D_MODEL), f32),
        "rel_bias": nrm(ks[1], (NUM_BUCKETS, N_HEADS), 0.5),
        "norm_mix": gain(ks[2], (DEPTH, D_MODEL)),
        "norm_ffn": gain(ks[3], (DEPTH, D_MODEL)),
        "a_w_in": w(ks[4], (N_A_LAYERS, D_MODEL, A_IN_DIM), D_MODEL),
        "a_b_gate": nrm(ks[5], (N_A_LAYERS, 3 * N_HEADS), 0.1),
        "a_pe_k": nrm(ks[6], (N_A_LAYERS, CMP_BLOCK, HEAD_DIM), 0.1),
        "a_w1_k": w(ks[7], (N_A_LAYERS, cmp_in, CMP_HIDDEN), cmp_in),
        "a_w2_k": w(ks[8], (N_A_LAYERS, CMP_HIDDEN, HEAD_DIM), CMP_HIDDEN),
        "a_pe_v": nrm(ks[9], (N_A_LAYERS, CMP_BLOCK, HEAD_DIM), 0.1),
        "a_w1_v": w(ks[10], (N_A_LAYERS, cmp_in, CMP_HIDDEN), cmp_in),
        "a_w2_v": w(ks[11], (N_A_LAYERS, CMP_HIDDEN, HEAD_DIM), CMP_HIDDEN),
        "a_w_out": w(ks[12], (N_A_LAYERS, D_MODEL, D_MODEL), D_MODEL),
        "kv_norm": gain(ks[13], (D_MODEL,)),
        "kv_w": w(ks[14], (D_MODEL, SHARED_KV_DIM), D_MODEL),
        "b_w_q": w(ks[15], (N_B_LAYERS, D_MODEL, B_Q_DIM), D_MODEL),
        "b_w_out": w(ks[16], (N_B_LAYERS, D_MODEL, D_MODEL), D_MODEL),
        "ffn_w_up": w(ks[17], (DEPTH, D_MODEL, 2 * FFN_HIDDEN), D_MODEL),
        "ffn_w_down": w(ks[18], (DEPTH, FFN_HIDDEN, D_MODEL), FFN_HIDDEN),
        "final_norm": gain(ks[19], (D_MODEL,)),
    }

def second_block(x, rel_bias, norm_mix, norm_ffn, a_w_in, a_b_gate, a_pe_k, a_w1_k, a_w2_k, a_pe_v, a_w1_v, a_w2_v,
              a_w_out, kv_norm, kv_w, b_w_q, b_w_out, ffn_w_up, ffn_w_down, final_norm):
    B, S, _ = x.shape
    k_shared = v_shared = None
    for layer in range(DEPTH):
        h = rmsnorm(x, norm_mix[layer])
        if layer < N_A_LAYERS:
            i = layer
            mix = nsa_attention(h, a_w_in[i], a_b_gate[i], a_pe_k[i], a_w1_k[i], a_w2_k[i],
                                a_pe_v[i], a_w1_v[i], a_w2_v[i], a_w_out[i], rel_bias)
        else:
            if layer == N_A_LAYERS:
                kv = (rmsnorm(x, kv_norm) @ kv_w).reshape(B, S, N_DIL, 2, N_KV, HEAD_DIM)
                k_shared, v_shared = kv[:, :, :, 0], kv[:, :, :, 1]
            j = layer - N_A_LAYERS
            mix = dilated_attention(h, b_w_q[j], k_shared, v_shared, b_w_out[j], rel_bias)
        x = x + mix.astype(x.dtype)
        x = x + swiglu(rmsnorm(x, norm_ffn[layer]), ffn_w_up[layer], ffn_w_down[layer]).astype(x.dtype)
    return rmsnorm(x, final_norm)


def setup_inputs(seed=0):
    out = dict(first_inputs(seed))
    for name, value in second_inputs(seed + 1).items():
        if name != "x":
            out[name + "_2"] = value
    return out


def reference(
    x, positions, g_mix, w_in, b_gate, g_qa, g_ka, g_kidx, w_oa, cb_conv_w, cb_conv_b, cb_ln_g,
    cb_ln_b, w_ob, cc_conv_w, w_oc, w_od, w_merge, g_ffn, w_ffn_gate, w_ffn_up, ffn_conv_w,
    w_ffn_down, rel_bias_2, norm_mix_2, norm_ffn_2, a_w_in_2, a_b_gate_2, a_pe_k_2, a_w1_k_2,
    a_w2_k_2, a_pe_v_2, a_w1_v_2, a_w2_v_2, a_w_out_2, kv_norm_2, kv_w_2, b_w_q_2, b_w_out_2,
    ffn_w_up_2, ffn_w_down_2, final_norm_2,
):
    x = first_block(
        x, positions, g_mix, w_in, b_gate, g_qa, g_ka, g_kidx, w_oa, cb_conv_w, cb_conv_b,
        cb_ln_g, cb_ln_b, w_ob, cc_conv_w, w_oc, w_od, w_merge, g_ffn, w_ffn_gate, w_ffn_up,
        ffn_conv_w, w_ffn_down,
    )
    return second_block(
        x, rel_bias_2, norm_mix_2, norm_ffn_2, a_w_in_2, a_b_gate_2, a_pe_k_2, a_w1_k_2,
        a_w2_k_2, a_pe_v_2, a_w1_v_2, a_w2_v_2, a_w_out_2, kv_norm_2, kv_w_2, b_w_q_2,
        b_w_out_2, ffn_w_up_2, ffn_w_down_2, final_norm_2,
    )


_drawn_inputs = setup_inputs


def setup_inputs(seed=0):
    import zlib

    import numpy as np

    out = dict(_drawn_inputs(seed))
    spreads = {}
    factors = {'g_qa': 6.286,
     'g_ka': 5.846,
     'cb_ln_b': 4.884,
     'norm_mix_2': 4.397,
     'a_b_gate_2': 5.842,
     'a_pe_k_2': 8.0,
     'a_pe_v_2': 3.044,
     'kv_norm_2': 6.677}
    for name, (base, spread) in spreads.items():
        noise = np.random.default_rng([zlib.crc32(name.encode()), seed]).standard_normal(out[name].shape)
        drawn = base * np.exp(spread * noise) if base else spread * noise
        out[name] = __import__('jax').numpy.asarray(drawn.astype(out[name].dtype))
    for name, factor in factors.items():
        out[name] = (out[name] * factor).astype(out[name].dtype)
    return out
```

```python
import math
from contextlib import ExitStack

import numpy as np
import concourse.bass as bass
from concourse import mybir

F32 = mybir.dt.float32
I32 = mybir.dt.int32
ALU = mybir.AluOpType
ACT = mybir.ActivationFunctionType
AX = mybir.AxisListType

P = 128
D = 1024
S = 256
TT = S // P
KT = D // P
DEPTH = 2
HEADS = 4
WIDTH = 512
IDX_DIM = 64
TOPK = S // 4
LONG = 31
SHORT = 3
FF = 2816
FT = FF // P
EPS = 1e-6
NEG = -1e30
TAKEN = -3e38
GROUPS = 4
PER_GROUP = 4
QH = 16
DH = 64
CMP_BLOCK = 32
CMP_STRIDE = 16
CMP_N = (S - CMP_BLOCK) // CMP_STRIDE + 1
CMP_PAD = 32
CMP_HIDDEN = 256
DILATIONS = (1, 4, 16)
BAND = 128
BUCKETS = 32
MAX_DISTANCE = 2048
SPAN = 384

W_Q, W_IDX, W_GLU, W_CC, W_SQ, W_SV, W_GATE = 0, 1536, 1860, 2884, 4420, 5444, 5956
IDX_COLS = 324
A_Q, A_KC, A_VC, A_KS, A_VS, A_KW, A_VW, A_GL = 0, 1024, 1280, 1536, 1792, 2048, 2304, 2560

SLOTS = 4
CHUNK = 4096

C_ID, C_MEAN, C_ONE, C_TRI, C_SNEG, C_SKEEP, C_CAUS, C_LOW, C_HIGH, C_FREQ, C_CMP = (
    0, 128, 256, 384, 512, 640, 768, 896, 1024, 1152, 1176)
C_COLS = C_CMP + TT * CMP_N
O_FULL, O_DIL, O_CMP = 0, SPAN, 4 * SPAN
O_COLS = O_CMP + 512

R_LONG = lambda l: 3 * l * P
R_MISC = lambda l: (3 * l + 1) * P
R_FFC = lambda l: (3 * l + 2) * P
R_PART2 = 3 * DEPTH * P
M_GATE, M_MIX, M_FFN, M_CB, M_LNG, M_LNB, M_CC = 0, 32, 40, 48, 52, 56, 60
M2_MIX, M2_FFN, M2_KV, M2_PEK, M2_PEV = 0, 16, 32, 40, 56
PARAM_TILES = 3 * DEPTH + 1


def t5_bucket(dist):
    d = np.maximum(dist, 0)
    half = BUCKETS // 2
    ratio = (np.log(np.maximum(d, half).astype(np.float32) / np.float32(half)).astype(np.float32)
             / np.float32(math.log(MAX_DISTANCE / half)))
    large = half + (ratio * np.float32(BUCKETS - half)).astype(np.int32)
    return np.where(d < half, d, np.minimum(large, BUCKETS - 1))


def shape_constants():
    c = np.zeros((P, C_COLS), np.float32)
    p = np.arange(P)[:, None]
    f = np.arange(P)[None, :]
    c[:, C_ID:C_ID + P] = p == f
    c[:, C_MEAN:C_MEAN + P] = 1.0 / WIDTH
    c[:, C_ONE:C_ONE + P] = 1.0
    c[:, C_TRI:C_TRI + P] = p >= f
    c[:, C_SNEG:C_SNEG + P] = np.where(p < f, 0.0, NEG)
    c[:, C_SKEEP:C_SKEEP + P] = p < f
    c[:, C_CAUS:C_CAUS + P] = np.where(f <= p, 0.0, NEG)
    c[:, C_LOW:C_LOW + P] = p == f % DH
    c[:, C_HIGH:C_HIGH + P] = p == f % DH + DH
    for at, half in ((0, 16), (16, 8)):
        rot = 2 * half
        c[:, C_FREQ + at:C_FREQ + at + half] = (
            np.float32(500000.0) ** (-(np.arange(half, dtype=np.float32) * np.float32(2.0)) / np.float32(rot)))
    for t in range(TT):
        dist = P * t + p - (CMP_STRIDE * np.arange(CMP_N)[None, :] + CMP_BLOCK - 1)
        c[:, C_CMP + t * CMP_N:C_CMP + (t + 1) * CMP_N] = dist >= 0
    return c


def distance_tables():
    o = np.zeros((BUCKETS + 1, O_COLS), np.float32)

    def put(col, dist, keep):
        cols = np.arange(len(dist)) + col
        o[t5_bucket(dist)[keep], cols[keep]] = 1.0
        o[BUCKETS, cols[~keep]] = 1.0

    back = (S - 1) - np.arange(SPAN)
    put(O_FULL, back, back >= 0)
    for n, dil in enumerate(DILATIONS):
        put(O_DIL + n * SPAN, back, (back >= 0) & (back % dil == 0) & (back <= BAND * dil))
    ahead = np.arange(512) - (S - 1)
    put(O_CMP, ahead, ahead >= 0)
    return o


def spread(ap, dim, n):
    dims = [list(x) for x in ap.ap]
    return bass.AP(ap.tensor, ap.offset, dims[:dim] + [[0, n]] + dims[dim:])


class Signal:

    def __init__(self, sem):
        self.sem, self.base = sem, 0

    def at(self, k):
        assert self.base + k > 0
        return self.base + k

    def close(self, n):
        self.base += n


class Ring:

    def __init__(self):
        self.loaded, self.landed, self.freed = 0, [0] * SLOTS, []


def two_part_transformer(nc, a, consts, onehots, out):
    ctx = ExitStack()
    with ctx:
        def sb(name, shape, dt=F32):
            return ctx.enter_context(nc.sbuf_tensor(name, shape, dt))

        def signal(name):
            return Signal(ctx.enter_context(nc.semaphore(name)))

        x = sb("x", [P, TT, D])
        hT = sb("hT", [P, KT, S])
        ring_buf = sb("ring_buf", [P, SLOTS, CHUNK])
        cst = sb("cst", [P, C_COLS])
        par = sb("par", [P, PARAM_TILES * P])
        g_head = sb("g_head", [P, DEPTH, 2, P])
        g_kidx = sb("g_kidx", [P, DEPTH, IDX_DIM])
        b_gl = sb("b_gl", [P, 3 * QH])
        rot = sb("rot", [P, 2, TT, 24])
        stat = sb("stat", [P, 160])
        WORK = 29200
        work = sb("work", [P, WORK])
        psum = ctx.enter_context(nc.psum_tensor("psum", [P, 8, 512], F32))
        table_dram = nc.dram_tensor("table_dram", [4, QH, P, SPAN + 1], F32, kind="Internal").ap()
        HEAD_SKEW = P * (SPAN + 1)
        TABLE_SKEW = QH * HEAD_SKEW

        ident = cst[:, C_ID:C_ID + P]

        def region(start, *shape):
            n = int(np.prod(shape))
            assert start + n <= WORK, (start, shape)
            v = work[:, start:start + n]
            if len(shape) == 2:
                return v.rearrange("p (a b) -> p a b", a=shape[0])
            if len(shape) == 3:
                return v.rearrange("p (a b c) -> p a b c", a=shape[0], b=shape[1])
            return v

        def bank(b, n=1):
            return psum[:, b:b + n, :].rearrange("p a b -> p (a b)")

        stage_done = signal("stage_done")
        chunk_landed = [ctx.enter_context(nc.semaphore(f"chunk_landed{i}")) for i in range(SLOTS)]
        chunk_used = signal("chunk_used")
        bank_full = signal("bank_full")
        bank_free = signal("bank_free")
        vector_step = signal("vector_step")
        scalar_step = signal("scalar_step")
        variance_ready = signal("variance_ready")
        root_ready = signal("root_ready")
        squares_ready = signal("squares_ready")
        rows_scaled = signal("rows_scaled")
        rows_turned = signal("rows_turned")
        side_full = signal("side_full")
        side_free = signal("side_free")
        scores_ready = signal("scores_ready")
        scores_read = signal("scores_read")
        maxima_ready = signal("maxima_ready")
        probs_ready = signal("probs_ready")
        probs_turned = signal("probs_turned")
        turned_copied = signal("turned_copied")
        context_ready = signal("context_ready")
        context_read = signal("context_read")
        operand_ready = signal("operand_ready")
        inner_ready = signal("inner_ready")
        inner_taken = signal("inner_taken")
        side_load = signal("side_load")
        table_load = signal("table_load")
        side_store = signal("side_store")
        stored = ctx.enter_context(nc.semaphore("stored"))

        block = ctx.enter_context(nc.Block())
        ring = Ring()

        COMPUTE = 3
        stage = [0]

        def begin(eng):
            if stage[0]:
                eng.wait_ge(stage_done.sem, COMPUTE * stage[0])

        def end(eng):
            eng.drain().then_inc(stage_done.sem, 1)

        def close_stage(**signals):
            stage[0] += 1

        def v_done(ins):
            ins.then_inc(vector_step.sem, 1)
            vector_step.base += 1
            return vector_step.base

        def v_wait(n):
            nc.vector.wait_ge(vector_step.sem, n)

        def v_link(ins):
            v_wait(v_done(ins))

        def s_done(ins):
            ins.then_inc(scalar_step.sem, 1)
            scalar_step.base += 1
            return scalar_step.base

        def s_wait(n):
            nc.scalar.wait_ge(scalar_step.sem, n)

        def load_chunk(sp, *pieces):
            n = ring.loaded
            slot = n % SLOTS
            if n >= SLOTS:
                sp.wait_ge(*ring.freed[n - SLOTS])
            for off, src in pieces:
                kt, cols = src.shape[0] // P, src.shape[1]
                dst = ring_buf[:, slot, off:off + kt * cols].rearrange("p (k c) -> p k c", k=kt)
                sp.dma_start(dst, src.rearrange("(k p) c -> p k c", p=P)).then_inc(chunk_landed[slot], 16)
            ring.loaded += 1

        def chunk_view(kt, cols, off=0):
            slot = len(ring.freed) % SLOTS
            return ring_buf[:, slot, off:off + kt * cols].rearrange("p (k c) -> p k c", k=kt)

        def take_chunk(pe, kt, cols, off=0, pieces=1):
            slot = len(ring.freed) % SLOTS
            ring.landed[slot] += 16 * pieces
            pe.wait_ge(chunk_landed[slot], ring.landed[slot])
            return chunk_view(kt, cols, off)

        def release_chunk(event, k):
            ring.freed.append((event.sem, event.at(k)))

        def free_bank(pe, n):
            if n >= 4:
                pe.wait_ge(bank_free.sem, bank_free.at(n - 3))
            return bank(n % 4)

        def columns_product(pe, n, w, src, cols):
            b = free_bank(pe, n)
            for j, c in enumerate(cols):
                for k in range(KT):
                    mm = nc.tensor.matmul(b[:, j * S:(j + 1) * S], w[:, k, c:c + P], src[:, k, :],
                                          start=(k == 0), stop=(k == KT - 1))
            return mm

        def rows_product(pe, n, w, src, t, width):
            b = free_bank(pe, n)
            for k in range(KT):
                mm = nc.tensor.matmul(b[:, 0:width], src[:, k, t * P:(t + 1) * P], w[:, k, 0:width],
                                      start=(k == 0), stop=(k == KT - 1))
            return mm

        def two_halves(pe, n, pairs, sets):
            pe.wait_ge(inner_ready.sem, inner_ready.at(1))
            for i in range(sets):
                for gp in range(2):
                    b = free_bank(pe, n)
                    for j, pick in enumerate((C_LOW, C_HIGH)):
                        mm = nc.tensor.matmul(b[:, j * S:(j + 1) * S], cst[:, pick:pick + P], pairs[:, i, gp, :],
                                              start=True, stop=True)
                    mm.then_inc(bank_full.sem, 1)
                    n += 1

        def setup_stage():
            praw = region(0, PARAM_TILES, P)
            onehot = region(4000, O_COLS)
            relb = region(7000, QH)
            posi = ctx.enter_context(nc.sbuf_tensor("posi", [P, TT], I32))
            tab = region(27600, 4, SPAN)
            ang = region(10000, 2 * TT, 24)
            tmp = region(10200, 2 * TT, 24)
            loads = []

            @block.gpsimd
            def _(pool):
                pool.memset(praw, 0.0).then_inc(operand_ready.sem, 1)
                pool.memset(work[0:BUCKETS + 1, 7000:7000 + QH], NEG).then_inc(operand_ready.sem, 1)

            @block.scalar
            def _(act):
                def load(dst, src):
                    act.dma_start(dst, src).then_inc(side_load.sem, 16)
                    loads.append(1)

                load(cst[:, :], consts)
                load(x[:, :, :], a["x"][0].rearrange("(t p) d -> p t d", p=P))
                load(onehot[0:BUCKETS + 1, :], onehots)
                for l in range(DEPTH):
                    for n, g in enumerate(("g_qa", "g_ka")):
                        load(g_head[:, l, n, :], a[g][l:l + 1, :].rearrange("a d -> (a d)").partition_broadcast(P))
                    load(g_kidx[:, l, :], a["g_kidx"][l:l + 1, :].rearrange("a d -> (a d)").partition_broadcast(P))
                load(b_gl[:, :], a["a_b_gate_2"][0:1, :].rearrange("a d -> (a d)").partition_broadcast(P))
                for t in range(TT):
                    load(posi[:, t:t + 1], a["positions"][0:1, t * P:(t + 1) * P].rearrange("a p -> p a"))
                act.wait_ge(operand_ready.sem, operand_ready.at(2))

                def rows(tile, row, src):
                    n = src.shape[0]
                    load(praw[row:row + n, tile, :], src)

                load(work[0:BUCKETS, 7000:7000 + QH], a["rel_bias_2"])
                for l in range(DEPTH):
                    rows(3 * l, 0, a["cb_conv_w"][l].rearrange("k (t p) -> (k t) p", p=P))
                    for at, name in ((M_GATE, "b_gate"), (M_MIX, "g_mix"), (M_FFN, "g_ffn"), (M_CB, "cb_conv_b"),
                                     (M_LNG, "cb_ln_g"), (M_LNB, "cb_ln_b")):
                        rows(3 * l + 1, at, a[name][l].rearrange("(t p) -> t p", p=P))
                    rows(3 * l + 1, M_CC, a["cc_conv_w"][l].rearrange("k (t p) -> (k t) p", p=P))
                    rows(3 * l + 2, 0, a["ffn_conv_w"][l].rearrange("k (t p) -> (k t) p", p=P))
                last = 3 * DEPTH
                for at, name in ((M2_MIX, "norm_mix_2"), (M2_FFN, "norm_ffn_2")):
                    rows(last, at, a[name].rearrange("l (t p) -> (l t) p", p=P))
                rows(last, M2_KV, a["kv_norm_2"].rearrange("(t p) -> t p", p=P))
                for at, name in ((M2_PEK, "a_pe_k_2"), (M2_PEV, "a_pe_v_2")):
                    rows(last, at, a[name][0].rearrange("(m j) d -> m (j d)", j=2))
                act.wait_ge(rows_scaled.sem, rows_scaled.at(1))
                act.activation(rot[:, :, :, :].rearrange("p a t f -> p (a t) f"), ang, ACT.Sin) \
                   .then_inc(inner_ready.sem, 1)
                end(act)

            @block.tensor
            def _(pe):
                pe.wait_ge(side_load.sem, side_load.at(16 * len(loads)))
                for n in range(PARAM_TILES):
                    mm = nc.tensor.transpose(bank(n // 4)[:, (n % 4) * P:(n % 4 + 1) * P], praw[:, n, :], ident)
                mm.then_inc(side_full.sem, 1)
                for n in range(4):
                    mm = nc.tensor.matmul(bank(2 + n)[0:QH, 0:SPAN], work[0:BUCKETS + 1, 7000:7000 + QH],
                                          onehot[0:BUCKETS + 1, n * SPAN:(n + 1) * SPAN], start=True, stop=True)
                mm.then_inc(side_full.sem, 1)
                end(pe)

            @block.vector
            def _(dve):
                dve.wait_ge(side_full.sem, side_full.at(1))
                dve.tensor_copy(par[:, 0:4 * P], bank(0))
                dve.tensor_copy(par[:, 4 * P:PARAM_TILES * P], bank(1)[:, 0:(PARAM_TILES - 4) * P])
                dve.wait_ge(side_full.sem, side_full.at(2))
                for n in range(4):
                    dve.tensor_copy(tab[0:QH, n, :], bank(2 + n)[0:QH, 0:SPAN]).then_inc(side_free.sem, 1)
                dve.wait_ge(side_load.sem, side_load.at(16 * len(loads)))
                pos = stat[:, 0:TT]
                v_link(dve.tensor_copy(pos, posi[:, :]))
                for t in range(TT):
                    n = v_done(dve.tensor_scalar(ang[:, TT + t, :], cst[:, C_FREQ:C_FREQ + 24], pos[:, t:t + 1],
                                                 None, ALU.mult))
                v_wait(n)
                s_ = ang[:, TT:2 * TT, :]
                c_ = ang[:, 0:TT, :]
                turns = tmp[:, 0:TT, :]
                magic = 1.5 * 2.0 ** 23
                v_link(dve.tensor_scalar(turns, s_, 1.0 / (2 * math.pi), magic, ALU.mult, ALU.add))
                v_link(dve.tensor_scalar(turns, turns, -magic, None, ALU.add))
                two_pi = 2 * math.pi
                c1 = 6.28125
                c2 = float(np.float32(int((two_pi - c1) * 2 ** 21) / 2 ** 21))
                c3 = two_pi - c1 - c2
                for c in (c1, c2, c3):
                    v_link(dve.scalar_tensor_tensor(s_, turns, -c, s_, ALU.mult, ALU.add))
                v_link(dve.tensor_scalar(c_, s_, math.pi / 2, None, ALU.add))
                v_link(dve.tensor_scalar(turns, c_, math.pi, -two_pi, ALU.is_gt, ALU.mult))
                v_link(dve.tensor_tensor(c_, c_, turns, ALU.add))
                edge = 3.1415925
                dve.tensor_scalar(ang, ang, edge, -edge, ALU.min, ALU.max).then_inc(rows_scaled.sem, 1)
                dve.wait_ge(inner_ready.sem, inner_ready.at(1))
                end(dve)

            @block.gpsimd
            def _(pool):
                pool.wait_ge(side_free.sem, side_free.at(4))
                for n in range(4):
                    pool.dma_start(table_dram[n, :, :, 0:SPAN], spread(tab[0:QH, n, :], 1, P)) \
                        .then_inc(side_store.sem, 16)

            operand_ready.close(2)
            side_load.close(16 * len(loads))
            rows_scaled.close(1)
            inner_ready.close(1)
            side_full.close(2)
            side_free.close(4)
            side_store.close(64)
            close_stage()

        def inverse_root(dve, y, v, t, src, n_over, k):
            dve.tensor_scalar(v, src, n_over, EPS, ALU.mult, ALU.add).then_inc(variance_ready.sem, 1)
            dve.wait_ge(root_ready.sem, root_ready.at(k))
            v_link(dve.reciprocal(y, t))
            v_link(dve.tensor_tensor(t, v, y, ALU.mult))
            v_link(dve.tensor_tensor(t, t, y, ALU.mult))
            v_link(dve.tensor_scalar(t, t, -0.5, 1.5, ALU.mult, ALU.add))
            v_link(dve.tensor_tensor(y, y, t, ALU.mult))

        def square_root(act, v, t, k):
            act.wait_ge(variance_ready.sem, variance_ready.at(k))
            act.activation(t, v, ACT.Sqrt).then_inc(root_ready.sem, 1)

        def close_roots(n):
            variance_ready.close(n)
            root_ready.close(n)

        def norm_stage(gain, scratch=0):
            xn = region(scratch, TT, D)

            @block.scalar
            def _(act):
                begin(act)
                for t in range(TT):
                    act.activation(xn[:, t, :], x[:, t, :], ACT.Square, accum_out=stat[:, t:t + 1]) \
                       .then_inc(squares_ready.sem, 1)
                square_root(act, stat[:, 6:6 + TT], stat[:, 8:8 + TT], 1)
                for b in range(4):
                    act.wait_ge(rows_turned.sem, rows_turned.at(b + 1))
                    act.activation(hT[:, 2 * b, :], bank(b)[:, 0:S], ACT.Copy, scale=gain(2 * b))
                    act.activation(hT[:, 2 * b + 1, :], bank(b)[:, S:2 * S], ACT.Copy, scale=gain(2 * b + 1))
                end(act)

            @block.vector
            def _(dve):
                begin(dve)
                dve.wait_ge(squares_ready.sem, squares_ready.at(TT))
                inverse_root(dve, stat[:, 4:4 + TT], stat[:, 6:6 + TT], stat[:, 8:8 + TT], stat[:, 0:TT], 1.0 / D, 1)
                for t in range(TT):
                    dve.tensor_scalar(xn[:, t, :], x[:, t, :], stat[:, 4 + t:5 + t], None, ALU.mult) \
                       .then_inc(rows_scaled.sem, 1)
                end(dve)

            @block.tensor
            def _(pe):
                begin(pe)
                pe.wait_ge(rows_scaled.sem, rows_scaled.at(TT))
                for b in range(4):
                    for j in range(4):
                        k, t = 2 * b + j // 2, j % 2
                        mm = nc.tensor.transpose(bank(b)[:, j * P:(j + 1) * P], xn[:, t, k * P:(k + 1) * P], ident)
                    mm.then_inc(rows_turned.sem, 1)
                end(pe)

            squares_ready.close(TT)
            close_roots(1)
            rows_scaled.close(TT)
            rows_turned.close(4)
            close_stage()

        def add_rows_product(weights, lhsT, nk):
            chunks = -(-nk // 4)

            @block.tensor
            def _(pe):
                begin(pe)
                for c in range(chunks):
                    n = min(4, nk - 4 * c)
                    w = take_chunk(pe, n, D)
                    for k in range(n):
                        for t in range(TT):
                            for h in range(2):
                                mm = nc.tensor.matmul(bank(4 + 2 * t + h), lhsT[:, 4 * c + k, t * P:(t + 1) * P],
                                                      w[:, k, h * 512:(h + 1) * 512],
                                                      start=(c + k == 0), stop=(4 * c + k == nk - 1))
                    mm.then_inc(chunk_used.sem, 1)
                    release_chunk(chunk_used, c + 1)
                end(pe)
            
            @block.sync
            def _(sp):
                for c in range(chunks):
                    load_chunk(sp, (0, weights[4 * c * P:min(4 * c + 4, nk) * P, :]))

            @block.scalar
            def _(act):
                begin(act)
                end(act)

            @block.vector
            def _(dve):
                begin(dve)
                dve.wait_ge(stage_done.sem, COMPUTE * stage[0] + 2)
                for t in range(TT):
                    dve.tensor_tensor(x[:, t, :], x[:, t, :], bank(4 + 2 * t, 2), ALU.add)
                end(dve)

            chunk_used.close(chunks)
            close_stage()

        def ffn_up_stage(gate_w, up_w, gate0, up0, fT, conv):
            pairs = FT // 2
            pad = SHORT - 1
            gpad = region(FT * S, 4, S + pad).rearrange("p (b j) s -> p b j s", b=2)
            cacc = region(FT * S + 4 * (S + pad), 4, S).rearrange("p (b j) s -> p b j s", b=2)

            @block.tensor
            def _(pe):
                begin(pe)
                for c in range(pairs):
                    w = take_chunk(pe, KT, S, 0, 2)
                    columns_product(pe, 2 * c, w, hT, (0, P)).then_inc(bank_full.sem, 1)
                    w = chunk_view(KT, S, KT * S)
                    mm = columns_product(pe, 2 * c + 1, w, hT, (0, P))
                    mm.then_inc(bank_full.sem, 1)
                    release_chunk(bank_full, 2 * c + 2)
                end(pe)

            @block.sync
            def _(sp):
                for c in range(pairs):
                    load_chunk(sp, (0, gate_w[:, gate0 + c * S:gate0 + (c + 1) * S]),
                               (KT * S, up_w[:, up0 + c * S:up0 + (c + 1) * S]))

            @block.scalar
            def _(act):
                begin(act)
                if conv is not None:
                    act.wait_ge(side_free.sem, side_free.at(1))
                for c in range(pairs):
                    act.wait_ge(bank_full.sem, bank_full.at(2 * c + 1))
                    if conv is None:
                        if c >= 2:
                            act.wait_ge(bank_free.sem, bank_free.at(2 * c - 2))
                        for j in range(2):
                            ins = act.activation(cacc[:, c % 2, j, :], bank(2 * c % 4)[:, j * S:(j + 1) * S], ACT.Silu)
                        ins.then_inc(inner_ready.sem, 1)
                        continue
                    if c >= 2:
                        act.wait_ge(operand_ready.sem, operand_ready.at(c - 1))
                    act.activation(gpad[:, c % 2, :, pad:], bank(2 * c % 4).rearrange("p (j s) -> p j s", j=2),
                                   ACT.Copy).then_inc(inner_ready.sem, 1)
                    if c:
                        act.wait_ge(operand_ready.sem, operand_ready.at(c))
                        b = (c - 1) % 2
                        act.activation(cacc[:, b], cacc[:, b], ACT.Silu).then_inc(inner_ready.sem, 1)
                if conv is not None:
                    act.wait_ge(operand_ready.sem, operand_ready.at(pairs))
                    b = (pairs - 1) % 2
                    act.activation(cacc[:, b], cacc[:, b], ACT.Silu).then_inc(inner_ready.sem, 1)
                end(act)

            @block.vector
            def _(dve):
                begin(dve)

                def product(c, ready):
                    dve.wait_ge(bank_full.sem, bank_full.at(2 * c + 2))
                    dve.wait_ge(inner_ready.sem, inner_ready.at(ready))
                    ins = dve.tensor_tensor(fT[:, 2 * c:2 * c + 2, :], cacc[:, c % 2],
                                            bank((2 * c + 1) % 4).rearrange("p (j s) -> p j s", j=2), ALU.mult)
                    ins.then_inc(bank_free.sem, 2)

                if conv is None:
                    for c in range(pairs):
                        product(c, c + 1)
                else:
                    dve.memset(gpad.rearrange("p b j s -> p (b j) s")[:, :, 0:pad], 0.0).then_inc(side_free.sem, 1)
                    for c in range(pairs + 1):
                        if c < pairs:
                            b = c % 2
                            dve.wait_ge(inner_ready.sem, inner_ready.at(2 * c if c else 1))
                            if c >= 2:
                                dve.wait_ge(bank_free.sem, bank_free.at(2 * c - 2))
                            n = [0, 0]
                            for k in range(SHORT):
                                for j in range(2):
                                    src = gpad[:, b, j, k:k + S]
                                    if k == 0:
                                        ins = dve.tensor_scalar(cacc[:, b, j, :], src, conv(k, 2 * c + j), None, ALU.mult)
                                    else:
                                        v_wait(n[j])
                                        ins = dve.scalar_tensor_tensor(cacc[:, b, j, :], src, conv(k, 2 * c + j),
                                                                       cacc[:, b, j, :], ALU.mult, ALU.add)
                                    n[j] = v_done(ins)
                            v_wait(n[1])
                            nc.vector.nop().then_inc(operand_ready.sem, 1)
                        if c:
                            last = c == pairs
                            product(c - 1, 2 * pairs if last else 2 * c + 1)
                end(dve)

            bank_full.close(2 * pairs)
            bank_free.close(2 * pairs)
            if conv is None:
                inner_ready.close(pairs)
            else:
                inner_ready.close(2 * pairs)
                operand_ready.close(pairs)
                side_free.close(1)
            close_stage()

        def attention(units, q, k, v, bias, scale, dh, bufs, finish, nq):
            sbuf_s, sbuf_p, sbuf_t = bufs
            U = len(units)
            width = [len(h) * len(st) * P * (t + 1) for t, h, st in units]
            keys = [P * (t + 1) for t, _, _ in units]
            rounds = []
            for u, (t, heads, sets) in enumerate(units):
                blocks = [(hi, si, kt) for hi in range(len(heads)) for si in range(len(sets)) for kt in range(t + 1)]
                for i in range(0, len(blocks), 4):
                    rounds.append((u, blocks[i:i + 4], i == 0, i + 4 >= len(blocks)))
            wide = max(width) > 512

            def score_bank(u):
                return bank(2 * (u % 2), 2) if wide else bank(u % 2)

            @block.tensor
            def _(pe):
                begin(pe)

                def scores(u):
                    t, heads, sets = units[u]
                    if u >= 2:
                        pe.wait_ge(scores_read.sem, scores_read.at(u - 1))
                    b = score_bank(u)
                    o = 0
                    for h in heads:
                        for st in sets:
                            mm = nc.tensor.matmul(b[:, o:o + keys[u]], q(h, st, t), k(h, st)[:, 0:keys[u]],
                                                  start=True, stop=True)
                            o += keys[u]
                    mm.then_inc(scores_ready.sem, 1)

                def context(r):
                    u, blocks, first, last = rounds[r]
                    t, heads, sets = units[u]
                    if first and u >= 2:
                        pe.wait_ge(context_read.sem, context_read.at(u - 1))
                    pe.wait_ge(turned_copied.sem, turned_copied.at(r + 1))
                    for n, (hi, si, kt) in enumerate(blocks):
                        mm = nc.tensor.matmul(bank(6 + u % 2)[:, hi * dh:(hi + 1) * dh],
                                              sbuf_t[:, r % 2, n * P:(n + 1) * P], v(sets[si], kt, heads[hi]),
                                              start=(si == 0 and kt == 0), stop=(si == len(sets) - 1 and kt == t))
                    if last:
                        mm.then_inc(context_ready.sem, 1)

                scores(0)
                for r, (u, blocks, first, last) in enumerate(rounds):
                    if first:
                        if u + 1 < U:
                            scores(u + 1)
                        pe.wait_ge(probs_ready.sem, probs_ready.at(u + 1))
                    if r >= 2:
                        pe.wait_ge(turned_copied.sem, turned_copied.at(r - 1))
                    for n, (hi, si, kt) in enumerate(blocks):
                        t, heads, sets = units[u]
                        o = (hi * len(sets) + si) * keys[u] + kt * P
                        mm = nc.tensor.transpose(bank(4 + r % 2)[:, n * P:(n + 1) * P],
                                                 sbuf_p[:, u % 2, o:o + P], ident)
                    mm.then_inc(probs_turned.sem, 1)
                    if r:
                        context(r - 1)
                context(len(rounds) - 1)
                end(pe)

            @block.vector
            def _(dve):
                begin(dve)
                mx = stat[:, 0:16]

                def use(u):
                    t, heads, sets = units[u]
                    dve.wait_ge(context_ready.sem, context_ready.at(u + 1))
                    dve.wait_ge(probs_ready.sem, probs_ready.at(u + 1))
                    den = stat[:, 16 + 8 * (u % 2):16 + 8 * (u % 2) + len(heads)]
                    rec = stat[:, 32 + 8 * (u % 2):32 + 8 * (u % 2) + len(heads)]
                    v_link(dve.reciprocal(rec, den))
                    finish(dve, u, units[u], bank(6 + u % 2)[:, 0:len(heads) * dh], rec)

                for u, (t, heads, sets) in enumerate(units):
                    nh = len(heads)
                    dve.wait_ge(scores_ready.sem, scores_ready.at(u + 1))
                    if u >= 2:
                        dve.wait_ge(probs_ready.sem, probs_ready.at(u - 1))
                    sc = score_bank(u)[:, 0:width[u]]
                    s_ = sbuf_s[:, u % 2, 0:width[u]]
                    for psrc, sdst, bsrc in bias(u, units[u], sc, s_, keys[u]):
                        ins = dve.scalar_tensor_tensor(sdst, psrc, scale, bsrc, ALU.mult, ALU.add)
                        n = v_done(ins)
                    v_wait(n)
                    nc.vector.nop().then_inc(scores_read.sem, 1)
                    dve.tensor_reduce(mx[:, 8 * (u % 2):8 * (u % 2) + nh], s_.rearrange("p (h s) -> p h s", h=nh),
                                      AX.X, ALU.max, negate=True).then_inc(maxima_ready.sem, 1)
                    if u:
                        use(u - 1)
                use(U - 1)
                end(dve)

            @block.scalar
            def _(act):
                begin(act)

                def copy(r):
                    blocks = rounds[r][1]
                    act.wait_ge(probs_turned.sem, probs_turned.at(r + 1))
                    if r >= 2:
                        act.wait_ge(turned_copied.sem, turned_copied.at(r - 1))
                    act.activation(sbuf_t[:, r % 2, 0:len(blocks) * P], bank(4 + r % 2)[:, 0:len(blocks) * P],
                                   ACT.Copy).then_inc(turned_copied.sem, 1)

                def exps(u):
                    t, heads, sets = units[u]
                    nh = len(heads)
                    w = width[u] // nh
                    act.wait_ge(maxima_ready.sem, maxima_ready.at(u + 1))
                    if u >= 2:
                        act.wait_ge(context_read.sem, context_read.at(u - 1))
                    for i in range(nh):
                        ins = act.activation(sbuf_p[:, u % 2, i * w:(i + 1) * w], sbuf_s[:, u % 2, i * w:(i + 1) * w],
                                             ACT.Exp, bias=stat[:, 8 * (u % 2) + i:8 * (u % 2) + i + 1],
                                             accum_out=stat[:, 16 + 8 * (u % 2) + i:17 + 8 * (u % 2) + i])
                    ins.then_inc(probs_ready.sem, 1)

                exps(0)
                r = 0
                for u in range(U):
                    mine = [i for i, rd in enumerate(rounds) if rd[0] == u]
                    copy(mine[0])
                    if u + 1 < U:
                        exps(u + 1)
                    for i in mine[1:]:
                        copy(i)
                end(act)

            scores_ready.close(U)
            scores_read.close(U)
            maxima_ready.close(U)
            probs_ready.close(U)
            probs_turned.close(len(rounds))
            turned_copied.close(len(rounds))
            context_ready.close(U)
            context_read.close(U)
            close_stage()

        def turn_rows(src, dst, tiles, act_copy=False):
            banks = -(-tiles // 2)

            @block.tensor
            def _(pe):
                begin(pe)
                for b in range(banks):
                    fb = free_bank(pe, b)
                    for j in range(min(2, tiles - 2 * b)):
                        for t in range(TT):
                            mm = nc.tensor.transpose(fb[:, j * S + t * P:j * S + (t + 1) * P], src(t, 2 * b + j), ident)
                    mm.then_inc(bank_full.sem, 1)
                end(pe)

            @block.scalar
            def _(act):
                begin(act)
                end(act)

            @block.vector
            def _(dve):
                begin(dve)
                for b in range(banks):
                    n = min(2, tiles - 2 * b)
                    dve.wait_ge(bank_full.sem, bank_full.at(b + 1))
                    dve.tensor_copy(dst[:, 2 * b:2 * b + n, :].rearrange("p a s -> p (a s)"), bank(b % 4)[:, 0:n * S]) \
                       .then_inc(bank_free.sem, 1)
                end(dve)

            bank_full.close(banks)
            bank_free.close(banks)
            close_stage()

        G = region(0, 32, S)
        Y = region(8192, 4, 4, S).rearrange("p a b s -> p a b s")
        L0 = 8192 + 4096
        qk = region(L0, TT, 1024)
        idx = region(L0 + 2048, TT, IDX_COLS)
        va = region(L0 + 2704, TT, WIDTH)
        qT = region(L0 + 3728, HEADS, S)
        kT = region(L0 + 4752, HEADS, S)
        qiT = region(L0 + 5776, 2, S)
        kiT = region(L0 + 6288, S)
        score = region(L0 + 6544, TT, S)
        picked = region(L0 + 7056, TT, S)
        X0 = L0 + 7568
        glu = region(X0, 4, S + LONG - 1)
        conv_b = region(X0 + 1144, 4, S)
        gb = region(X0 + 2168, 4, S)
        vpad = region(X0 + 3192, 4, S + SHORT - 1)
        SQ = X0 + 4224
        sqT = region(SQ, HEADS, S)
        skT = region(SQ + 1024, HEADS, S)
        sv = region(SQ + 2048, TT, WIDTH)
        extra = SQ + 3072

        def mixer_rows_stage(l):
            w_in = a["w_in"][l]
            widths = [WIDTH, WIDTH, WIDTH, IDX_COLS]

            @block.tensor
            def _(pe):
                begin(pe)
                for c, wd in enumerate(widths):
                    w = take_chunk(pe, KT, wd)
                    for t in range(TT):
                        mm = rows_product(pe, 2 * c + t, w, hT, t, wd)
                        mm.then_inc(bank_full.sem, 1)
                    release_chunk(bank_full, 2 * c + 2)
                end(pe)

            @block.sync
            def _(sp):
                c0 = 0
                for wd in widths:
                    load_chunk(sp, (0, w_in[:, c0:c0 + wd]))
                    c0 += wd

            @block.scalar
            def _(act):
                begin(act)
                for c, wd in enumerate(widths):
                    for t in range(TT):
                        n = 2 * c + t
                        dst = (qk[:, t, 0:512], qk[:, t, 512:1024], va[:, t, :], idx[:, t, :])[c]
                        act.wait_ge(bank_full.sem, bank_full.at(n + 1))
                        act.activation(dst, bank(n % 4)[:, 0:wd], ACT.Copy).then_inc(bank_free.sem, 1)
                end(act)

            @block.vector
            def _(dve):
                begin(dve)
                end(dve)

            bank_full.close(8)
            bank_free.close(8)
            close_stage()

        def rotate(dve, view, t, heads, half, at, tmp):
            c = spread(rot[:, 0, t, at:at + half], 1, heads)
            s = spread(rot[:, 1, t, at:at + half], 1, heads)
            x1, x2 = view[:, :, 0:half], view[:, :, half:2 * half]
            t1, t2, t3, t4 = (tmp[:, i, 0:heads * half].rearrange("p (h f) -> p h f", h=heads) for i in range(4))
            dve.tensor_tensor(t1, x1, c, ALU.mult)
            dve.tensor_tensor(t2, x2, s, ALU.mult)
            dve.tensor_tensor(t3, x2, c, ALU.mult)
            v_link(dve.tensor_tensor(t4, x1, s, ALU.mult))
            dve.tensor_tensor(x1, t1, t2, ALU.subtract)
            v_link(dve.tensor_tensor(x2, t3, t4, ALU.add))

        def mixer_columns_stage(l):
            w_in = a["w_in"][l]
            starts = [W_GLU, W_GLU + 512, W_CC, W_CC + 512, W_CC + 1024, W_SQ, W_SQ + 512]

            @block.tensor
            def _(pe):
                begin(pe)
                n = 0
                for c in range(len(starts)):
                    w = take_chunk(pe, KT, 512)
                    for j in range(2):
                        columns_product(pe, n, w, hT, (2 * j * P, (2 * j + 1) * P)).then_inc(bank_full.sem, 1)
                        n += 1
                    release_chunk(bank_full, n)
                w = take_chunk(pe, KT, 512)
                for t in range(TT):
                    rows_product(pe, n, w, hT, t, 512).then_inc(bank_full.sem, 1)
                    n += 1
                release_chunk(bank_full, n)
                end(pe)

            @block.sync
            def _(sp):
                for c0 in starts + [W_SV]:
                    load_chunk(sp, (0, w_in[:, c0:c0 + 512]))

            @block.scalar
            def _(act):
                begin(act)
                n = 0
                for c, (dst, off) in enumerate(((glu, LONG - 1), (conv_b, 0), (gb, 0), (vpad, SHORT - 1), (Y[:, 2], 0),
                                                (sqT, 0), (skT, 0))):
                    for j in range(2):
                        act.wait_ge(bank_full.sem, bank_full.at(n + 1))
                        act.activation(dst[:, 2 * j:2 * j + 2, off:off + S], bank(n % 4).rearrange("p (j s) -> p j s", j=2),
                                       ACT.Sigmoid if c == 1 else ACT.Copy).then_inc(bank_free.sem, 1)
                        n += 1
                        if n == 2:
                            square_root(act, stat[:, 84:102], stat[:, 102:120], 1)
                for t in range(TT):
                    act.wait_ge(bank_full.sem, bank_full.at(n + 1))
                    act.activation(sv[:, t, :], bank(n % 4), ACT.Copy).then_inc(bank_free.sem, 1)
                    n += 1
                end(act)

            @block.vector
            def _(dve):
                begin(dve)
                dve.memset(glu[:, :, 0:LONG - 1], 0.0)
                dve.memset(vpad[:, :, 0:SHORT - 1], 0.0)
                sq = region(0, 8, P)
                tmp = region(1024, 4, P)
                squares = stat[:, 48:66].rearrange("p (t h) -> p t h", t=TT)
                for t in range(TT):
                    view = qk[:, t, :].rearrange("p (h d) -> p h d", h=8)
                    ki = idx[:, t, 256:320]
                    v_link(dve.tensor_tensor(sq, view, view, ALU.mult))
                    v_link(dve.tensor_reduce(squares[:, t, 0:8], sq, AX.X, ALU.add))
                    v_link(dve.tensor_tensor(sq[:, 0, 0:IDX_DIM], ki, ki, ALU.mult))
                    v_link(dve.tensor_reduce(squares[:, t, 8:9], sq[:, 0, 0:IDX_DIM], AX.X, ALU.add))
                    v_link(dve.tensor_scalar(squares[:, t, 8:9], squares[:, t, 8:9], float(P) / IDX_DIM, None, ALU.mult))
                inverse_root(dve, stat[:, 120:138], stat[:, 84:102], stat[:, 102:120], stat[:, 48:66], 1.0 / P, 1)
                roots = stat[:, 120:138].rearrange("p (t h) -> p t h", t=TT)
                for t in range(TT):
                    view = qk[:, t, :].rearrange("p (h d) -> p h d", h=8)
                    ki = idx[:, t, 256:320]
                    v_link(dve.tensor_tensor(view, view, spread(roots[:, t, 0:8], 2, P), ALU.mult))
                    dve.tensor_tensor(view[:, 0:4], view[:, 0:4], spread(g_head[:, l, 0, :], 1, HEADS), ALU.mult)
                    v_link(dve.tensor_tensor(view[:, 4:8], view[:, 4:8], spread(g_head[:, l, 1, :], 1, HEADS), ALU.mult))
                    rotate(dve, view, t, 8, 16, 0, tmp)
                    v_link(dve.scalar_tensor_tensor(ki, ki, roots[:, t, 8:9], g_kidx[:, l, :], ALU.mult, ALU.mult))
                    rotate(dve, idx[:, t, 0:320].rearrange("p (h d) -> p h d", h=5), t, 5, 8, 16, tmp)
                end(dve)

            bank_full.close(16)
            bank_free.close(16)
            close_roots(1)
            close_stage()

        def mixer_turn_stage(l):
            kk = region(0, TT, P)
            srcs = []
            for h in range(8):
                dst = qT[:, h, :] if h < 4 else kT[:, h - 4, :]
                srcs.append((lambda t, h=h: qk[:, t, h * P:(h + 1) * P], dst))
            for h in range(2):
                srcs.append((lambda t, h=h: idx[:, t, h * P:(h + 1) * P], qiT[:, h, :]))
            srcs.append((lambda t: kk[:, t, :], kiT))

            @block.vector
            def _(dve):
                begin(dve)
                kd = kk.rearrange("p t (a d) -> p t a d", a=2)
                for t in range(TT):
                    ins = dve.tensor_copy(kd[:, t], spread(idx[:, t, 256:320], 1, 2))
                    ins.then_inc(operand_ready.sem, 1)
                dve.tensor_tensor(glu[:, :, LONG - 1:], glu[:, :, LONG - 1:], conv_b, ALU.mult)
                dve.tensor_tensor(vpad[:, :, SHORT - 1:], vpad[:, :, SHORT - 1:], Y[:, 2], ALU.mult)
                for n in range(0, len(srcs), 2):
                    dve.wait_ge(bank_full.sem, bank_full.at(n // 2 + 1))
                    for j, (_, dst) in enumerate(srcs[n:n + 2]):
                        ins = dve.tensor_copy(dst, bank(n // 2 % 4)[:, j * S:(j + 1) * S])
                    ins.then_inc(bank_free.sem, 1)
                end(dve)

            @block.scalar
            def _(act):
                begin(act)
                end(act)

            @block.tensor
            def _(pe):
                begin(pe)
                for n in range(0, len(srcs), 2):
                    b = free_bank(pe, n // 2)
                    if n == len(srcs) - 1:
                        pe.wait_ge(operand_ready.sem, operand_ready.at(TT))
                    for j, (src, _) in enumerate(srcs[n:n + 2]):
                        for t in range(TT):
                            mm = nc.tensor.transpose(b[:, j * S + t * P:j * S + (t + 1) * P], src(t), ident)
                    mm.then_inc(bank_full.sem, 1)
                end(pe)

            operand_ready.close(TT)
            bank_full.close(6)
            bank_free.close(6)
            close_stage()

        def gates_stage(l):
            w_in = a["w_in"][l]

            def index_scores(t, h):
                L = (t + 1) * P
                return bank((6, 4)[t] + h % 2)[:, (h // 2) * L:(h // 2 + 1) * L]

            @block.tensor
            def _(pe):
                begin(pe)
                for h in range(HEADS):
                    lo = IDX_DIM * (h % 2)
                    for t in range(TT):
                        dst = index_scores(t, h)
                        mm = nc.tensor.matmul(dst, qiT[lo:lo + IDX_DIM, h // 2, t * P:(t + 1) * P],
                                              kiT[lo:lo + IDX_DIM, 0:(t + 1) * P], start=True, stop=True)
                mm.then_inc(side_full.sem, 1)
                n = 0
                for c in range(8):
                    w = take_chunk(pe, KT, 512)
                    for j in range(2):
                        columns_product(pe, n, w, hT, (2 * j * P, (2 * j + 1) * P)).then_inc(bank_full.sem, 1)
                        n += 1
                    release_chunk(bank_full, n)
                pe.wait_ge(operand_ready.sem, operand_ready.at(1))
                for ct in range(4):
                    mm = nc.tensor.matmul(bank(7)[:, 0:S], cst[:, C_MEAN:C_MEAN + P], conv_b[:, ct, :],
                                          start=(ct == 0), stop=(ct == 3))
                mm.then_inc(side_full.sem, 1)
                pe.wait_ge(operand_ready.sem, operand_ready.at(2))
                for ct in range(4):
                    mm = nc.tensor.matmul(bank(7)[:, S:2 * S], cst[:, C_MEAN:C_MEAN + P], glu[:, ct, 0:S],
                                          start=(ct == 0), stop=(ct == 3))
                mm.then_inc(side_full.sem, 1)
                end(pe)

            @block.sync
            def _(sp):
                for c in range(8):
                    load_chunk(sp, (0, w_in[:, W_GATE + c * 512:W_GATE + (c + 1) * 512]))

            @block.scalar
            def _(act):
                begin(act)
                for n in range(16):
                    act.wait_ge(bank_full.sem, bank_full.at(n + 1))
                    for j in range(2):
                        g = 2 * n + j
                        col = R_MISC(l) + M_GATE + g
                        ins = act.activation(G[:, g, :], bank(n % 4)[:, j * S:(j + 1) * S], ACT.Sigmoid,
                                             bias=par[:, col:col + 1])
                    ins.then_inc(bank_free.sem, 1)
                square_root(act, gb[:, 1, :], gb[:, 2, :], 1)
                act.wait_ge(operand_ready.sem, operand_ready.at(3))
                for ct in range(4):
                    cg, cb = R_MISC(l) + M_LNG + ct, R_MISC(l) + M_LNB + ct
                    act.activation(Y[:, 1, ct, :], conv_b[:, ct, :], ACT.Silu, bias=par[:, cb:cb + 1],
                                   scale=par[:, cg:cg + 1])
                end(act)

            @block.vector
            def _(dve):
                begin(dve)
                last = [0] * 4
                for k in range(SHORT):
                    for ct in range(4):
                        col = R_MISC(l) + M_CC + 4 * k + ct
                        tap = par[:, col:col + 1]
                        if k == 0:
                            ins = dve.tensor_scalar(Y[:, 2, ct, :], vpad[:, ct, 0:S], tap, None, ALU.mult)
                        else:
                            v_wait(last[ct])
                            ins = dve.scalar_tensor_tensor(Y[:, 2, ct, :], vpad[:, ct, k:k + S], tap, Y[:, 2, ct, :],
                                                           ALU.mult, ALU.add)
                        last[ct] = v_done(ins)
                v_wait(last[3])
                dve.tensor_tensor(Y[:, 2], Y[:, 2], gb, ALU.mult)
                v_link(dve.memset(score[:, 0, P:S], NEG))
                dve.wait_ge(side_full.sem, side_full.at(1))
                tmp = picked
                for t in range(TT):
                    L = (t + 1) * P
                    for h in range(HEADS):
                        src = index_scores(t, h)
                        w = idx[:, t, 320 + h:321 + h]
                        if h == 0:
                            v_link(dve.tensor_scalar(score[:, t, 0:L], src, 0.0, w, ALU.max, ALU.mult))
                        else:
                            v_link(dve.tensor_scalar(tmp[:, t, 0:L], src, 0.0, w, ALU.max, ALU.mult))
                            v_link(dve.tensor_tensor(score[:, t, 0:L], score[:, t, 0:L], tmp[:, t, 0:L], ALU.add))
                    v_link(dve.tensor_tensor(score[:, t, t * P:L], score[:, t, t * P:L], cst[:, C_CAUS:C_CAUS + P],
                                             ALU.add))
                top = stat[:, 64:80].rearrange("p (t e) -> p t e", t=TT)
                for r in range(TOPK // 8):
                    n = [v_done(dve.max(top[:, t, :], score[:, t, :])) for t in range(TT)]
                    for t in range(TT):
                        v_wait(n[t])
                        n[t] = v_done(dve.match_replace(score[:, t, :], top[:, t, :], score[:, t, :], TAKEN))
                    v_wait(n[-1])
                v_link(dve.tensor_scalar(picked, score, 0.5 * TAKEN, NEG, ALU.is_gt, ALU.mult))
                for t in range(TT):
                    last_ = v_done(dve.tensor_tensor(picked[:, t, t * P:(t + 1) * P], picked[:, t, t * P:(t + 1) * P],
                                                     cst[:, C_CAUS:C_CAUS + P], ALU.add))
                last = [0] * 4
                for k in range(LONG):
                    for ct in range(4):
                        tap = par[:, R_LONG(l) + 4 * k + ct:R_LONG(l) + 4 * k + ct + 1]
                        if k == 0:
                            cb = R_MISC(l) + M_CB + ct
                            ins = dve.tensor_scalar(conv_b[:, ct, :], glu[:, ct, 0:S], tap, par[:, cb:cb + 1],
                                                    ALU.mult, ALU.add)
                        else:
                            v_wait(last[ct])
                            ins = dve.scalar_tensor_tensor(conv_b[:, ct, :], glu[:, ct, k:k + S], tap, conv_b[:, ct, :],
                                                           ALU.mult, ALU.add)
                        last[ct] = v_done(ins)
                v_wait(last[3])
                nc.vector.nop().then_inc(operand_ready.sem, 1)
                dve.wait_ge(side_full.sem, side_full.at(2))
                v_link(dve.tensor_tensor(conv_b, conv_b, spread(bank(7)[:, 0:S], 1, 4), ALU.subtract))
                dve.tensor_tensor(glu[:, :, 0:S], conv_b, conv_b, ALU.mult).then_inc(operand_ready.sem, 1)
                dve.wait_ge(side_full.sem, side_full.at(3))
                rstd = gb[:, 0, :]
                inverse_root(dve, rstd, gb[:, 1, :], gb[:, 2, :], bank(7)[:, S:2 * S], 1.0, 1)
                dve.tensor_tensor(conv_b, conv_b, spread(rstd, 1, 4), ALU.mult).then_inc(operand_ready.sem, 1)
                end(dve)

            side_full.close(3)
            operand_ready.close(3)
            close_roots(1)
            bank_full.close(16)
            bank_free.close(16)
            close_stage()

        def sparse_attention_stage(l):
            sbuf_s = region(X0, 2, 512)
            sbuf_p = region(X0 + 1024, 2, 512)
            sbuf_t = region(X0 + 2048, 2, 512)
            ctx_rows = region(X0 + 3072, TT, WIDTH)
            units = [(1, (0, 1), (0,)), (1, (2, 3), (0,)), (0, (0, 1, 2, 3), (0,))]

            def bias(u, unit, sc, dst, L):
                t, heads, _ = unit
                n = len(heads)
                yield (sc.rearrange("p (h s) -> p h s", h=n), dst.rearrange("p (h s) -> p h s", h=n),
                       spread(picked[:, t, 0:L], 1, n))

            def finish(dve, u, unit, res, rec):
                t, heads, _ = unit
                n = len(heads)
                o = ctx_rows[:, t, heads[0] * P:(heads[0] + n) * P].rearrange("p (h d) -> p h d", h=n)
                dve.tensor_tensor(o, res.rearrange("p (h d) -> p h d", h=n), spread(rec, 2, P), ALU.mult) \
                   .then_inc(context_read.sem, 1)

            attention(units, lambda h, st, t: qT[:, h, t * P:(t + 1) * P], lambda h, st: kT[:, h, :],
                      lambda st, kt, h: va[:, kt, h * P:(h + 1) * P], bias, float(P) ** -0.5, P,
                      (sbuf_s, sbuf_p, sbuf_t), finish, 0)
            turn_rows(lambda t, j: ctx_rows[:, t, j * P:(j + 1) * P], Y[:, 0], 4)

        def stick_breaking_stage():
            W = S + P
            z = region(X0, HEADS, W)
            lk = region(X0 + HEADS * W, HEADS, W)
            soft = region(L0, HEADS, W)

            @block.tensor
            def _(pe):
                begin(pe)
                for h in range(HEADS):
                    b = bank(h)
                    nc.tensor.matmul(b[:, 0:S], skT[:, h, 0:P], sqT[:, h, :], start=True, stop=True)
                    nc.tensor.matmul(b[:, S:W], skT[:, h, P:S], sqT[:, h, P:S], start=True, stop=True) \
                      .then_inc(scores_ready.sem, 1)
                for h in range(HEADS):
                    pe.wait_ge(operand_ready.sem, operand_ready.at(h + 1))
                    b = bank(4 + h)
                    tri, one = cst[:, C_TRI:C_TRI + P], cst[:, C_ONE:C_ONE + P]
                    nc.tensor.matmul(b[:, 0:S], tri, lk[:, h, 0:S], start=True, stop=False)
                    nc.tensor.matmul(b[:, P:S], one, lk[:, h, S:W], start=False, stop=True)
                    nc.tensor.matmul(b[:, S:W], tri, lk[:, h, S:W], start=True, stop=True) \
                      .then_inc(side_full.sem, 1)
                for h in range(HEADS):
                    pe.wait_ge(probs_ready.sem, probs_ready.at(h + 1))
                    b = bank(h)
                    nc.tensor.matmul(b[:, 0:S], sv[:, 0, h * P:(h + 1) * P], lk[:, h, 0:S], start=True, stop=False)
                    nc.tensor.matmul(b[:, P:S], sv[:, 1, h * P:(h + 1) * P], lk[:, h, S:W], start=False, stop=True) \
                      .then_inc(context_ready.sem, 1)
                end(pe)

            @block.vector
            def _(dve):
                begin(dve)
                scale = float(P) ** -0.5
                dst = lk
                for h in range(HEADS):
                    dve.wait_ge(scores_ready.sem, scores_ready.at(h + 1))
                    v_link(dve.tensor_scalar(z[:, h, :], bank(h)[:, 0:W], scale, None, ALU.mult))
                    dve.scalar_tensor_tensor(soft[:, h, :], z[:, h, :], -1.0, z[:, h, :], ALU.mult, ALU.min) \
                       .then_inc(inner_taken.sem, 1)
                for h in range(HEADS):
                    dve.wait_ge(inner_ready.sem, inner_ready.at(h + 1))
                    v_link(dve.scalar_tensor_tensor(lk[:, h, :], z[:, h, :], 0.0, soft[:, h, :], ALU.max, ALU.add))
                    keep, neg = cst[:, C_SKEEP:C_SKEEP + P], cst[:, C_SNEG:C_SNEG + P]
                    v_link(dve.tensor_scalar(lk[:, h, :], lk[:, h, :], -1.0, None, ALU.mult))
                    for c in (0, S):
                        dve.tensor_tensor(z[:, h, c:c + P], z[:, h, c:c + P], neg, ALU.add)
                        n = v_done(dve.tensor_tensor(lk[:, h, c:c + P], lk[:, h, c:c + P], keep, ALU.mult))
                    v_wait(n)
                    nc.vector.nop().then_inc(operand_ready.sem, 1)
                for h in range(HEADS):
                    dve.wait_ge(side_full.sem, side_full.at(h + 1))
                    dve.tensor_tensor(z[:, h, :], z[:, h, :], bank(4 + h)[:, 0:W], ALU.add).then_inc(side_free.sem, 1)
                for h in range(HEADS):
                    dve.wait_ge(context_ready.sem, context_ready.at(h + 1))
                    dve.tensor_copy(Y[:, 3, h, :], bank(h)[:, 0:S])
                end(dve)

            @block.scalar
            def _(act):
                begin(act)
                done = []
                for h in range(HEADS):
                    act.wait_ge(inner_taken.sem, inner_taken.at(h + 1))
                    done.append(s_done(act.activation(soft[:, h, :], soft[:, h, :], ACT.Exp)))
                for h in range(HEADS):
                    s_wait(done[h])
                    act.activation(soft[:, h, :], soft[:, h, :], ACT.Ln, bias=1.0).then_inc(inner_ready.sem, 1)
                for h in range(HEADS):
                    act.wait_ge(side_free.sem, side_free.at(h + 1))
                    act.activation(lk[:, h, :], z[:, h, :], ACT.Exp).then_inc(probs_ready.sem, 1)
                end(act)

            scores_ready.close(HEADS)
            inner_taken.close(HEADS)
            inner_ready.close(HEADS)
            operand_ready.close(HEADS)
            side_full.close(HEADS)
            side_free.close(HEADS)
            probs_ready.close(HEADS)
            context_ready.close(HEADS)
            close_stage()

        def branch_output_stage(l):
            names = ("w_oa", "w_ob", "w_oc", "w_od")

            @block.tensor
            def _(pe):
                begin(pe)
                n = 0
                for i in range(4):
                    w = take_chunk(pe, 4, D)
                    for j in range(4):
                        b = free_bank(pe, n)
                        for m in range(2):
                            c = (2 * j + m) * P
                            for k in range(4):
                                mm = nc.tensor.matmul(b[:, m * S:(m + 1) * S], w[:, k, c:c + P], Y[:, i, k, :],
                                                      start=(k == 0), stop=(k == 3))
                        mm.then_inc(bank_full.sem, 1)
                        n += 1
                    release_chunk(bank_full, n)
                end(pe)

            @block.sync
            def _(sp):
                for name in names:
                    load_chunk(sp, (0, a[name][l]))

            @block.scalar
            def _(act):
                begin(act)
                end(act)

            @block.vector
            def _(dve):
                begin(dve)
                for n in range(16):
                    i, j = n // 4, n % 4
                    g = G[:, 8 * i + 2 * j:8 * i + 2 * j + 2, :].rearrange("p a s -> p (a s)")
                    m = hT[:, 2 * j:2 * j + 2, :].rearrange("p a s -> p (a s)")
                    dve.wait_ge(bank_full.sem, bank_full.at(n + 1))
                    if i == 0:
                        v_link(dve.tensor_tensor(m, g, bank(n % 4), ALU.mult))
                    else:
                        v_link(dve.tensor_tensor(g, g, bank(n % 4), ALU.mult))
                        v_link(dve.tensor_tensor(m, m, g, ALU.add))
                    nc.vector.nop().then_inc(bank_free.sem, 1)
                end(dve)

            bank_full.close(16)
            bank_free.close(16)
            close_stage()

        fT = region(0, FT, S)

        def compressed_attention_layer():
            w_in = a["a_w_in_2"][0]
            table = region(0, QH, S)
            q2 = region(4096, KT, S)
            kcmp = region(6144, 2, GROUPS, S).rearrange("p a g s -> p a g s")
            kd = region(8192, 2, GROUPS, S).rearrange("p a g s -> p a g s")
            vv = region(10240, 2, TT, S).rearrange("p a g s -> p a g s")
            gl = region(11264, TT, 3 * QH)
            o = region(11360, TT, D)
            c0 = 13408
            blk = region(c0, CMP_BLOCK // 2, P)
            pairs = region(c0, 4, 2, S)
            hid = region(c0 + 2048, CMP_HIDDEN)
            hid2 = region(c0 + 2304, CMP_HIDDEN)
            hidT = region(c0 + 2560, 2, P)
            kcT = region(c0 + 2816, P)
            vc = region(c0 + 2944, GROUPS, DH)
            cbias = region(c0 + 3200, TT, CMP_N, QH)
            cprob = region(c0 + 3680, TT, QH, CMP_PAD)
            w2 = region(c0 + 4704, 2, 2, DH)
            relb = region(c0 + 4960, QH)
            onehot = region(c0 + 4976, 512)
            sbuf_s = region(c0 + 5488, 2, 512)
            sbuf_p = region(c0 + 6512, 2, 512)
            sbuf_t = region(c0 + 7536, 2, 512)
            assert CMP_N <= CMP_PAD

            @block.gpsimd
            def _(pool):
                pool.wait_ge(stage_done.sem, COMPUTE * stage[0])
                pool.wait_ge(side_store.sem, side_store.at(0))
                pool.memset(work[0:BUCKETS + 1, c0 + 4960:c0 + 4976], NEG).then_inc(operand_ready.sem, 1)
                pool.wait_ge(operand_ready.sem, operand_ready.at(1))
                src = bass.AP(table_dram.tensor, P - 1, [[SPAN, P], [HEAD_SKEW, QH], [1, S]])
                pool.dma_start(table, src).then_inc(table_load.sem, 16)
                pool.dma_start(work[0:BUCKETS, c0 + 4960:c0 + 4976], a["rel_bias_2"]).then_inc(table_load.sem, 16)
                pool.dma_start(onehot[0:BUCKETS + 1, :], onehots[:, O_CMP:O_CMP + 512]).then_inc(table_load.sem, 16)
                for n, name in enumerate(("a_w2_k_2", "a_w2_v_2")):
                    pool.dma_start(w2[:, n], a[name][0].rearrange("(k p) d -> p k d", p=P)).then_inc(table_load.sem, 16)

            @block.tensor
            def _(pe):
                begin(pe)
                n = 0
                for c in range(2):
                    w = take_chunk(pe, KT, 512)
                    for j in range(2):
                        columns_product(pe, n, w, hT, (2 * j * P, (2 * j + 1) * P)).then_inc(bank_full.sem, 1)
                        n += 1
                    release_chunk(bank_full, n)
                w = take_chunk(pe, KT, 512)
                for i in range(2):
                    columns_product(pe, n, w, hT, (2 * i * P, (2 * i + 1) * P)).then_inc(bank_full.sem, 1)
                    n += 1
                release_chunk(bank_full, n)
                take_chunk(pe, KT, 256, 0, 2)
                for i in range(2):
                    w = chunk_view(KT, 256, i * KT * 256)
                    columns_product(pe, n, w, hT, (0, P)).then_inc(bank_full.sem, 1)
                    n += 1
                release_chunk(bank_full, n)
                take_chunk(pe, KT, 256, 0, 2)
                for i in range(2):
                    w = chunk_view(KT, 256, i * KT * 256)
                    for t in range(TT):
                        rows_product(pe, n, w, hT, t, 256).then_inc(bank_full.sem, 1)
                        n += 1
                release_chunk(bank_full, n)
                w = take_chunk(pe, KT, 48)
                for t in range(TT):
                    rows_product(pe, n, w, hT, t, 48).then_inc(bank_full.sem, 1)
                    n += 1
                release_chunk(bank_full, n)
                two_halves(pe, n, pairs, 4)
                pe.wait_ge(table_load.sem, table_load.at(5 * 16))
                for t in range(TT):
                    for m in range(CMP_N):
                        d0 = (S - 1) + t * P - CMP_STRIDE * m - (CMP_BLOCK - 1)
                        mm = nc.tensor.matmul(bank(4 + t)[:, m * QH:(m + 1) * QH], onehot[0:BUCKETS + 1, d0:d0 + P],
                                              relb[0:BUCKETS + 1, :], start=True, stop=True)
                mm.then_inc(side_full.sem, 1)
                end(pe)

            @block.sync
            def _(sp):
                for c in range(2):
                    load_chunk(sp, (0, w_in[:, c * 512:(c + 1) * 512]))
                load_chunk(sp, (0, w_in[:, A_KC:A_KC + 512]))
                load_chunk(sp, (0, w_in[:, A_KS:A_KS + 256]), (KT * 256, w_in[:, A_KW:A_KW + 256]))
                load_chunk(sp, (0, w_in[:, A_VS:A_VS + 256]), (KT * 256, w_in[:, A_VW:A_VW + 256]))
                load_chunk(sp, (0, w_in[:, A_GL:A_GL + 48]))
                for name in ("a_w1_k_2", "a_w1_v_2"):
                    load_chunk(sp, (0, a[name][0]))

            @block.scalar
            def _(act):
                begin(act)
                n = 0
                for c in range(4):
                    act.wait_ge(bank_full.sem, bank_full.at(n + 1))
                    act.activation(q2[:, 2 * c:2 * c + 2, :].rearrange("p a s -> p (a s)"), bank(n % 4), ACT.Copy) \
                       .then_inc(bank_free.sem, 1)
                    n += 1
                for i in range(4):
                    act.wait_ge(bank_full.sem, bank_full.at(n + 1))
                    act.activation(pairs[:, i].rearrange("p a s -> p (a s)"), bank(n % 4), ACT.Copy) \
                       .then_inc(bank_free.sem, 1)
                    n += 1
                act.wait_ge(bank_free.sem, bank_free.at(n))
                nc.scalar.nop().then_inc(inner_ready.sem, 1)
                for i in range(2):
                    for t in range(TT):
                        act.wait_ge(bank_full.sem, bank_full.at(n + 1))
                        act.activation(vv[:, i, t, :], bank(n % 4)[:, 0:256], ACT.Copy).then_inc(bank_free.sem, 1)
                        n += 1
                for t in range(TT):
                    act.wait_ge(bank_full.sem, bank_full.at(n + 1))
                    act.activation(gl[:, t, :], bank(n % 4)[:, 0:3 * QH], ACT.Copy).then_inc(bank_free.sem, 1)
                    n += 1
                for i in range(4):
                    for gp in range(2):
                        act.wait_ge(bank_full.sem, bank_full.at(n + 1))
                        b = bank(n % 4).rearrange("p (j s) -> p j s", j=2)
                        if i < 2:
                            act.activation(kcmp[0:DH, i, 2 * gp:2 * gp + 2, :], b[0:DH], ACT.Copy)
                            ins = act.activation(kcmp[DH:P, i, 2 * gp:2 * gp + 2, 0:S - 1], b[DH:P, :, 1:S], ACT.Copy)
                        else:
                            ins = act.activation(kd[:, i - 2, 2 * gp:2 * gp + 2, :], b, ACT.Copy)
                        ins.then_inc(bank_free.sem, 1)
                        n += 1
                end(act)

            @block.vector
            def _(dve):
                begin(dve)
                dve.wait_ge(bank_free.sem, bank_free.at(14))
                dve.tensor_tensor(gl, gl, spread(b_gl[:, :], 1, TT), ALU.add)
                dve.wait_ge(side_full.sem, side_full.at(1))
                for t in range(TT):
                    dve.tensor_copy(cbias[:, t].rearrange("p n h -> p (n h)"), bank(4 + t)[:, 0:CMP_N * QH])
                end(dve)

            bank_full.close(22)
            bank_free.close(22)
            inner_ready.close(1)
            operand_ready.close(1)
            table_load.close(5 * 16)
            side_full.close(1)
            close_stage()

            for i in range(2):
                pe_col = R_PART2 + (M2_PEK, M2_PEV)[i]

                @block.vector
                def _(dve):
                    begin(dve)
                    v_link(dve.memset(blk, 0.0))
                    bv = blk.rearrange("p m (g n) -> p m g n", g=GROUPS)
                    for m in range(CMP_BLOCK // 2):
                        src = kcmp[:, i, :, 2 * m:2 * m + CMP_STRIDE * (CMP_N - 1) + 1:CMP_STRIDE]
                        ins = dve.tensor_scalar(bv[:, m, :, 0:CMP_N], src, par[:, pe_col + m:pe_col + m + 1], None, ALU.add)
                    ins.then_inc(operand_ready.sem, 1)
                    dve.wait_ge(side_full.sem, side_full.at(1))
                    v_link(dve.tensor_copy(hid, bank(0)[:, 0:CMP_HIDDEN]))
                    v_link(dve.tensor_tensor(hid2, hid, hid, ALU.mult))
                    v_link(dve.tensor_scalar(hid2, hid2, 0.044715, 1.0, ALU.mult, ALU.add))
                    dve.tensor_tensor(hid2, hid2, hid, ALU.mult).then_inc(operand_ready.sem, 1)
                    dve.wait_ge(inner_ready.sem, inner_ready.at(1))
                    v_link(dve.tensor_scalar(hid2, hid2, 1.0, 0.5, ALU.add, ALU.mult))
                    dve.tensor_tensor(hid, hid, hid2, ALU.mult).then_inc(operand_ready.sem, 1)
                    dve.wait_ge(side_full.sem, side_full.at(2))
                    dve.tensor_copy(hidT.rearrange("p a b -> p (a b)"), bank(1)[:, 0:2 * P]).then_inc(operand_ready.sem, 1)
                    dve.wait_ge(side_full.sem, side_full.at(3))
                    if i == 0:
                        dve.tensor_copy(kcT, bank(2)[:, 0:P])
                    else:
                        for g in range(GROUPS):
                            ins = dve.tensor_copy(vc[0:CMP_PAD, g, :], bank(2)[0:CMP_PAD, g * DH:(g + 1) * DH])
                    end(dve)

                @block.scalar
                def _(act):
                    begin(act)
                    act.wait_ge(operand_ready.sem, operand_ready.at(2))
                    act.activation(hid2, hid2, ACT.Tanh, scale=math.sqrt(2.0 / math.pi)).then_inc(inner_ready.sem, 1)
                    end(act)

                @block.tensor
                def _(pe):
                    begin(pe)
                    pe.wait_ge(operand_ready.sem, operand_ready.at(1))
                    w = take_chunk(pe, CMP_BLOCK // 2, CMP_HIDDEN)
                    for m in range(CMP_BLOCK // 2):
                        mm = nc.tensor.matmul(bank(0)[:, 0:CMP_HIDDEN], blk[:, m, :], w[:, m, :], start=(m == 0),
                                              stop=(m == CMP_BLOCK // 2 - 1))
                    mm.then_inc(side_full.sem, 1)
                    release_chunk(side_full, 1)
                    pe.wait_ge(operand_ready.sem, operand_ready.at(3))
                    for k in range(2):
                        mm = nc.tensor.transpose(bank(1)[:, k * P:(k + 1) * P], hid[:, k * P:(k + 1) * P], ident)
                    mm.then_inc(side_full.sem, 1)
                    pe.wait_ge(operand_ready.sem, operand_ready.at(4))
                    if i == 0:
                        for lo in (0, DH):
                            for k in range(2):
                                mm = nc.tensor.matmul(bank(2)[lo:lo + DH, 0:P], w2[:, 0, k, :], hidT[:, k, :],
                                                      start=(k == 0), stop=(k == 1))
                    else:
                        for g in range(GROUPS):
                            for k in range(2):
                                mm = nc.tensor.matmul(bank(2)[0:CMP_PAD, g * DH:(g + 1) * DH],
                                                      hidT[:, k, g * CMP_PAD:(g + 1) * CMP_PAD], w2[:, 1, k, :],
                                                      start=(k == 0), stop=(k == 1))
                    mm.then_inc(side_full.sem, 1)
                    end(pe)

                operand_ready.close(4)
                inner_ready.close(1)
                side_full.close(3)
                close_stage()

            @block.tensor
            def _(pe):
                begin(pe)
                for t in range(TT):
                    for h in range(QH):
                        lo, g = DH * (h % 2), h // PER_GROUP
                        mm = nc.tensor.matmul(bank(2 * (h % 2) + t)[:, (h // 2) * CMP_PAD:(h // 2 + 1) * CMP_PAD],
                                              q2[lo:lo + DH, h // 2, t * P:(t + 1) * P],
                                              kcT[lo:lo + DH, g * CMP_PAD:(g + 1) * CMP_PAD], start=True, stop=True)
                    mm.then_inc(scores_ready.sem, 1)
                pe.wait_ge(operand_ready.sem, operand_ready.at(TT))
                for t in range(TT):
                    for hb in range(4):
                        n = 4 * t + hb
                        if n >= 2:
                            pe.wait_ge(turned_copied.sem, turned_copied.at(n - 1))
                        for j in range(4):
                            mm = nc.tensor.transpose(bank(n % 2)[0:CMP_PAD, j * P:(j + 1) * P],
                                                     cprob[:, t, 4 * hb + j, :], ident)
                        mm.then_inc(probs_turned.sem, 1)
                        pe.wait_ge(turned_copied.sem, turned_copied.at(n + 1))
                        for j in range(4):
                            h = 4 * hb + j
                            b = bank(4 + 2 * t + h // 8)
                            mm = nc.tensor.matmul(b[:, (h % 8) * DH:(h % 8 + 1) * DH],
                                                  sbuf_t[0:CMP_PAD, n % 2, j * P:(j + 1) * P], vc[0:CMP_PAD, hb, :],
                                                  start=True, stop=True)
                    mm.then_inc(context_ready.sem, 1)
                end(pe)

            @block.scalar
            def _(act):
                begin(act)
                act.activation(gl.rearrange("p t c -> p (t c)"), gl.rearrange("p t c -> p (t c)"), ACT.Sigmoid)
                for t in range(TT):
                    act.wait_ge(maxima_ready.sem, maxima_ready.at(t + 1))
                    act.activation(cprob[:, t, :, 0:CMP_N], cprob[:, t, :, 0:CMP_N], ACT.Exp) \
                       .then_inc(probs_ready.sem, 1)
                for n in range(8):
                    act.wait_ge(probs_turned.sem, probs_turned.at(n + 1))
                    act.activation(sbuf_t[0:CMP_PAD, n % 2, :], bank(n % 2)[0:CMP_PAD, :], ACT.Copy) \
                       .then_inc(turned_copied.sem, 1)
                end(act)

            @block.vector
            def _(dve):
                begin(dve)
                v_link(dve.memset(cprob.rearrange("p t h n -> p (t h n)"), 0.0))
                for t in range(TT):
                    dve.wait_ge(scores_ready.sem, scores_ready.at(t + 1))
                    pr = cprob[:, t, :, 0:CMP_N]
                    for j in range(2):
                        sc = bank(2 * j + t)[:, 0:QH // 2 * CMP_PAD].rearrange("p (h n) -> p h n", n=CMP_PAD)[:, :, 0:CMP_N]
                        v_link(dve.scalar_tensor_tensor(pr[:, j:QH:2], sc, DH ** -0.5,
                                                        cbias[:, t, :, j:QH:2].rearrange("p n h -> p h n"),
                                                        ALU.mult, ALU.add))
                    mx = stat[:, 0:QH]
                    v_link(dve.tensor_reduce(mx, pr, AX.X, ALU.max))
                    dve.tensor_tensor(pr, pr, spread(mx, 2, CMP_N), ALU.subtract).then_inc(maxima_ready.sem, 1)
                    dve.wait_ge(probs_ready.sem, probs_ready.at(t + 1))
                    keep = cst[:, C_CMP + t * CMP_N:C_CMP + (t + 1) * CMP_N]
                    v_link(dve.tensor_tensor(pr, pr, spread(keep, 1, QH), ALU.mult))
                    v_link(dve.tensor_reduce(mx, pr, AX.X, ALU.add))
                    v_link(dve.tensor_scalar(mx, mx, 1e-30, None, ALU.max))
                    v_link(dve.reciprocal(mx, mx))
                    dve.tensor_tensor(pr, pr, spread(mx, 2, CMP_N), ALU.mult).then_inc(operand_ready.sem, 1)
                for t in range(TT):
                    dve.wait_ge(context_ready.sem, context_ready.at(t + 1))
                    g = gl[:, t, :].rearrange("p (h c) -> p h c", c=3)
                    dve.tensor_tensor(o[:, t, :].rearrange("p (h d) -> p h d", h=QH),
                                      bank(4 + 2 * t, 2).rearrange("p (h d) -> p h d", h=QH),
                                      spread(g[:, :, 0], 2, DH), ALU.mult)
                end(dve)

            scores_ready.close(TT)
            maxima_ready.close(TT)
            probs_ready.close(TT)
            operand_ready.close(TT)
            probs_turned.close(8)
            turned_copied.close(8)
            context_ready.close(TT)
            close_stage()

            units = []
            for st in range(2):
                units += [(1, (h, h + 2), (st,)) for g in range(0, QH, 4) for h in (g, g + 1)]
                units += [(0, (h, h + 2, h + 4, h + 6), (st,)) for g in range(0, QH, 8) for h in (g, g + 1)]

            def bias(u, unit, sc, dst, L):
                t, heads, _ = unit
                n = len(heads)
                yield (sc.rearrange("p (h s) -> p h s", h=n), dst.rearrange("p (h s) -> p h s", h=n),
                       table[:, heads[0]:heads[-1] + 1:2, S - L:S])

            tmp = region(c0, 2, 4 * DH)

            def finish(dve, u, unit, res, rec):
                t, heads, sets = unit
                n = len(heads)
                g = gl[:, t, :].rearrange("p (h c) -> p h c", c=3)[:, heads[0]:heads[-1] + 1:2, 1 + sets[0]]
                v_link(dve.tensor_tensor(rec, rec, g, ALU.mult))
                tv = tmp[:, u % 2, 0:n * DH].rearrange("p (h d) -> p h d", h=n)
                v_link(dve.tensor_tensor(tv, res.rearrange("p (h d) -> p h d", h=n), spread(rec, 2, DH), ALU.mult))
                nc.vector.nop().then_inc(context_read.sem, 1)
                ov = o[:, t, :].rearrange("p (h d) -> p h d", h=QH)[:, heads[0]:heads[-1] + 1:2]
                v_link(dve.tensor_tensor(ov, ov, tv, ALU.add))

            attention(units,
                      lambda h, st, t: q2[DH * (h % 2):DH * (h % 2) + DH, h // 2, t * P:(t + 1) * P],
                      lambda h, st: kd[DH * (h % 2):DH * (h % 2) + DH, st, h // PER_GROUP, :],
                      lambda st, kt, h: vv[:, st, kt, (h // PER_GROUP) * DH:(h // PER_GROUP + 1) * DH],
                      bias, DH ** -0.5, DH, (sbuf_s, sbuf_p, sbuf_t), finish, 0)
            turn_rows(lambda t, j: o[:, t, j * P:(j + 1) * P], hT, KT)
            add_rows_product(a["a_w_out_2"][0], hT, KT)

        ND = len(DILATIONS)
        d_k = region(0, ND, GROUPS, S).rearrange("p a g s -> p a g s")
        d_v = region(3072, ND, TT, S).rearrange("p a g s -> p a g s")
        d_q = region(4608, ND * KT, S)
        d_table = region(10752, ND, QH, S).rearrange("p n h s -> p n h s")
        d_rest = 10752 + ND * QH * S

        def shared_keys_stage():
            w = a["kv_w_2"]
            pairs = region(d_rest, ND, 2, S)

            @block.tensor
            def _(pe):
                begin(pe)
                for n in range(ND):
                    wv = take_chunk(pe, KT, 512)
                    columns_product(pe, 3 * n, wv, hT, (0, P)).then_inc(bank_full.sem, 1)
                    for t in range(TT):
                        b = free_bank(pe, 3 * n + 1 + t)
                        for k in range(KT):
                            mm = nc.tensor.matmul(b[:, 0:S], hT[:, k, t * P:(t + 1) * P], wv[:, k, S:2 * S],
                                                  start=(k == 0), stop=(k == KT - 1))
                        mm.then_inc(bank_full.sem, 1)
                    release_chunk(bank_full, 3 * n + 3)
                two_halves(pe, 3 * ND, pairs, ND)
                end(pe)

            @block.sync
            def _(sp):
                for n in range(ND):
                    load_chunk(sp, (0, w[:, n * 512:(n + 1) * 512]))

            @block.scalar
            def _(act):
                begin(act)
                for n in range(3 * ND):
                    i, part = n // 3, n % 3
                    act.wait_ge(bank_full.sem, bank_full.at(n + 1))
                    if part == 0:
                        ins = act.activation(pairs[:, i].rearrange("p a s -> p (a s)"), bank(n % 4), ACT.Copy)
                    else:
                        ins = act.activation(d_v[:, i, part - 1, :], bank(n % 4)[:, 0:S], ACT.Copy)
                    ins.then_inc(bank_free.sem, 1)
                act.wait_ge(bank_free.sem, bank_free.at(3 * ND))
                nc.scalar.nop().then_inc(inner_ready.sem, 1)
                for m in range(2 * ND):
                    n = 3 * ND + m
                    i, gp = m // 2, m % 2
                    act.wait_ge(bank_full.sem, bank_full.at(n + 1))
                    act.activation(d_k[:, i, 2 * gp:2 * gp + 2, :], bank(n % 4).rearrange("p (j s) -> p j s", j=2),
                                   ACT.Copy).then_inc(bank_free.sem, 1)
                end(act)

            @block.vector
            def _(dve):
                begin(dve)
                end(dve)

            @block.gpsimd
            def _(pool):
                pool.wait_ge(stage_done.sem, COMPUTE * stage[0])
                for n in range(ND):
                    src = bass.AP(table_dram.tensor, (1 + n) * TABLE_SKEW + P - 1, [[SPAN, P], [HEAD_SKEW, QH], [1, S]])
                    pool.dma_start(d_table[:, n], src).then_inc(table_load.sem, 16)

            bank_full.close(5 * ND)
            bank_free.close(5 * ND)
            inner_ready.close(1)
            close_stage()

        def dilated_attention_layer():
            w_q = a["b_w_q_2"][0]

            @block.tensor
            def _(pe):
                begin(pe)
                for c in range(2 * ND):
                    w = take_chunk(pe, KT, 512)
                    for j in range(2):
                        columns_product(pe, 2 * c + j, w, hT, (2 * j * P, (2 * j + 1) * P)).then_inc(bank_full.sem, 1)
                    release_chunk(bank_full, 2 * c + 2)
                end(pe)

            @block.sync
            def _(sp):
                for c in range(2 * ND):
                    load_chunk(sp, (0, w_q[:, c * 512:(c + 1) * 512]))

            @block.scalar
            def _(act):
                begin(act)
                for n in range(4 * ND):
                    act.wait_ge(bank_full.sem, bank_full.at(n + 1))
                    act.activation(d_q[:, 2 * n:2 * n + 2, :].rearrange("p a s -> p (a s)"), bank(n % 4), ACT.Copy) \
                       .then_inc(bank_free.sem, 1)
                end(act)

            @block.vector
            def _(dve):
                begin(dve)
                dve.wait_ge(table_load.sem, table_load.at(16 * ND))
                end(dve)

            bank_full.close(4 * ND)
            bank_free.close(4 * ND)
            table_load.close(16 * ND)
            close_stage()

            sbuf_s = region(d_rest, 2, 768)
            sbuf_p = region(d_rest + 1536, 2, 768)
            sbuf_t = region(d_rest + 3072, 2, 512)
            o = region(d_rest + 4096, TT, D)
            sets = tuple(range(ND))
            units = [(t, (h,), sets) for h in range(QH) for t in (1, 0)]

            def bias(u, unit, sc, dst, L):
                t, heads, _ = unit
                yield (sc.rearrange("p (n s) -> p n s", n=ND), dst.rearrange("p (n s) -> p n s", n=ND),
                       d_table[:, :, heads[0], S - L:S])

            def finish(dve, u, unit, res, rec):
                t, heads, _ = unit
                h = heads[0]
                dve.tensor_scalar(o[:, t, h * DH:(h + 1) * DH], res, rec, None, ALU.mult).then_inc(context_read.sem, 1)

            attention(units,
                      lambda h, st, t: d_q[DH * (h % 2):DH * (h % 2) + DH, st * KT + h // 2, t * P:(t + 1) * P],
                      lambda h, st: d_k[DH * (h % 2):DH * (h % 2) + DH, st, h // PER_GROUP, :],
                      lambda st, kt, h: d_v[:, st, kt, (h // PER_GROUP) * DH:(h // PER_GROUP + 1) * DH],
                      bias, DH ** -0.5, DH, (sbuf_s, sbuf_p, sbuf_t), finish, 0)
            turn_rows(lambda t, j: o[:, t, j * P:(j + 1) * P], hT, KT)
            add_rows_product(a["b_w_out_2"][0], hT, KT)

        def output_stage():
            xn = region(0, TT, D)
            gain = region(2048, D)

            @block.scalar
            def _(act):
                begin(act)
                act.dma_start(gain, a["final_norm_2"].partition_broadcast(P)).then_inc(side_load.sem, 16)
                for t in range(TT):
                    act.activation(xn[:, t, :], x[:, t, :], ACT.Square, accum_out=stat[:, t:t + 1]) \
                       .then_inc(squares_ready.sem, 1)
                square_root(act, stat[:, 6:6 + TT], stat[:, 8:8 + TT], 1)

            @block.vector
            def _(dve):
                begin(dve)
                dve.wait_ge(squares_ready.sem, squares_ready.at(TT))
                inverse_root(dve, stat[:, 4:4 + TT], stat[:, 6:6 + TT], stat[:, 8:8 + TT], stat[:, 0:TT], 1.0 / D, 1)
                dve.wait_ge(side_load.sem, side_load.at(16))
                for t in range(TT):
                    dve.scalar_tensor_tensor(xn[:, t, :], x[:, t, :], stat[:, 4 + t:5 + t], gain, ALU.mult, ALU.mult) \
                       .then_inc(rows_scaled.sem, 1)

            @block.sync
            def _(sp):
                for t in range(TT):
                    sp.wait_ge(rows_scaled.sem, rows_scaled.at(t + 1))
                    sp.dma_start(out[0, t * P:(t + 1) * P, :], xn[:, t, :]).then_inc(stored, 16)
                sp.wait_ge(stored, 16 * TT)

        def col(base):
            return lambda k: par[:, base + k:base + k + 1]

        setup_stage()
        for l in range(DEPTH):
            norm_stage(col(R_MISC(l) + M_MIX))
            mixer_rows_stage(l)
            mixer_columns_stage(l)
            mixer_turn_stage(l)
            gates_stage(l)
            sparse_attention_stage(l)
            stick_breaking_stage()
            branch_output_stage(l)
            add_rows_product(a["w_merge"][l], hT, KT)
            norm_stage(col(R_MISC(l) + M_FFN))
            ffn_up_stage(a["w_ffn_gate"][l], a["w_ffn_up"][l], 0, 0, fT,
                         lambda k, j, l=l: par[:, R_FFC(l) + FT * k + j:R_FFC(l) + FT * k + j + 1])
            add_rows_product(a["w_ffn_down"][l], fT, FT)
        for l in range(2):
            if l == 0:
                norm_stage(col(R_PART2 + M2_MIX))
                compressed_attention_layer()
            else:
                norm_stage(col(R_PART2 + M2_KV))
                shared_keys_stage()
                norm_stage(col(R_PART2 + M2_MIX + KT), d_rest)
                dilated_attention_layer()
            norm_stage(col(R_PART2 + M2_FFN + KT * l))
            ffn_up_stage(a["ffn_w_up_2"][l], a["ffn_w_up_2"][l], 0, FF, fT, None)
            add_rows_product(a["ffn_w_down_2"][l], fT, FT)
        output_stage()


_INS = ["x", "positions", "g_mix", "w_in", "b_gate", "g_qa", "g_ka", "g_kidx", "w_oa", "cb_conv_w", "cb_conv_b",
        "cb_ln_g", "cb_ln_b", "w_ob", "cc_conv_w", "w_oc", "w_od", "w_merge", "g_ffn", "w_ffn_gate", "w_ffn_up",
        "ffn_conv_w", "w_ffn_down", "rel_bias_2", "norm_mix_2", "norm_ffn_2", "a_w_in_2", "a_b_gate_2", "a_pe_k_2",
        "a_w1_k_2", "a_w2_k_2", "a_pe_v_2", "a_w1_v_2", "a_w2_v_2", "a_w_out_2", "kv_norm_2", "kv_w_2", "b_w_q_2",
        "b_w_out_2", "ffn_w_up_2", "ffn_w_down_2", "final_norm_2"]


def kernel(**inputs):
    import numpy as _np
    import concourse.bacc as _bacc
    from concourse import mybir as _mybir
    from concourse.bass_utils import run_bass_kernel_spmd as _run

    nc = _bacc.Bacc("TRN2", target_bir_lowering=False, num_devices=1)
    arrays, aps = {}, {}
    for name in _INS:
        v = _np.ascontiguousarray(inputs[name])
        arrays[f"in_{name}"] = v
        aps[name] = nc.dram_tensor(f"in_{name}", v.shape, _mybir.dt.from_np(v.dtype), kind="ExternalInput").ap()
    extra = []
    for name, v in (("shape_constants", shape_constants()), ("distance_tables", distance_tables())):
        arrays[f"in_{name}"] = v
        extra.append(nc.dram_tensor(f"in_{name}", v.shape, F32, kind="ExternalInput").ap())
    out = nc.dram_tensor("out_dram", [1, S, D], F32, kind="ExternalOutput").ap()
    two_part_transformer(nc, aps, extra[0], extra[1], out)
    r = _run(nc, [arrays], core_ids=[0])
    return r.results[0]["out_dram"]
```

```python
import math
from contextlib import ExitStack

import numpy as np
import concourse.bass as bass
from concourse import mybir

F32 = mybir.dt.float32
F32R = mybir.dt.float32r
I32 = mybir.dt.int32
ALU = mybir.AluOpType
ACT = mybir.ActivationFunctionType
AX = mybir.AxisListType

P = 128
D = 1024
S = 256
TT = S // P
KT = D // P
DEPTH = 2
HEADS = 4
WIDTH = 512
IDX_DIM = 64
TOPK = S // 4
LONG = 31
SHORT = 3
FF = 2816
FT = FF // P
EPS = 1e-6
NEG = -1e30
TAKEN = -3e38
GROUPS = 4
PER_GROUP = 4
QH = 16
DH = 64
CMP_BLOCK = 32
CMP_STRIDE = 16
CMP_N = (S - CMP_BLOCK) // CMP_STRIDE + 1
CMP_PAD = 32
CMP_HIDDEN = 256
DILATIONS = (1, 4, 16)
BAND = 128
BUCKETS = 32
MAX_DISTANCE = 2048
SPAN = 384

W_Q, W_IDX, W_GLU, W_CC, W_SQ, W_SV, W_GATE = 0, 1536, 1860, 2884, 4420, 5444, 5956
IDX_COLS = 324
A_Q, A_KC, A_VC, A_KS, A_VS, A_KW, A_VW, A_GL = 0, 1024, 1280, 1536, 1792, 2048, 2304, 2560

UNIT = 2048
RAW_SLOTS, HIGH_SLOTS, LOW_SLOTS = 3, 3, 2

C_ID, C_MEAN, C_ONE, C_TRI, C_SNEG, C_SKEEP, C_CAUS, C_LOW, C_HIGH, C_FREQ, C_CMP = (
    0, 128, 256, 384, 512, 640, 768, 896, 1024, 1152, 1176)
C_COLS = C_CMP + TT * CMP_N
O_FULL, O_DIL, O_CMP = 0, SPAN, 4 * SPAN
O_COLS = O_CMP + 512

R_LONG = lambda l: 3 * l * P
R_MISC = lambda l: (3 * l + 1) * P
R_FFC = lambda l: (3 * l + 2) * P
R_PART2 = 3 * DEPTH * P
M_GATE, M_MIX, M_FFN, M_CB, M_LNG, M_LNB, M_CC = 0, 32, 40, 48, 52, 56, 60
M2_MIX, M2_FFN, M2_KV, M2_PEK, M2_PEV = 0, 16, 32, 40, 56
PARAM_TILES = 3 * DEPTH + 1


def t5_bucket(dist):
    d = np.maximum(dist, 0)
    half = BUCKETS // 2
    ratio = (np.log(np.maximum(d, half).astype(np.float32) / np.float32(half)).astype(np.float32)
             / np.float32(math.log(MAX_DISTANCE / half)))
    large = half + (ratio * np.float32(BUCKETS - half)).astype(np.int32)
    return np.where(d < half, d, np.minimum(large, BUCKETS - 1))


def shape_constants():
    c = np.zeros((P, C_COLS), np.float32)
    p = np.arange(P)[:, None]
    f = np.arange(P)[None, :]
    c[:, C_ID:C_ID + P] = p == f
    c[:, C_MEAN:C_MEAN + P] = 1.0 / WIDTH
    c[:, C_ONE:C_ONE + P] = 1.0
    c[:, C_TRI:C_TRI + P] = p >= f
    c[:, C_SNEG:C_SNEG + P] = np.where(p < f, 0.0, NEG)
    c[:, C_SKEEP:C_SKEEP + P] = p < f
    c[:, C_CAUS:C_CAUS + P] = np.where(f <= p, 0.0, NEG)
    c[:, C_LOW:C_LOW + P] = p == f % DH
    c[:, C_HIGH:C_HIGH + P] = p == f % DH + DH
    for at, half in ((0, 16), (16, 8)):
        rot = 2 * half
        c[:, C_FREQ + at:C_FREQ + at + half] = (
            np.float32(500000.0) ** (-(np.arange(half, dtype=np.float32) * np.float32(2.0)) / np.float32(rot)))
    for t in range(TT):
        dist = P * t + p - (CMP_STRIDE * np.arange(CMP_N)[None, :] + CMP_BLOCK - 1)
        c[:, C_CMP + t * CMP_N:C_CMP + (t + 1) * CMP_N] = dist >= 0
    return c


def distance_tables():
    o = np.zeros((BUCKETS + 1, O_COLS), np.float32)

    def put(col, dist, keep):
        cols = np.arange(len(dist)) + col
        o[t5_bucket(dist)[keep], cols[keep]] = 1.0
        o[BUCKETS, cols[~keep]] = 1.0

    back = (S - 1) - np.arange(SPAN)
    put(O_FULL, back, back >= 0)
    for n, dil in enumerate(DILATIONS):
        put(O_DIL + n * SPAN, back, (back >= 0) & (back % dil == 0) & (back <= BAND * dil))
    ahead = np.arange(512) - (S - 1)
    put(O_CMP, ahead, ahead >= 0)
    return o


def spread(ap, dim, n):
    dims = [list(x) for x in ap.ap]
    return bass.AP(ap.tensor, ap.offset, dims[:dim] + [[0, n]] + dims[dim:])


class Signal:

    def __init__(self, sem):
        self.sem, self.base = sem, 0

    def at(self, k):
        assert self.base + k > 0
        return self.base + k

    def close(self, n):
        self.base += n


class Stream:

    def __init__(self):
        self.units = []
        self.low = []
        self.freed = []
        self.high = 0
        self.made = {"P": 0, "V": 0}


def column_units(w, first, last, engines):
    n = -(-(last - first) // S)
    return [(w[:, first + i * S:min(first + (i + 1) * S, last)], engines[i % len(engines)]) for i in range(n)]


def row_units(w, tiles, engines):
    return [(w[2 * i * P:2 * (i + 1) * P, :], engines[i % len(engines)]) for i in range(tiles // 2)]


def weight_units(a):
    u = []
    for l in range(DEPTH):
        w = a["w_in"][l]
        u += column_units(w, W_Q, W_IDX, "PPVVVV")
        u += column_units(w, W_IDX, W_GLU, "VV")
        u += column_units(w, W_GLU, W_GATE, "P")
        u += column_units(w, W_GATE, W_GATE + 4 * D, "P")
        for name in ("w_oa", "w_ob", "w_oc", "w_od"):
            u += [(a[name][l][:, h * 512:(h + 1) * 512], "P") for h in range(2)]
        u += row_units(a["w_merge"][l], KT, "PPVV")
        for c in range(FT // 2):
            u += [(a["w_ffn_gate"][l][:, c * S:(c + 1) * S], "P"), (a["w_ffn_up"][l][:, c * S:(c + 1) * S], "PV"[c > 0])]
        u += row_units(a["w_ffn_down"][l], FT, "PV")
    for l in range(2):
        if l == 0:
            w = a["a_w_in_2"][0]
            u += column_units(w, A_KC, A_KS, "P") + column_units(w, 0, A_KC, "PVPP")
            u += column_units(w, A_KS, A_GL + 3 * QH, "PVPPP")
            for name in ("a_w1_k_2", "a_w1_v_2"):
                u += [(a[name][0][i * 1024:(i + 1) * 1024, :], "P") for i in range(2)]
            u += row_units(a["a_w_out_2"][0], KT, "PPVV")
        else:
            u += column_units(a["kv_w_2"], 0, 2 * S * len(DILATIONS), "PPVVVV")
            u += column_units(a["b_w_q_2"][0], 0, D * len(DILATIONS), "PPPV")
            u += row_units(a["b_w_out_2"][0], KT, "PPVV")
        w = a["ffn_w_up_2"][l]
        for c in range(FT // 2):
            u += [(w[:, c * S:(c + 1) * S], "P"), (w[:, FF + c * S:FF + (c + 1) * S], "PV"[c > 0])]
        u += row_units(a["ffn_w_down_2"][l], FT, "PV")
    return u


def two_part_transformer(nc, a, consts, onehots, out):
    ctx = ExitStack()
    with ctx:
        place = {}

        def sb(name, shape, dt=F32):
            place[name] = -(-nc.sbuf_base // 32) * 32
            return ctx.enter_context(nc.sbuf_tensor(name, shape, dt))

        def signal(name):
            return Signal(ctx.enter_context(nc.semaphore(name)))

        x = sb("x", [P, TT, D])
        h_place = sb("h_place", [P, 2 * KT * S])
        raw = sb("raw", [P, RAW_SLOTS, UNIT])
        whi = sb("whi", [P, HIGH_SLOTS, UNIT], F32R)
        wlo = sb("wlo", [P, LOW_SLOTS, UNIT], F32R)
        cst = sb("cst", [P, C_COLS])
        par = sb("par", [P, PARAM_TILES * P])
        g_head = sb("g_head", [P, DEPTH, 2, P])
        g_kidx = sb("g_kidx", [P, DEPTH, IDX_DIM])
        b_gl = sb("b_gl", [P, 3 * QH])
        rot = sb("rot", [P, 2, TT, 24])
        stat = sb("stat", [P, 160])
        WORK = 27160
        work = sb("work", [P, WORK])
        posi = sb("posi", [P, TT], I32)
        psum = ctx.enter_context(nc.psum_tensor("psum", [P, 8, 512], F32))
        at_h, at_work = place["h_place"], place["work"]

        def over(name, base, start, shape, dt=F32R):
            return nc.alloc_sbuf_tensor_at(name, [P] + shape, dt, offset=base + 4 * start)

        hT = [over(f"hT{i}", at_h, i * KT * S, [KT, S]) for i in range(2)]
        table_dram = nc.dram_tensor("table_dram", [4, QH, P, SPAN + 1], F32, kind="Internal").ap()
        HEAD_SKEW = P * (SPAN + 1)
        TABLE_SKEW = QH * HEAD_SKEW

        ident = cst[:, C_ID:C_ID + P]

        def region(start, *shape):
            n = int(np.prod(shape))
            assert start + n <= WORK, (start, shape)
            v = work[:, start:start + n]
            if len(shape) == 2:
                return v.rearrange("p (a b) -> p a b", a=shape[0])
            if len(shape) == 3:
                return v.rearrange("p (a b c) -> p a b c", a=shape[0], b=shape[1])
            return v

        def bank(b, n=1):
            return psum[:, b:b + n, :].rearrange("p a b -> p (a b)")

        stage_done = signal("stage_done")
        raw_landed = [ctx.enter_context(nc.semaphore(f"raw_landed{i}")) for i in range(RAW_SLOTS)]
        high_made = ctx.enter_context(nc.semaphore("high_made"))
        low_made = {"P": ctx.enter_context(nc.semaphore("low_made_pool")),
                    "V": ctx.enter_context(nc.semaphore("low_made_vector"))}
        unit_used = signal("unit_used")
        bank_full = signal("bank_full")
        bank_free = signal("bank_free")
        vector_step = signal("vector_step")
        scalar_step = signal("scalar_step")
        variance_ready = signal("variance_ready")
        root_ready = signal("root_ready")
        parts_ready = signal("parts_ready")
        rows_added = signal("rows_added")
        rows_scaled = signal("rows_scaled")
        rows_turned = signal("rows_turned")
        side_full = signal("side_full")
        side_free = signal("side_free")
        scores_ready = signal("scores_ready")
        scores_read = signal("scores_read")
        maxima_ready = signal("maxima_ready")
        probs_ready = signal("probs_ready")
        probs_turned = signal("probs_turned")
        turned_copied = signal("turned_copied")
        context_ready = signal("context_ready")
        context_read = signal("context_read")
        operand_ready = signal("operand_ready")
        inner_ready = signal("inner_ready")
        inner_taken = signal("inner_taken")
        side_load = signal("side_load")
        table_load = signal("table_load")
        side_store = signal("side_store")
        stored = ctx.enter_context(nc.semaphore("stored"))

        block = ctx.enter_context(nc.Block())
        stream = Stream()
        stream.units = [(src, src.shape[0] // P, src.shape[1], e) for src, e in weight_units(a)]
        for _, _, _, e in stream.units:
            stream.made[e] += 1
            stream.low.append((low_made[e], stream.made[e]))

        COMPUTE = 3
        stage = [0]

        def begin(eng):
            if stage[0]:
                eng.wait_ge(stage_done.sem, COMPUTE * stage[0])

        def end(eng):
            eng.drain().then_inc(stage_done.sem, 1)

        def close_stage(**signals):
            stage[0] += 1

        def v_done(ins):
            ins.then_inc(vector_step.sem, 1)
            vector_step.base += 1
            return vector_step.base

        def v_wait(n):
            nc.vector.wait_ge(vector_step.sem, n)

        def v_link(ins):
            v_wait(v_done(ins))

        def s_done(ins):
            ins.then_inc(scalar_step.sem, 1)
            scalar_step.base += 1
            return scalar_step.base

        def s_wait(n):
            nc.scalar.wait_ge(scalar_step.sem, n)

        def part(buf, n, slots):
            _, kt, cols, _ = stream.units[n]
            return buf[:, n % slots, 0:kt * cols]

        def make_high(act, upto):
            while stream.high < min(upto, len(stream.units)):
                n = stream.high
                act.wait_ge(raw_landed[n % RAW_SLOTS], 16 * (n // RAW_SLOTS + 1))
                if n >= HIGH_SLOTS:
                    act.wait_ge(*stream.freed[n - HIGH_SLOTS])
                act.activation(part(whi, n, HIGH_SLOTS), part(raw, n, RAW_SLOTS), ACT.Copy).then_inc(high_made, 1)
                stream.high += 1

        def make_low(eng, n):
            eng.wait_ge(high_made, n + 1)
            if n >= LOW_SLOTS:
                eng.wait_ge(*stream.freed[n - LOW_SLOTS])
            eng.tensor_tensor(part(wlo, n, LOW_SLOTS), part(raw, n, RAW_SLOTS),
                              part(whi, n, HIGH_SLOTS).bitcast(F32), ALU.subtract).then_inc(stream.low[n][0], 1)

        vector_next = [0]

        def make_lows(dve, upto):
            for n in range(vector_next[0], upto):
                if stream.units[n][3] == "V":
                    make_low(dve, n)
            vector_next[0] = max(vector_next[0], upto)

        def take_unit(pe, n):
            pe.wait_ge(*stream.low[n])
            _, kt, _, _ = stream.units[n]
            return [part(b, n, k).rearrange("p (k c) -> p k c", k=kt) for b, k in ((whi, HIGH_SLOTS), (wlo, LOW_SLOTS))]

        def release_unit(event, k):
            stream.freed.append((event.sem, event.at(k)))

        def three_passes(dst, left, right, first, last):
            nc.tensor.matmul(dst, left[0], right[0], start=first, stop=False)
            nc.tensor.matmul(dst, left[0], right[1], start=False, stop=False)
            return nc.tensor.matmul(dst, left[1], right[0], start=False, stop=last)

        handed_over = []

        def hand_over(pairs):
            handed_over[:] = [(parts_ready.sem, parts_ready.at(i + 1)) for i in range(pairs)]
            parts_ready.close(pairs)

        def await_pair(pe):
            if handed_over:
                pe.wait_ge(*handed_over.pop(0))

        def free_bank(pe, n):
            if n >= 4:
                pe.wait_ge(bank_free.sem, bank_free.at(n - 3))
            return bank(n % 4)

        def columns_product(pe, n, w, src, cols):
            b = free_bank(pe, n)
            kt = w[0].shape[1]
            for j, c in enumerate(cols):
                for k in range(kt):
                    if k % 2 == 0:
                        await_pair(pe)
                    mm = three_passes(b[:, j * S:(j + 1) * S], [v[:, k, c:c + P] for v in w], [v[:, k, :] for v in src],
                                      k == 0, k == kt - 1)
            return mm

        def rows_product(pe, n, w, src, width):
            b = free_bank(pe, n)
            for t in range(TT):
                for k in range(KT):
                    if k % 2 == 0:
                        await_pair(pe)
                    mm = three_passes(b[:, t * S:t * S + width], [v[:, k, t * P:(t + 1) * P] for v in src],
                                      [v[:, k, 0:width] for v in w], k == 0, k == KT - 1)
            return mm

        def two_halves(pe, n, pairs, sets, ready=1):
            pe.wait_ge(inner_ready.sem, inner_ready.at(ready))
            for i in sets:
                for gp in range(2):
                    b = free_bank(pe, n)
                    for j, pick in enumerate((C_LOW, C_HIGH)):
                        mm = nc.tensor.matmul(b[:, j * S:(j + 1) * S], cst[:, pick:pick + P], pairs[:, i, gp, :],
                                              start=True, stop=True)
                    mm.then_inc(bank_full.sem, 1)
                    n += 1

        def setup_stage():
            praw = region(0, PARAM_TILES, P)
            onehot = region(4000, O_COLS)
            relb = region(7000, QH)
            squared = region(12000, TT, D)
            loads = []

            @block.gpsimd
            def _(pool):
                pool.memset(praw, 0.0).then_inc(operand_ready.sem, 1)
                pool.memset(work[0:BUCKETS + 1, 7000:7000 + QH], NEG).then_inc(operand_ready.sem, 1)

            @block.scalar
            def _(act):
                def load(dst, src):
                    act.dma_start(dst, src).then_inc(side_load.sem, 16)
                    loads.append(1)

                load(cst[:, :], consts)
                load(x[:, :, :], a["x"][0].rearrange("(t p) d -> p t d", p=P))
                load(onehot[0:BUCKETS + 1, :], onehots)
                for n, g in enumerate(("g_qa", "g_ka")):
                    load(g_head[:, :, n, :], a[g].partition_broadcast(P))
                load(g_kidx[:, :, :], a["g_kidx"].partition_broadcast(P))
                load(b_gl[:, :], a["a_b_gate_2"][0:1, :].rearrange("a d -> (a d)").partition_broadcast(P))
                for t in range(TT):
                    load(posi[:, t:t + 1], a["positions"][0:1, t * P:(t + 1) * P].rearrange("a p -> p a"))
                act.wait_ge(operand_ready.sem, operand_ready.at(2))

                def rows(tile, row, src):
                    n = src.shape[0]
                    load(praw[row:row + n, tile, :], src)

                load(work[0:BUCKETS, 7000:7000 + QH], a["rel_bias_2"])

                def layer_rows(tile, row, src):
                    n = src.shape[0]
                    load(praw[row:row + n, tile:3 * DEPTH:3, :], src)

                layer_rows(0, 0, a["cb_conv_w"].rearrange("l k (t p) -> (k t) l p", p=P))
                for at, name in ((M_GATE, "b_gate"), (M_MIX, "g_mix"), (M_FFN, "g_ffn"), (M_CB, "cb_conv_b"),
                                 (M_LNG, "cb_ln_g"), (M_LNB, "cb_ln_b")):
                    layer_rows(1, at, a[name].rearrange("l (t p) -> t l p", p=P))
                layer_rows(1, M_CC, a["cc_conv_w"].rearrange("l k (t p) -> (k t) l p", p=P))
                layer_rows(2, 0, a["ffn_conv_w"].rearrange("l k (t p) -> (k t) l p", p=P))
                last = 3 * DEPTH
                for at, name in ((M2_MIX, "norm_mix_2"), (M2_FFN, "norm_ffn_2")):
                    rows(last, at, a[name].rearrange("l (t p) -> (l t) p", p=P))
                rows(last, M2_KV, a["kv_norm_2"].rearrange("(t p) -> t p", p=P))
                for at, name in ((M2_PEK, "a_pe_k_2"), (M2_PEV, "a_pe_v_2")):
                    rows(last, at, a[name][0].rearrange("(m j) d -> m (j d)", j=2))
                act.wait_ge(side_load.sem, side_load.at(16 * len(loads)))
                for t in range(TT):
                    act.activation(squared[:, t, :], x[:, t, :], ACT.Square, accum_out=stat[:, t:t + 1])
                end(act)

            @block.tensor
            def _(pe):
                pe.wait_ge(side_load.sem, side_load.at(16 * len(loads)))
                for n in range(PARAM_TILES):
                    mm = nc.tensor.transpose(bank(n // 4)[:, (n % 4) * P:(n % 4 + 1) * P], praw[:, n, :], ident)
                mm.then_inc(side_full.sem, 1)
                for n in range(4):
                    mm = nc.tensor.matmul(bank(2 + n)[0:QH, 0:SPAN], work[0:BUCKETS + 1, 7000:7000 + QH],
                                          onehot[0:BUCKETS + 1, n * SPAN:(n + 1) * SPAN], start=True, stop=True)
                mm.then_inc(side_full.sem, 1)
                end(pe)

            @block.vector
            def _(dve):
                dve.wait_ge(side_full.sem, side_full.at(1))
                dve.tensor_copy(par[:, 0:4 * P], bank(0))
                dve.tensor_copy(par[:, 4 * P:PARAM_TILES * P], bank(1)[:, 0:(PARAM_TILES - 4) * P])
                dve.wait_ge(side_full.sem, side_full.at(2))
                for n in range(4):
                    dve.tensor_copy(tab[0:QH, n, :], bank(2 + n)[0:QH, 0:SPAN]).then_inc(side_free.sem, 1)
                end(dve)

            operand_ready.close(2)
            side_load.close(16 * len(loads))
            side_full.close(2)
            side_free.close(4)
            close_stage()

        tab = region(2100, 4, SPAN)
        ang = region(10000, 2 * TT, 24)

        def rotary_angles(dve):
            tmp = region(10200, 2 * TT, 24)
            pos = stat[:, 140:140 + TT]
            v_link(dve.tensor_copy(pos, posi[:, :]))
            for t in range(TT):
                n = v_done(dve.tensor_scalar(ang[:, TT + t, :], cst[:, C_FREQ:C_FREQ + 24], pos[:, t:t + 1],
                                             None, ALU.mult))
            v_wait(n)
            s_ = ang[:, TT:2 * TT, :]
            c_ = ang[:, 0:TT, :]
            turns = tmp[:, 0:TT, :]
            magic = 1.5 * 2.0 ** 23
            v_link(dve.tensor_scalar(turns, s_, 1.0 / (2 * math.pi), magic, ALU.mult, ALU.add))
            v_link(dve.tensor_scalar(turns, turns, -magic, None, ALU.add))
            two_pi = 2 * math.pi
            c1 = 6.28125
            c2 = float(np.float32(int((two_pi - c1) * 2 ** 21) / 2 ** 21))
            c3 = two_pi - c1 - c2
            for c in (c1, c2, c3):
                v_link(dve.scalar_tensor_tensor(s_, turns, -c, s_, ALU.mult, ALU.add))
            v_link(dve.tensor_scalar(c_, s_, math.pi / 2, None, ALU.add))
            v_link(dve.tensor_scalar(turns, c_, math.pi, -two_pi, ALU.is_gt, ALU.mult))
            v_link(dve.tensor_tensor(c_, c_, turns, ALU.add))
            edge = 3.1415925
            dve.tensor_scalar(ang, ang, edge, -edge, ALU.min, ALU.max).then_inc(rows_scaled.sem, 1)


        def inverse_root(dve, y, v, t, src, n_over, k):
            dve.tensor_scalar(v, src, n_over, EPS, ALU.mult, ALU.add).then_inc(variance_ready.sem, 1)
            dve.wait_ge(root_ready.sem, root_ready.at(k))
            v_link(dve.reciprocal(y, t))
            v_link(dve.tensor_tensor(t, v, y, ALU.mult))
            v_link(dve.tensor_tensor(t, t, y, ALU.mult))
            v_link(dve.tensor_scalar(t, t, -0.5, 1.5, ALU.mult, ALU.add))
            v_link(dve.tensor_tensor(y, y, t, ALU.mult))

        def square_root(act, v, t, k):
            act.wait_ge(variance_ready.sem, variance_ready.at(k))
            act.activation(t, v, ACT.Sqrt).then_inc(root_ready.sem, 1)

        def close_roots(n):
            variance_ready.close(n)
            root_ready.close(n)

        def norm_stage(gain, scratch=0):
            dst = hT
            xn = region(scratch, TT, D)

            @block.scalar
            def _(act):
                begin(act)
                square_root(act, stat[:, 6:6 + TT], stat[:, 8:8 + TT], 1)
                act.wait_ge(operand_ready.sem, operand_ready.at(1))
                act.activation(xn[:, 1, :], x[:, 1, :], ACT.Copy, scale=stat[:, 5:6]).then_inc(scores_ready.sem, 1)
                for b in range(4):
                    act.wait_ge(rows_turned.sem, rows_turned.at(b + 1))
                    for j in range(2):
                        ins = act.activation(dst[0][:, 2 * b + j, :], bank(b)[:, j * S:(j + 1) * S], ACT.Copy,
                                             scale=gain(2 * b + j))
                    ins.then_inc(inner_ready.sem, 1)
                end(act)

            @block.vector
            def _(dve):
                begin(dve)
                inverse_root(dve, stat[:, 4:4 + TT], stat[:, 6:6 + TT], stat[:, 8:8 + TT], stat[:, 0:TT], 1.0 / D, 1)
                nc.vector.nop().then_inc(operand_ready.sem, 1)
                dve.tensor_scalar(xn[:, 0, :], x[:, 0, :], stat[:, 4:5], None, ALU.mult).then_inc(rows_scaled.sem, 1)
                for b in range(4):
                    dve.wait_ge(inner_ready.sem, inner_ready.at(b + 1))
                    for j in range(2):
                        ins = dve.scalar_tensor_tensor(dst[1][:, 2 * b + j, :], bank(b)[:, j * S:(j + 1) * S],
                                                       gain(2 * b + j), dst[0][:, 2 * b + j, :].bitcast(F32),
                                                       ALU.mult, ALU.subtract)
                    ins.then_inc(parts_ready.sem, 1)
                end(dve)

            @block.tensor
            def _(pe):
                begin(pe)
                pe.wait_ge(rows_scaled.sem, rows_scaled.at(1))
                pe.wait_ge(scores_ready.sem, scores_ready.at(1))
                for b in range(4):
                    for j in range(4):
                        k, t = 2 * b + j // 2, j % 2
                        mm = nc.tensor.transpose(bank(b)[:, j * P:(j + 1) * P], xn[:, t, k * P:(k + 1) * P], ident)
                    mm.then_inc(rows_turned.sem, 1)
                end(pe)

            close_roots(1)
            operand_ready.close(1)
            scores_ready.close(1)
            rows_scaled.close(1)
            rows_turned.close(4)
            inner_ready.close(4)
            hand_over(4)
            close_stage()

        def add_rows_product(lhsT, nk):
            squared = region(0, TT, D)
            n0, count = len(stream.freed), nk // 2

            @block.tensor
            def _(pe):
                for c in range(count):
                    w = take_unit(pe, n0 + c)
                    await_pair(pe)
                    for t in range(TT):
                        for k in range(2):
                            for h in range(2):
                                mm = three_passes(bank(4 + 2 * t + h),
                                                  [v[:, 2 * c + k, t * P:(t + 1) * P] for v in lhsT],
                                                  [v[:, k, h * 512:(h + 1) * 512] for v in w],
                                                      c + k == 0, 2 * c + k == nk - 1)
                        if t == 0 and c == count - 1:
                            mm.then_inc(unit_used.sem, 1)
                    mm.then_inc(unit_used.sem, 1)
                    release_unit(unit_used, c + 1 + (c == count - 1))
                end(pe)

            @block.scalar
            def _(act):
                begin(act)
                make_high(act, n0 + count + 2)
                act.activation(stat[:, 150:151], cst[:, C_ONE:C_ONE + 1], ACT.Sqrt)
                for t in range(TT):
                    act.wait_ge(rows_added.sem, rows_added.at(t + 1))
                    act.activation(squared[:, t, :], x[:, t, :], ACT.Square, accum_out=stat[:, t:t + 1])
                make_high(act, n0 + count + HIGH_SLOTS)
                end(act)

            @block.vector
            def _(dve):
                begin(dve)
                make_lows(dve, n0 + count)
                for t in range(TT):
                    dve.wait_ge(unit_used.sem, unit_used.at(count + t))
                    dve.tensor_tensor(x[:, t, :], x[:, t, :], bank(4 + 2 * t, 2), ALU.add).then_inc(rows_added.sem, 1)
                end(dve)

            unit_used.close(count + 1)
            rows_added.close(TT)
            close_stage()

        def ffn_up_stage(conv):
            pairs = FT // 2
            pad = SHORT - 1
            gpad = region(2 * FT * S, 4, S + pad).rearrange("p (b j) s -> p b j s", b=2)
            cacc = region(2 * FT * S + 4 * (S + pad), 4, S).rearrange("p (b j) s -> p b j s", b=2)
            prod = region(2 * FT * S + 4 * (S + pad) + 4 * S, 4, S).rearrange("p (b j) s -> p b j s", b=2)
            n0 = len(stream.freed)

            @block.tensor
            def _(pe):
                for n in range(2 * pairs):
                    columns_product(pe, n, take_unit(pe, n0 + n), hT, (0, P)).then_inc(bank_full.sem, 1)
                    release_unit(bank_full, n + 1)
                end(pe)

            @block.scalar
            def _(act):
                begin(act)

                def silu(c):
                    if conv is None:
                        ins = act.activation(cacc[:, c % 2], bank(2 * c % 4).rearrange("p (j s) -> p j s", j=2), ACT.Silu)
                    else:
                        act.wait_ge(operand_ready.sem, operand_ready.at(c + 1))
                        ins = act.activation(cacc[:, c % 2], cacc[:, c % 2], ACT.Silu)
                    ins.then_inc(inner_ready.sem, 1)

                def high(c):
                    act.wait_ge(context_ready.sem, context_ready.at(c + 1))
                    act.activation(fT[0][:, 2 * c:2 * c + 2, :], prod[:, c % 2], ACT.Copy).then_inc(context_read.sem, 1)

                if conv is not None:
                    act.wait_ge(side_free.sem, side_free.at(1))
                for c in range(pairs):
                    make_high(act, n0 + 2 * c + 3)
                    act.wait_ge(bank_full.sem, bank_full.at(2 * c + 1))
                    if conv is None:
                        if c >= 2:
                            act.wait_ge(bank_free.sem, bank_free.at(2 * c - 2))
                        silu(c)
                        make_high(act, n0 + 2 * c + 4)
                        if c:
                            high(c - 1)
                        continue
                    if c >= 2:
                        act.wait_ge(operand_ready.sem, operand_ready.at(c - 1))
                    act.activation(gpad[:, c % 2, :, pad:], bank(2 * c % 4).rearrange("p (j s) -> p j s", j=2),
                                   ACT.Copy).then_inc(scores_ready.sem, 1)
                    make_high(act, n0 + 2 * c + 4)
                    silu(c)
                    if c:
                        high(c - 1)
                high(pairs - 1)
                make_high(act, n0 + 2 * pairs + HIGH_SLOTS)
                end(act)

            @block.vector
            def _(dve):
                begin(dve)

                def product(c):
                    dve.wait_ge(bank_full.sem, bank_full.at(2 * c + 2))
                    dve.wait_ge(inner_ready.sem, inner_ready.at(c + 1))
                    if c >= 2:
                        dve.wait_ge(context_read.sem, context_read.at(c - 1))
                    v_link(dve.tensor_tensor(prod[:, c % 2], cacc[:, c % 2],
                                             bank((2 * c + 1) % 4).rearrange("p (j s) -> p j s", j=2), ALU.mult))
                    nc.vector.nop().then_inc(context_ready.sem, 1)
                    nc.vector.nop().then_inc(bank_free.sem, 2)

                def low(c):
                    dve.wait_ge(context_read.sem, context_read.at(c + 1))
                    dve.tensor_tensor(fT[1][:, 2 * c:2 * c + 2, :], prod[:, c % 2],
                                      fT[0][:, 2 * c:2 * c + 2, :].bitcast(F32), ALU.subtract) \
                       .then_inc(parts_ready.sem, 1)

                if conv is not None:
                    dve.memset(gpad.rearrange("p b j s -> p (b j) s")[:, :, 0:pad], 0.0).then_inc(side_free.sem, 1)
                for c in range(pairs):
                    b = c % 2
                    make_lows(dve, n0 + 2 * c + 2)
                    if conv is not None:
                        dve.wait_ge(scores_ready.sem, scores_ready.at(c + 1))
                        n = [0, 0]
                        for k in range(SHORT):
                            for j in range(2):
                                src = gpad[:, b, j, k:k + S]
                                if k == 0:
                                    ins = dve.tensor_scalar(cacc[:, b, j, :], src, conv(k, 2 * c + j), None, ALU.mult)
                                else:
                                    v_wait(n[j])
                                    ins = dve.scalar_tensor_tensor(cacc[:, b, j, :], src, conv(k, 2 * c + j),
                                                                   cacc[:, b, j, :], ALU.mult, ALU.add)
                                n[j] = v_done(ins)
                        v_wait(n[1])
                        nc.vector.nop().then_inc(operand_ready.sem, 1)
                    if c:
                        low(c - 1)
                    make_lows(dve, n0 + 2 * c + 3)
                    product(c)
                make_lows(dve, n0 + 2 * pairs + 2)
                low(pairs - 1)
                end(dve)

            bank_full.close(2 * pairs)
            bank_free.close(2 * pairs)
            inner_ready.close(pairs)
            context_ready.close(pairs)
            context_read.close(pairs)
            hand_over(pairs)
            if conv is not None:
                scores_ready.close(pairs)
                operand_ready.close(pairs)
                side_free.close(1)
            close_stage()

        def attention(units, q, k, v, bias, scale, dh, bufs, finish):
            sbuf_s, sbuf_p, sbuf_t = bufs
            U = len(units)
            width = [len(h) * len(st) * P * (t + 1) for t, h, st in units]
            keys = [P * (t + 1) for t, _, _ in units]
            rounds = []
            for u, (t, heads, sets) in enumerate(units):
                blocks = [(hi, si, kt) for hi in range(len(heads)) for si in range(len(sets)) for kt in range(t + 1)]
                for i in range(0, len(blocks), 4):
                    rounds.append((u, blocks[i:i + 4], i == 0, i + 4 >= len(blocks)))
            wide = max(width) > 512

            slots, ahead = (2, 1) if wide else (4, 2)

            def score_bank(u):
                return bank(2 * (u % 2), 2) if wide else bank(u % 4)

            @block.tensor
            def _(pe):
                begin(pe)

                def scores(u):
                    t, heads, sets = units[u]
                    if u >= slots:
                        pe.wait_ge(scores_read.sem, scores_read.at(u - slots + 1))
                    b = score_bank(u)
                    o = 0
                    for h in heads:
                        for st in sets:
                            mm = nc.tensor.matmul(b[:, o:o + keys[u]], q(h, st, t), k(h, st)[:, 0:keys[u]],
                                                  start=True, stop=True)
                            o += keys[u]
                    mm.then_inc(scores_ready.sem, 1)

                def context(r):
                    u, blocks, first, last = rounds[r]
                    t, heads, sets = units[u]
                    if first and u >= 2:
                        pe.wait_ge(context_read.sem, context_read.at(u - 1))
                    pe.wait_ge(turned_copied.sem, turned_copied.at(r + 1))
                    for n, (hi, si, kt) in enumerate(blocks):
                        mm = nc.tensor.matmul(bank(6 + u % 2)[:, hi * dh:(hi + 1) * dh],
                                              sbuf_t[:, r % 2, n * P:(n + 1) * P], v(sets[si], kt, heads[hi]),
                                              start=(si == 0 and kt == 0), stop=(si == len(sets) - 1 and kt == t))
                    if last:
                        mm.then_inc(context_ready.sem, 1)

                for u in range(ahead):
                    scores(u)
                for r, (u, blocks, first, last) in enumerate(rounds):
                    if first:
                        if u + ahead < U:
                            scores(u + ahead)
                        pe.wait_ge(probs_ready.sem, probs_ready.at(u + 1))
                    if r >= 2:
                        pe.wait_ge(turned_copied.sem, turned_copied.at(r - 1))
                    for n, (hi, si, kt) in enumerate(blocks):
                        t, heads, sets = units[u]
                        o = (hi * len(sets) + si) * keys[u] + kt * P
                        mm = nc.tensor.transpose(bank(4 + r % 2)[:, n * P:(n + 1) * P],
                                                 sbuf_p[:, u % 2, o:o + P], ident)
                    mm.then_inc(probs_turned.sem, 1)
                    if r:
                        context(r - 1)
                context(len(rounds) - 1)
                end(pe)

            @block.vector
            def _(dve):
                begin(dve)
                mx = stat[:, 0:16]

                def use(u):
                    t, heads, sets = units[u]
                    dve.wait_ge(context_ready.sem, context_ready.at(u + 1))
                    dve.wait_ge(probs_ready.sem, probs_ready.at(u + 1))
                    den = stat[:, 16 + 8 * (u % 4):16 + 8 * (u % 4) + len(heads)]
                    rec = stat[:, 48 + 8 * (u % 4):48 + 8 * (u % 4) + len(heads)]
                    v_link(dve.reciprocal(rec, den))
                    finish(dve, u, units[u], bank(6 + u % 2)[:, 0:len(heads) * dh], rec)

                for u, (t, heads, sets) in enumerate(units):
                    nh = len(heads)
                    dve.wait_ge(scores_ready.sem, scores_ready.at(u + 1))
                    if u >= 2:
                        dve.wait_ge(probs_ready.sem, probs_ready.at(u - 1))
                    sc = score_bank(u)[:, 0:width[u]]
                    s_ = sbuf_s[:, u % 2, 0:width[u]]
                    for psrc, sdst, bsrc in bias(u, units[u], sc, s_, keys[u]):
                        ins = dve.scalar_tensor_tensor(sdst, psrc, scale, bsrc, ALU.mult, ALU.add)
                        n = v_done(ins)
                    v_wait(n)
                    nc.vector.nop().then_inc(scores_read.sem, 1)
                    dve.tensor_reduce(mx[:, 8 * (u % 2):8 * (u % 2) + nh], s_.rearrange("p (h s) -> p h s", h=nh),
                                      AX.X, ALU.max, negate=True).then_inc(maxima_ready.sem, 1)
                    if u >= 2:
                        use(u - 2)
                for u in range(U - 2, U):
                    use(u)
                end(dve)

            @block.scalar
            def _(act):
                begin(act)

                def copy(r):
                    blocks = rounds[r][1]
                    act.wait_ge(probs_turned.sem, probs_turned.at(r + 1))
                    if r >= 2:
                        act.wait_ge(turned_copied.sem, turned_copied.at(r - 1))
                    act.activation(sbuf_t[:, r % 2, 0:len(blocks) * P], bank(4 + r % 2)[:, 0:len(blocks) * P],
                                   ACT.Copy).then_inc(turned_copied.sem, 1)

                def exps(u):
                    t, heads, sets = units[u]
                    nh = len(heads)
                    w = width[u] // nh
                    act.wait_ge(maxima_ready.sem, maxima_ready.at(u + 1))
                    if u >= 4:
                        act.wait_ge(context_read.sem, context_read.at(u - 3))
                    for i in range(nh):
                        ins = act.activation(sbuf_p[:, u % 2, i * w:(i + 1) * w], sbuf_s[:, u % 2, i * w:(i + 1) * w],
                                             ACT.Exp, bias=stat[:, 8 * (u % 2) + i:8 * (u % 2) + i + 1],
                                             accum_out=stat[:, 16 + 8 * (u % 4) + i:17 + 8 * (u % 4) + i])
                    ins.then_inc(probs_ready.sem, 1)

                exps(0)
                r = 0
                for u in range(U):
                    mine = [i for i, rd in enumerate(rounds) if rd[0] == u]
                    copy(mine[0])
                    if u + 1 < U:
                        exps(u + 1)
                    for i in mine[1:]:
                        copy(i)
                end(act)

            scores_ready.close(U)
            scores_read.close(U)
            maxima_ready.close(U)
            probs_ready.close(U)
            probs_turned.close(len(rounds))
            turned_copied.close(len(rounds))
            context_ready.close(U)
            context_read.close(U)
            close_stage()

        def turn_rows(src, dst, tiles):
            banks = tiles // 2
            assert banks <= 4

            @block.tensor
            def _(pe):
                begin(pe)
                for b in range(banks):
                    fb = bank(b)
                    for j in range(2):
                        for t in range(TT):
                            mm = nc.tensor.transpose(fb[:, j * S + t * P:j * S + (t + 1) * P], src(t, 2 * b + j), ident)
                    mm.then_inc(bank_full.sem, 1)
                end(pe)

            @block.scalar
            def _(act):
                begin(act)
                for b in range(banks):
                    act.wait_ge(bank_full.sem, bank_full.at(b + 1))
                    act.activation(dst[0][:, 2 * b:2 * b + 2, :].rearrange("p a s -> p (a s)"), bank(b % 4), ACT.Copy) \
                       .then_inc(inner_ready.sem, 1)
                end(act)

            @block.vector
            def _(dve):
                begin(dve)
                for b in range(banks):
                    dve.wait_ge(inner_ready.sem, inner_ready.at(b + 1))
                    dve.tensor_tensor(dst[1][:, 2 * b:2 * b + 2, :].rearrange("p a s -> p (a s)"), bank(b % 4),
                                      dst[0][:, 2 * b:2 * b + 2, :].rearrange("p a s -> p (a s)").bitcast(F32),
                                      ALU.subtract).then_inc(parts_ready.sem, 1)
                end(dve)

            bank_full.close(banks)
            inner_ready.close(banks)
            hand_over(banks)
            close_stage()

        G = region(0, 32, S)
        Y = region(8192, 4, 4, S).rearrange("p a b s -> p a b s")
        L0 = 8192 + 4096
        qk = region(L0, TT, 1024)
        idx = region(L0 + 2048, TT, IDX_COLS)
        va = region(L0 + 2704, TT, WIDTH)
        qT = region(L0 + 3728, HEADS, S)
        kT = region(L0 + 4752, HEADS, S)
        qiT = region(L0 + 5776, 2, S)
        kiT = region(L0 + 6288, S)
        score = region(L0 + 6544, TT, S)
        picked = region(L0 + 7056, TT, S)
        X0 = L0 + 7568
        glu = region(X0, 4, S + LONG - 1)
        conv_b = region(X0 + 1144, 4, S)
        gb = region(X0 + 2168, 4, S)
        vpad = region(X0 + 3192, 4, S + SHORT - 1)
        SQ = X0 + 4224
        sqT = region(SQ, HEADS, S)
        skT = region(SQ + 1024, HEADS, S)
        sv = region(SQ + 2048, TT, WIDTH)
        YT = [over("branches_high", at_h, 0, [16, S]), over("branches_low", at_work, L0, [16, S])]
        mT = [over(f"merged{i}", at_work, X0 + 2048 + i * KT * S, [KT, S]) for i in range(2)]

        def mixer_rows_stage(l):
            n0, count = len(stream.freed), 8

            @block.tensor
            def _(pe):
                for n in range(count):
                    wd = stream.units[n0 + n][2]
                    rows_product(pe, n, take_unit(pe, n0 + n), hT, wd).then_inc(bank_full.sem, 1)
                    release_unit(bank_full, n + 1)
                end(pe)

            @block.scalar
            def _(act):
                begin(act)
                for n in range(count):
                    make_high(act, n0 + n + HIGH_SLOTS)
                    wd = stream.units[n0 + n][2]
                    c = n % 2 * S
                    buf, at = ((qk, 0), (qk, WIDTH), (va, 0), (idx, 0))[n // 2]
                    dst = buf[:, :, at + c:at + c + wd]
                    act.wait_ge(bank_full.sem, bank_full.at(n + 1))
                    act.activation(dst, bank(n % 4).rearrange("p (t s) -> p t s", t=TT)[:, :, 0:wd], ACT.Copy) \
                       .then_inc(bank_free.sem, 1)
                if l == 0:
                    act.wait_ge(rows_scaled.sem, rows_scaled.at(1))
                    act.activation(rot[:, :, :, :].rearrange("p a t f -> p (a t) f"), ang, ACT.Sin)
                make_high(act, n0 + count + HIGH_SLOTS)
                end(act)

            @block.vector
            def _(dve):
                begin(dve)
                if l == 0:
                    rotary_angles(dve)
                make_lows(dve, n0 + count)
                end(dve)

            if l == 0:
                rows_scaled.close(1)
            bank_full.close(count)
            bank_free.close(count)
            close_stage()

        def rotate(dve, view, t, heads, half, at, tmp):
            c = spread(rot[:, 0, t, at:at + half], 1, heads)
            s = spread(rot[:, 1, t, at:at + half], 1, heads)
            x1, x2 = view[:, :, 0:half], view[:, :, half:2 * half]
            t1, t2, t3, t4 = (tmp[:, i, 0:heads * half].rearrange("p (h f) -> p h f", h=heads) for i in range(4))
            dve.tensor_tensor(t1, x1, c, ALU.mult)
            dve.tensor_tensor(t2, x2, s, ALU.mult)
            dve.tensor_tensor(t3, x2, c, ALU.mult)
            v_link(dve.tensor_tensor(t4, x1, s, ALU.mult))
            dve.tensor_tensor(x1, t1, t2, ALU.subtract)
            v_link(dve.tensor_tensor(x2, t3, t4, ALU.add))

        def mixer_columns_stage(l):
            n0, count = len(stream.freed), 16
            dsts = ((glu, LONG - 1), (conv_b, 0), (gb, 0), (vpad, SHORT - 1), (Y[:, 2], 0), (sqT, 0), (skT, 0))

            @block.tensor
            def _(pe):
                begin(pe)
                for n in range(count):
                    w = take_unit(pe, n0 + n)
                    if n < 2 * len(dsts):
                        mm = columns_product(pe, n, w, hT, (0, P))
                    else:
                        mm = rows_product(pe, n, w, hT, S)
                    mm.then_inc(bank_full.sem, 1)
                    release_unit(bank_full, n + 1)
                end(pe)

            @block.scalar
            def _(act):
                begin(act)
                for n in range(count):
                    make_high(act, n0 + n + HIGH_SLOTS)
                    act.wait_ge(bank_full.sem, bank_full.at(n + 1))
                    j = n % 2
                    if n < 2 * len(dsts):
                        dst, off = dsts[n // 2]
                        view = dst[:, 2 * j:2 * j + 2, off:off + S]
                    else:
                        view = sv[:, :, j * S:(j + 1) * S]
                    act.activation(view, bank(n % 4).rearrange("p (j s) -> p j s", j=2),
                                   ACT.Sigmoid if n // 2 == 1 else ACT.Copy).then_inc(bank_free.sem, 1)
                    if n == 1:
                        square_root(act, stat[:, 84:102], stat[:, 102:120], 1)
                    if l == 0 and n % 4 == 3:
                        act.dma_start(table_dram[n // 4, :, :, 0:SPAN], spread(tab[0:QH, n // 4, :], 1, P)) \
                           .then_inc(side_store.sem, 16)
                make_high(act, n0 + count + HIGH_SLOTS)
                end(act)

            @block.vector
            def _(dve):
                begin(dve)
                dve.memset(glu[:, :, 0:LONG - 1], 0.0)
                dve.memset(vpad[:, :, 0:SHORT - 1], 0.0)
                sq = region(0, 8, P)
                tmp = region(1024, 4, P)
                squares = stat[:, 48:66].rearrange("p (t h) -> p t h", t=TT)
                for t in range(TT):
                    view = qk[:, t, :].rearrange("p (h d) -> p h d", h=8)
                    ki = idx[:, t, 256:320]
                    v_link(dve.tensor_tensor(sq, view, view, ALU.mult))
                    v_link(dve.tensor_reduce(squares[:, t, 0:8], sq, AX.X, ALU.add))
                    v_link(dve.tensor_tensor(sq[:, 0, 0:IDX_DIM], ki, ki, ALU.mult))
                    v_link(dve.tensor_reduce(squares[:, t, 8:9], sq[:, 0, 0:IDX_DIM], AX.X, ALU.add))
                    v_link(dve.tensor_scalar(squares[:, t, 8:9], squares[:, t, 8:9], float(P) / IDX_DIM, None, ALU.mult))
                inverse_root(dve, stat[:, 120:138], stat[:, 84:102], stat[:, 102:120], stat[:, 48:66], 1.0 / P, 1)
                roots = stat[:, 120:138].rearrange("p (t h) -> p t h", t=TT)
                for t in range(TT):
                    view = qk[:, t, :].rearrange("p (h d) -> p h d", h=8)
                    ki = idx[:, t, 256:320]
                    v_link(dve.tensor_tensor(view, view, spread(roots[:, t, 0:8], 2, P), ALU.mult))
                    dve.tensor_tensor(view[:, 0:4], view[:, 0:4], spread(g_head[:, l, 0, :], 1, HEADS), ALU.mult)
                    v_link(dve.tensor_tensor(view[:, 4:8], view[:, 4:8], spread(g_head[:, l, 1, :], 1, HEADS), ALU.mult))
                    rotate(dve, view, t, 8, 16, 0, tmp)
                    v_link(dve.scalar_tensor_tensor(ki, ki, roots[:, t, 8:9], g_kidx[:, l, :], ALU.mult, ALU.mult))
                    rotate(dve, idx[:, t, 0:320].rearrange("p (h d) -> p h d", h=5), t, 5, 8, 16, tmp)
                dve.wait_ge(bank_free.sem, bank_free.at(4))
                v_link(dve.tensor_tensor(glu[:, :, LONG - 1:], glu[:, :, LONG - 1:], conv_b, ALU.mult))
                last = [0] * 4
                for k in range(LONG):
                    for ct in range(4):
                        tap = par[:, R_LONG(l) + 4 * k + ct:R_LONG(l) + 4 * k + ct + 1]
                        if k == 0:
                            cb = R_MISC(l) + M_CB + ct
                            ins = dve.tensor_scalar(conv_b[:, ct, :], glu[:, ct, 0:S], tap, par[:, cb:cb + 1],
                                                    ALU.mult, ALU.add)
                        else:
                            v_wait(last[ct])
                            ins = dve.scalar_tensor_tensor(conv_b[:, ct, :], glu[:, ct, k:k + S], tap, conv_b[:, ct, :],
                                                           ALU.mult, ALU.add)
                        last[ct] = v_done(ins)
                end(dve)

            bank_full.close(16)
            bank_free.close(16)
            if l == 0:
                side_store.close(64)
            close_roots(1)
            close_stage()

        def mixer_turn_stage(l):
            kk = region(0, TT, P)
            srcs = []
            for h in range(8):
                dst = qT[:, h, :] if h < 4 else kT[:, h - 4, :]
                srcs.append((lambda t, h=h: qk[:, t, h * P:(h + 1) * P], dst))
            for h in range(2):
                srcs.append((lambda t, h=h: idx[:, t, h * P:(h + 1) * P], qiT[:, h, :]))
            srcs.append((lambda t: kk[:, t, :], kiT))

            @block.vector
            def _(dve):
                begin(dve)
                kd = kk.rearrange("p t (a d) -> p t a d", a=2)
                for t in range(TT):
                    ins = dve.tensor_copy(kd[:, t], spread(idx[:, t, 256:320], 1, 2))
                    ins.then_inc(operand_ready.sem, 1)
                dve.tensor_tensor(vpad[:, :, SHORT - 1:], vpad[:, :, SHORT - 1:], Y[:, 2], ALU.mult)
                for n in range(0, len(srcs), 2):
                    dve.wait_ge(bank_full.sem, bank_full.at(n // 2 + 1))
                    for j, (_, dst) in enumerate(srcs[n:n + 2]):
                        ins = dve.tensor_copy(dst, bank(n // 2 % 4)[:, j * S:(j + 1) * S])
                    ins.then_inc(bank_free.sem, 1)
                end(dve)

            @block.scalar
            def _(act):
                begin(act)
                end(act)

            @block.tensor
            def _(pe):
                begin(pe)
                for n in range(0, len(srcs), 2):
                    b = free_bank(pe, n // 2)
                    if n == len(srcs) - 1:
                        pe.wait_ge(operand_ready.sem, operand_ready.at(TT))
                    for j, (src, _) in enumerate(srcs[n:n + 2]):
                        for t in range(TT):
                            mm = nc.tensor.transpose(b[:, j * S + t * P:j * S + (t + 1) * P], src(t), ident)
                    mm.then_inc(bank_full.sem, 1)
                end(pe)

            operand_ready.close(TT)
            bank_full.close(6)
            bank_free.close(6)
            close_stage()

        def gates_stage(l):
            n0, count = len(stream.freed), 16

            def index_scores(t, h):
                L = (t + 1) * P
                return bank((6, 4)[t] + h % 2)[:, (h // 2) * L:(h // 2 + 1) * L]

            @block.tensor
            def _(pe):
                begin(pe)
                for h in range(HEADS):
                    lo = IDX_DIM * (h % 2)
                    for t in range(TT):
                        dst = index_scores(t, h)
                        mm = nc.tensor.matmul(dst, qiT[lo:lo + IDX_DIM, h // 2, t * P:(t + 1) * P],
                                              kiT[lo:lo + IDX_DIM, 0:(t + 1) * P], start=True, stop=True)
                mm.then_inc(side_full.sem, 1)

                def channel_means(i, src):
                    pe.wait_ge(operand_ready.sem, operand_ready.at(i + 1))
                    for ct in range(4):
                        mm = nc.tensor.matmul(bank(7)[:, i * S:(i + 1) * S], cst[:, C_MEAN:C_MEAN + P], src[:, ct, 0:S],
                                              start=(ct == 0), stop=(ct == 3))
                    mm.then_inc(side_full.sem, 1)

                for n in range(count):
                    columns_product(pe, n, take_unit(pe, n0 + n), hT, (0, P)).then_inc(bank_full.sem, 1)
                    release_unit(bank_full, n + 1)
                    if n == 5:
                        channel_means(0, conv_b)
                    if n == 9:
                        channel_means(1, glu)
                end(pe)

            @block.scalar
            def _(act):
                begin(act)
                act.wait_ge(side_store.sem, side_store.at(0))
                for n in range(count):
                    make_high(act, n0 + n + HIGH_SLOTS)
                    act.wait_ge(bank_full.sem, bank_full.at(n + 1))
                    for j in range(2):
                        g = 2 * n + j
                        col = R_MISC(l) + M_GATE + g
                        ins = act.activation(G[:, g, :], bank(n % 4)[:, j * S:(j + 1) * S], ACT.Sigmoid,
                                             bias=par[:, col:col + 1])
                    ins.then_inc(bank_free.sem, 1)
                    if n == 11:
                        square_root(act, gb[:, 1, :], gb[:, 2, :], 1)
                make_high(act, n0 + count + HIGH_SLOTS)
                act.wait_ge(operand_ready.sem, operand_ready.at(3))
                for ct in range(4):
                    cg, cb = R_MISC(l) + M_LNG + ct, R_MISC(l) + M_LNB + ct
                    act.activation(Y[:, 1, ct, :], conv_b[:, ct, :], ACT.Silu, bias=par[:, cb:cb + 1],
                                   scale=par[:, cg:cg + 1])
                end(act)

            @block.vector
            def _(dve):
                begin(dve)
                last = [0] * 4
                for k in range(SHORT):
                    for ct in range(4):
                        col = R_MISC(l) + M_CC + 4 * k + ct
                        tap = par[:, col:col + 1]
                        if k == 0:
                            ins = dve.tensor_scalar(Y[:, 2, ct, :], vpad[:, ct, 0:S], tap, None, ALU.mult)
                        else:
                            v_wait(last[ct])
                            ins = dve.scalar_tensor_tensor(Y[:, 2, ct, :], vpad[:, ct, k:k + S], tap, Y[:, 2, ct, :],
                                                           ALU.mult, ALU.add)
                        last[ct] = v_done(ins)
                v_wait(last[3])
                dve.tensor_tensor(Y[:, 2], Y[:, 2], gb, ALU.mult)
                v_link(dve.memset(score[:, 0, P:S], NEG))
                dve.wait_ge(side_full.sem, side_full.at(1))
                tmp = picked
                for t in range(TT):
                    L = (t + 1) * P
                    for h in range(HEADS):
                        src = index_scores(t, h)
                        w = idx[:, t, 320 + h:321 + h]
                        if h == 0:
                            v_link(dve.tensor_scalar(score[:, t, 0:L], src, 0.0, w, ALU.max, ALU.mult))
                        else:
                            v_link(dve.tensor_scalar(tmp[:, t, 0:L], src, 0.0, w, ALU.max, ALU.mult))
                            v_link(dve.tensor_tensor(score[:, t, 0:L], score[:, t, 0:L], tmp[:, t, 0:L], ALU.add))
                    v_link(dve.tensor_tensor(score[:, t, t * P:L], score[:, t, t * P:L], cst[:, C_CAUS:C_CAUS + P],
                                             ALU.add))
                nc.vector.nop().then_inc(operand_ready.sem, 1)
                top = stat[:, 64:80].rearrange("p (t e) -> p t e", t=TT)
                for r in range(TOPK // 8):
                    n = [v_done(dve.max(top[:, t, :], score[:, t, :])) for t in range(TT)]
                    for t in range(TT):
                        v_wait(n[t])
                        n[t] = v_done(dve.match_replace(score[:, t, :], top[:, t, :], score[:, t, :], TAKEN))
                    v_wait(n[-1])
                v_link(dve.tensor_scalar(picked, score, 0.5 * TAKEN, NEG, ALU.is_gt, ALU.mult))
                for t in range(TT):
                    last_ = v_done(dve.tensor_tensor(picked[:, t, t * P:(t + 1) * P], picked[:, t, t * P:(t + 1) * P],
                                                     cst[:, C_CAUS:C_CAUS + P], ALU.add))
                dve.wait_ge(side_full.sem, side_full.at(2))
                v_link(dve.tensor_tensor(conv_b, conv_b, spread(bank(7)[:, 0:S], 1, 4), ALU.subtract))
                dve.tensor_tensor(glu[:, :, 0:S], conv_b, conv_b, ALU.mult).then_inc(operand_ready.sem, 1)
                dve.wait_ge(side_full.sem, side_full.at(3))
                rstd = gb[:, 0, :]
                inverse_root(dve, rstd, gb[:, 1, :], gb[:, 2, :], bank(7)[:, S:2 * S], 1.0, 1)
                dve.tensor_tensor(conv_b, conv_b, spread(rstd, 1, 4), ALU.mult).then_inc(operand_ready.sem, 1)
                end(dve)

            side_full.close(3)
            operand_ready.close(3)
            close_roots(1)
            bank_full.close(16)
            bank_free.close(16)
            close_stage()

        def sparse_attention_stage(l):
            sbuf_s = region(X0, 2, 512)
            sbuf_p = region(X0 + 1024, 2, 512)
            sbuf_t = region(X0 + 2048, 2, 512)
            ctx_rows = region(X0 + 3072, TT, WIDTH)
            units = [(1, (0, 1), (0,)), (1, (2, 3), (0,)), (0, (0, 1, 2, 3), (0,))]

            def bias(u, unit, sc, dst, L):
                t, heads, _ = unit
                n = len(heads)
                yield (sc.rearrange("p (h s) -> p h s", h=n), dst.rearrange("p (h s) -> p h s", h=n),
                       spread(picked[:, t, 0:L], 1, n))

            def finish(dve, u, unit, res, rec):
                t, heads, _ = unit
                n = len(heads)
                o = ctx_rows[:, t, heads[0] * P:(heads[0] + n) * P].rearrange("p (h d) -> p h d", h=n)
                dve.tensor_tensor(o, res.rearrange("p (h d) -> p h d", h=n), spread(rec, 2, P), ALU.mult) \
                   .then_inc(context_read.sem, 1)

            attention(units, lambda h, st, t: qT[:, h, t * P:(t + 1) * P], lambda h, st: kT[:, h, :],
                      lambda st, kt, h: va[:, kt, h * P:(h + 1) * P], bias, float(P) ** -0.5, P,
                      (sbuf_s, sbuf_p, sbuf_t), finish)
            turn_rows(lambda t, j: ctx_rows[:, t, j * P:(j + 1) * P], [v[:, 0:4] for v in YT], 4)
            handed_over.clear()

        def stick_breaking_stage():
            W = S + P
            z = region(X0, HEADS, W)
            lk = region(X0 + HEADS * W, HEADS, W)
            soft = region(L0 + 3728, HEADS, W)

            @block.tensor
            def _(pe):
                begin(pe)
                for h in range(HEADS):
                    b = bank(h)
                    nc.tensor.matmul(b[:, 0:S], skT[:, h, 0:P], sqT[:, h, :], start=True, stop=True)
                    nc.tensor.matmul(b[:, S:W], skT[:, h, P:S], sqT[:, h, P:S], start=True, stop=True) \
                      .then_inc(scores_ready.sem, 1)
                for h in range(HEADS):
                    pe.wait_ge(operand_ready.sem, operand_ready.at(h + 1))
                    b = bank(4 + h)
                    tri, one = cst[:, C_TRI:C_TRI + P], cst[:, C_ONE:C_ONE + P]
                    nc.tensor.matmul(b[:, 0:S], tri, lk[:, h, 0:S], start=True, stop=False)
                    nc.tensor.matmul(b[:, P:S], one, lk[:, h, S:W], start=False, stop=True)
                    nc.tensor.matmul(b[:, S:W], tri, lk[:, h, S:W], start=True, stop=True) \
                      .then_inc(side_full.sem, 1)
                for h in range(HEADS):
                    pe.wait_ge(probs_ready.sem, probs_ready.at(h + 1))
                    b = bank(h)
                    nc.tensor.matmul(b[:, 0:S], sv[:, 0, h * P:(h + 1) * P], lk[:, h, 0:S], start=True, stop=False)
                    nc.tensor.matmul(b[:, P:S], sv[:, 1, h * P:(h + 1) * P], lk[:, h, S:W], start=False, stop=True) \
                      .then_inc(context_ready.sem, 1)
                end(pe)

            @block.vector
            def _(dve):
                begin(dve)
                scale = float(P) ** -0.5
                dst = lk
                for h in range(HEADS):
                    dve.wait_ge(scores_ready.sem, scores_ready.at(h + 1))
                    v_link(dve.tensor_scalar(z[:, h, :], bank(h)[:, 0:W], scale, None, ALU.mult))
                    dve.scalar_tensor_tensor(soft[:, h, :], z[:, h, :], -1.0, z[:, h, :], ALU.mult, ALU.min) \
                       .then_inc(inner_taken.sem, 1)
                for h in range(HEADS):
                    dve.wait_ge(inner_ready.sem, inner_ready.at(h + 1))
                    v_link(dve.scalar_tensor_tensor(lk[:, h, :], z[:, h, :], 0.0, soft[:, h, :], ALU.max, ALU.add))
                    keep, neg = cst[:, C_SKEEP:C_SKEEP + P], cst[:, C_SNEG:C_SNEG + P]
                    v_link(dve.tensor_scalar(lk[:, h, :], lk[:, h, :], -1.0, None, ALU.mult))
                    for c in (0, S):
                        dve.tensor_tensor(z[:, h, c:c + P], z[:, h, c:c + P], neg, ALU.add)
                        n = v_done(dve.tensor_tensor(lk[:, h, c:c + P], lk[:, h, c:c + P], keep, ALU.mult))
                    v_wait(n)
                    nc.vector.nop().then_inc(operand_ready.sem, 1)
                for h in range(HEADS):
                    dve.wait_ge(side_full.sem, side_full.at(h + 1))
                    dve.tensor_tensor(z[:, h, :], z[:, h, :], bank(4 + h)[:, 0:W], ALU.add).then_inc(side_free.sem, 1)
                for h in range(HEADS):
                    dve.wait_ge(context_ready.sem, context_ready.at(h + 1))
                    dve.tensor_copy(Y[:, 3, h, :], bank(h)[:, 0:S])
                end(dve)

            @block.scalar
            def _(act):
                begin(act)
                done = []
                for h in range(HEADS):
                    act.wait_ge(inner_taken.sem, inner_taken.at(h + 1))
                    done.append(s_done(act.activation(soft[:, h, :], soft[:, h, :], ACT.Exp)))
                for h in range(HEADS):
                    s_wait(done[h])
                    act.activation(soft[:, h, :], soft[:, h, :], ACT.Ln, bias=1.0).then_inc(inner_ready.sem, 1)
                for h in range(HEADS):
                    act.wait_ge(side_free.sem, side_free.at(h + 1))
                    act.activation(lk[:, h, :], z[:, h, :], ACT.Exp).then_inc(probs_ready.sem, 1)
                end(act)

            scores_ready.close(HEADS)
            inner_taken.close(HEADS)
            inner_ready.close(HEADS)
            operand_ready.close(HEADS)
            side_full.close(HEADS)
            side_free.close(HEADS)
            probs_ready.close(HEADS)
            context_ready.close(HEADS)
            close_stage()

        def branch_output_stage():
            n0 = len(stream.freed)
            merged = region(X0, KT, S)

            @block.tensor
            def _(pe):
                begin(pe)
                for i in range(4):
                    if i:
                        pe.wait_ge(operand_ready.sem, operand_ready.at(i))
                    for h in range(2):
                        w = take_unit(pe, n0 + 2 * i + h)
                        for j in range(2):
                            n = 4 * i + 2 * h + j
                            columns_product(pe, n, w, [v[:, 4 * i:4 * i + 4] for v in YT],
                                            (2 * j * P, (2 * j + 1) * P)).then_inc(bank_full.sem, 1)
                        release_unit(bank_full, n + 1)
                end(pe)

            @block.scalar
            def _(act):
                begin(act)
                for i in range(1, 4):
                    act.activation(YT[0][:, 4 * i:4 * i + 4], Y[:, i], ACT.Copy).then_inc(inner_ready.sem, 1)
                for i in range(4):
                    make_high(act, n0 + 2 * i + 4)
                for j in range(4):
                    make_high(act, n0 + 8 + (j + 2) // 2)
                    act.wait_ge(context_ready.sem, context_ready.at(j + 1))
                    act.activation(mT[0][:, 2 * j:2 * j + 2], merged[:, 2 * j:2 * j + 2], ACT.Copy) \
                       .then_inc(inner_ready.sem, 1)
                make_high(act, n0 + 8 + HIGH_SLOTS)
                end(act)

            @block.vector
            def _(dve):
                begin(dve)
                for i in range(1, 4):
                    dve.wait_ge(inner_ready.sem, inner_ready.at(i))
                    dve.tensor_tensor(YT[1][:, 4 * i:4 * i + 4], Y[:, i], YT[0][:, 4 * i:4 * i + 4].bitcast(F32),
                                      ALU.subtract).then_inc(operand_ready.sem, 1)
                for n in range(16):
                    i, j = n // 4, n % 4
                    g = G[:, 8 * i + 2 * j:8 * i + 2 * j + 2, :].rearrange("p a s -> p (a s)")
                    m = merged[:, 2 * j:2 * j + 2, :].rearrange("p a s -> p (a s)")
                    dve.wait_ge(bank_full.sem, bank_full.at(n + 1))
                    if i == 0:
                        v_link(dve.tensor_tensor(m, g, bank(n % 4), ALU.mult))
                    else:
                        v_link(dve.tensor_tensor(g, g, bank(n % 4), ALU.mult))
                        v_link(dve.tensor_tensor(m, m, g, ALU.add))
                    if i == 3:
                        nc.vector.nop().then_inc(context_ready.sem, 1)
                    nc.vector.nop().then_inc(bank_free.sem, 1)
                for j in range(4):
                    dve.wait_ge(inner_ready.sem, inner_ready.at(4 + j))
                    dve.tensor_tensor(mT[1][:, 2 * j:2 * j + 2], merged[:, 2 * j:2 * j + 2],
                                      mT[0][:, 2 * j:2 * j + 2].bitcast(F32), ALU.subtract) \
                       .then_inc(parts_ready.sem, 1)
                end(dve)

            bank_full.close(16)
            bank_free.close(16)
            operand_ready.close(3)
            inner_ready.close(7)
            context_ready.close(4)
            hand_over(4)
            close_stage()

        fT = [over(f"hidden{i}", at_work, i * FT * S, [FT, S]) for i in range(2)]

        def compressed_attention_layer():
            table = region(0, QH, S)
            q2 = region(4096, KT, S)
            kcmp = region(6144, 2, GROUPS, S).rearrange("p a g s -> p a g s")
            kd = region(8192, 2, GROUPS, S).rearrange("p a g s -> p a g s")
            vv = region(10240, 2, TT, S).rearrange("p a g s -> p a g s")
            gl = region(11264, TT, 3 * QH)
            o = region(11360, TT, D)
            c0 = 13408
            blk = [region(11360, CMP_BLOCK // 2, P), region(c0 + 5488, CMP_BLOCK // 2, P)]
            pairs = region(c0, 4, 2, S)
            hid = region(c0, 2, CMP_HIDDEN)
            hid2 = region(c0 + 512, 2, CMP_HIDDEN)
            hidT = region(c0 + 1024, 2, 2, P).rearrange("p i a b -> p i a b")
            kcT = region(c0 + 2816, P)
            vc = region(c0 + 2944, GROUPS, DH)
            cbias = region(c0 + 3200, TT, CMP_N, QH)
            cprob = region(c0 + 3680, TT, QH, CMP_PAD)
            w2 = region(c0 + 4704, 2, 2, DH)
            relb = region(c0 + 4960, QH)
            onehot = region(c0 + 4976, 512)
            sbuf_s = region(c0 + 5488, 2, 512)
            sbuf_p = region(c0 + 6512, 2, 512)
            sbuf_t = region(c0 + 7536, 2, 512)
            assert CMP_N <= CMP_PAD
            blkT = [[over(f"key_blocks{i}", at_work, 22000 + i * 2048, [CMP_BLOCK // 2, P]) for i in range(2)],
                    [over(f"value_blocks{i}", at_h, i * 2048, [CMP_BLOCK // 2, P]) for i in range(2)]]
            n0, count = len(stream.freed), 11
            by_rows = (7, 9, 10)
            EARLY = 4
            after_half = lambda n: n + 4 * (n >= EARLY)

            @block.tensor
            def _(pe):
                for n in range(count):
                    if n == EARLY:
                        two_halves(pe, EARLY, pairs, (0, 1), 1)
                    w = take_unit(pe, n0 + n)
                    b = after_half(n)
                    if n in by_rows:
                        mm = rows_product(pe, b, w, hT, stream.units[n0 + n][2])
                    else:
                        mm = columns_product(pe, b, w, hT, (0, P))
                    mm.then_inc(bank_full.sem, 1)
                    release_unit(bank_full, b + 1)
                two_halves(pe, count + 4, pairs, (2, 3), 2)
                pe.wait_ge(table_load.sem, table_load.at(5 * 16))
                for t in range(TT):
                    for m in range(CMP_N):
                        d0 = (S - 1) + t * P - CMP_STRIDE * m - (CMP_BLOCK - 1)
                        mm = nc.tensor.matmul(bank(4 + t)[:, m * QH:(m + 1) * QH], onehot[0:BUCKETS + 1, d0:d0 + P],
                                              relb[0:BUCKETS + 1, :], start=True, stop=True)
                mm.then_inc(side_full.sem, 1)
                end(pe)

            @block.scalar
            def _(act):
                begin(act)
                act.wait_ge(side_store.sem, side_store.at(0))
                src = bass.AP(table_dram.tensor, P - 1, [[SPAN, P], [HEAD_SKEW, QH], [1, S]])
                act.dma_start(table, src).then_inc(table_load.sem, 16)
                act.dma_start(onehot[0:BUCKETS + 1, :], onehots[:, O_CMP:O_CMP + 512]).then_inc(table_load.sem, 16)
                for n, name in enumerate(("a_w2_k_2", "a_w2_v_2")):
                    act.dma_start(w2[:, n], a[name][0].rearrange("(k p) d -> p k d", p=P)).then_inc(table_load.sem, 16)
                act.wait_ge(operand_ready.sem, operand_ready.at(1))
                act.dma_start(work[0:BUCKETS, c0 + 4960:c0 + 4976], a["rel_bias_2"]).then_inc(table_load.sem, 16)

                def halves(n, sets):
                    for i in sets:
                        for gp in range(2):
                            act.wait_ge(bank_full.sem, bank_full.at(n + 1))
                            b = bank(n % 4).rearrange("p (j s) -> p j s", j=2)
                            if i < 2:
                                act.activation(kcmp[0:DH, i, 2 * gp:2 * gp + 2, :], b[0:DH], ACT.Copy)
                                ins = act.activation(kcmp[DH:P, i, 2 * gp:2 * gp + 2, 0:S - 1], b[DH:P, :, 1:S], ACT.Copy)
                            else:
                                ins = act.activation(kd[:, i - 2, 2 * gp:2 * gp + 2, :], b, ACT.Copy)
                            ins.then_inc(bank_free.sem, 1)
                            n += 1

                for n, dst in enumerate((pairs[:, 0], pairs[:, 1], q2[:, 0:2], q2[:, 2:4], q2[:, 4:6], q2[:, 6:8],
                                         pairs[:, 2], vv[:, 0], pairs[:, 3], vv[:, 1], gl)):
                    make_high(act, n0 + n + HIGH_SLOTS)
                    if n == EARLY:
                        halves(EARLY, (0, 1))
                    b = after_half(n)
                    act.wait_ge(bank_full.sem, bank_full.at(b + 1))
                    wd = stream.units[n0 + n][2]
                    act.activation(dst, bank(b % 4).rearrange("p (a s) -> p a s", a=2)[:, :, 0:wd], ACT.Copy) \
                       .then_inc(bank_free.sem, 1)
                    if n in (1, 8):
                        act.wait_ge(bank_free.sem, bank_free.at(b + 1))
                        nc.scalar.nop().then_inc(inner_ready.sem, 1)
                halves(count + 4, (2, 3))
                act.wait_ge(operand_ready.sem, operand_ready.at(2))
                act.activation(blkT[0][0][:, :, :], blk[0], ACT.Copy).then_inc(inner_ready.sem, 1)
                make_high(act, n0 + count + HIGH_SLOTS)
                end(act)

            @block.vector
            def _(dve):
                begin(dve)
                dve.memset(work[0:BUCKETS + 1, c0 + 4960:c0 + 4976], NEG).then_inc(operand_ready.sem, 1)
                for i in range(2):
                    v_link(dve.memset(blk[i], 0.0))
                make_lows(dve, n0 + EARLY)
                dve.wait_ge(bank_free.sem, bank_free.at(EARLY + 4))
                for i in range(2):
                    pe_col = R_PART2 + (M2_PEK, M2_PEV)[i]
                    bv = blk[i].rearrange("p m (g n) -> p m g n", g=GROUPS)
                    for m in range(CMP_BLOCK // 2):
                        src = kcmp[:, i, :, 2 * m:2 * m + CMP_STRIDE * (CMP_N - 1) + 1:CMP_STRIDE]
                        ins = dve.tensor_scalar(bv[:, m, :, 0:CMP_N], src, par[:, pe_col + m:pe_col + m + 1], None, ALU.add)
                    v_link(ins)
                nc.vector.nop().then_inc(operand_ready.sem, 1)
                make_lows(dve, n0 + count)
                dve.wait_ge(bank_free.sem, bank_free.at(count + 4))
                dve.tensor_tensor(gl, gl, spread(b_gl[:, :], 1, TT), ALU.add)
                dve.wait_ge(inner_ready.sem, inner_ready.at(3))
                dve.tensor_tensor(blkT[0][1][:, :, :], blk[0], blkT[0][0][:, :, :].bitcast(F32), ALU.subtract)
                dve.wait_ge(side_full.sem, side_full.at(1))
                for t in range(TT):
                    dve.tensor_copy(cbias[:, t].rearrange("p n h -> p (n h)"), bank(4 + t)[:, 0:CMP_N * QH])
                end(dve)

            bank_full.close(count + 8)
            bank_free.close(count + 8)
            inner_ready.close(3)
            operand_ready.close(2)
            table_load.close(5 * 16)
            side_full.close(1)
            close_stage()

            u0 = len(stream.freed)

            @block.tensor
            def _(pe):
                begin(pe)
                for i in range(2):
                    if i:
                        pe.wait_ge(operand_ready.sem, operand_ready.at(1))
                    for c in range(2):
                        w = take_unit(pe, u0 + 2 * i + c)
                        for k in range(8):
                            m = 8 * c + k
                            mm = three_passes(bank(i)[:, 0:CMP_HIDDEN], [v[:, m, :] for v in blkT[i]],
                                              [v[:, k, :] for v in w], m == 0, m == CMP_BLOCK // 2 - 1)
                        mm.then_inc(side_full.sem, 1)
                        release_unit(side_full, 2 * i + c + 1)
                for i in range(2):
                    pe.wait_ge(operand_ready.sem, operand_ready.at(3 * i + 3))
                    for k in range(2):
                        mm = nc.tensor.transpose(bank(2 + 2 * i)[:, k * P:(k + 1) * P], hid[:, i, k * P:(k + 1) * P],
                                                 ident)
                    mm.then_inc(side_full.sem, 1)
                    pe.wait_ge(operand_ready.sem, operand_ready.at(3 * i + 4))
                    if i == 0:
                        for lo in (0, DH):
                            for k in range(2):
                                mm = nc.tensor.matmul(bank(3)[lo:lo + DH, 0:P], w2[:, 0, k, :], hidT[:, 0, k, :],
                                                      start=(k == 0), stop=(k == 1))
                    else:
                        for g in range(GROUPS):
                            for k in range(2):
                                mm = nc.tensor.matmul(bank(5)[0:CMP_PAD, g * DH:(g + 1) * DH],
                                                      hidT[:, 1, k, g * CMP_PAD:(g + 1) * CMP_PAD], w2[:, 1, k, :],
                                                      start=(k == 0), stop=(k == 1))
                    mm.then_inc(side_full.sem, 1)
                end(pe)

            @block.scalar
            def _(act):
                begin(act)
                act.activation(blkT[1][0][:, :, :], blk[1], ACT.Copy).then_inc(inner_ready.sem, 1)
                make_high(act, u0 + 4)
                for i in range(2):
                    act.wait_ge(operand_ready.sem, operand_ready.at(3 * i + 2))
                    act.activation(hid2[:, i, :], hid2[:, i, :], ACT.Tanh, scale=math.sqrt(2.0 / math.pi)) \
                       .then_inc(inner_ready.sem, 1)
                make_high(act, u0 + 4 + HIGH_SLOTS)
                end(act)

            @block.vector
            def _(dve):
                begin(dve)
                dve.wait_ge(inner_ready.sem, inner_ready.at(1))
                dve.tensor_tensor(blkT[1][1][:, :, :], blk[1], blkT[1][0][:, :, :].bitcast(F32), ALU.subtract) \
                   .then_inc(operand_ready.sem, 1)
                for i in range(2):
                    dve.wait_ge(side_full.sem, side_full.at((2, 4)[i]))
                    y, z = hid[:, i, :], hid2[:, i, :]
                    v_link(dve.tensor_copy(y, bank(i)[:, 0:CMP_HIDDEN]))
                    v_link(dve.tensor_tensor(z, y, y, ALU.mult))
                    v_link(dve.tensor_scalar(z, z, 0.044715, 1.0, ALU.mult, ALU.add))
                    dve.tensor_tensor(z, z, y, ALU.mult).then_inc(operand_ready.sem, 1)
                    dve.wait_ge(inner_ready.sem, inner_ready.at(i + 2))
                    v_link(dve.tensor_scalar(z, z, 1.0, 0.5, ALU.add, ALU.mult))
                    dve.tensor_tensor(y, y, z, ALU.mult).then_inc(operand_ready.sem, 1)
                    if i:
                        dve.wait_ge(side_full.sem, side_full.at(6))
                        dve.tensor_copy(kcT, bank(3)[:, 0:P])
                    dve.wait_ge(side_full.sem, side_full.at(2 * i + 5))
                    dve.tensor_copy(hidT[:, i].rearrange("p a b -> p (a b)"), bank(2 + 2 * i)[:, 0:2 * P]) \
                       .then_inc(operand_ready.sem, 1)
                dve.wait_ge(side_full.sem, side_full.at(8))
                for g in range(GROUPS):
                    dve.tensor_copy(vc[0:CMP_PAD, g, :], bank(5)[0:CMP_PAD, g * DH:(g + 1) * DH])
                end(dve)

            operand_ready.close(7)
            inner_ready.close(3)
            side_full.close(8)
            close_stage()

            @block.tensor
            def _(pe):
                begin(pe)
                for t in range(TT):
                    for h in range(QH):
                        lo, g = DH * (h % 2), h // PER_GROUP
                        mm = nc.tensor.matmul(bank(2 * (h % 2) + t)[:, (h // 2) * CMP_PAD:(h // 2 + 1) * CMP_PAD],
                                              q2[lo:lo + DH, h // 2, t * P:(t + 1) * P],
                                              kcT[lo:lo + DH, g * CMP_PAD:(g + 1) * CMP_PAD], start=True, stop=True)
                    mm.then_inc(scores_ready.sem, 1)
                pe.wait_ge(operand_ready.sem, operand_ready.at(TT))
                for t in range(TT):
                    for hb in range(4):
                        n = 4 * t + hb
                        if n >= 2:
                            pe.wait_ge(turned_copied.sem, turned_copied.at(n - 1))
                        for j in range(4):
                            mm = nc.tensor.transpose(bank(n % 2)[0:CMP_PAD, j * P:(j + 1) * P],
                                                     cprob[:, t, 4 * hb + j, :], ident)
                        mm.then_inc(probs_turned.sem, 1)
                        pe.wait_ge(turned_copied.sem, turned_copied.at(n + 1))
                        for j in range(4):
                            h = 4 * hb + j
                            b = bank(4 + 2 * t + h // 8)
                            mm = nc.tensor.matmul(b[:, (h % 8) * DH:(h % 8 + 1) * DH],
                                                  sbuf_t[0:CMP_PAD, n % 2, j * P:(j + 1) * P], vc[0:CMP_PAD, hb, :],
                                                  start=True, stop=True)
                    mm.then_inc(context_ready.sem, 1)
                end(pe)

            @block.scalar
            def _(act):
                begin(act)
                act.activation(gl.rearrange("p t c -> p (t c)"), gl.rearrange("p t c -> p (t c)"), ACT.Sigmoid)
                for t in range(TT):
                    act.wait_ge(maxima_ready.sem, maxima_ready.at(t + 1))
                    act.activation(cprob[:, t, :, 0:CMP_N], cprob[:, t, :, 0:CMP_N], ACT.Exp) \
                       .then_inc(probs_ready.sem, 1)
                for n in range(8):
                    act.wait_ge(probs_turned.sem, probs_turned.at(n + 1))
                    act.activation(sbuf_t[0:CMP_PAD, n % 2, :], bank(n % 2)[0:CMP_PAD, :], ACT.Copy) \
                       .then_inc(turned_copied.sem, 1)
                end(act)

            @block.vector
            def _(dve):
                begin(dve)
                v_link(dve.memset(cprob.rearrange("p t h n -> p (t h n)"), 0.0))
                for t in range(TT):
                    dve.wait_ge(scores_ready.sem, scores_ready.at(t + 1))
                    pr = cprob[:, t, :, 0:CMP_N]
                    for j in range(2):
                        sc = bank(2 * j + t)[:, 0:QH // 2 * CMP_PAD].rearrange("p (h n) -> p h n", n=CMP_PAD)[:, :, 0:CMP_N]
                        v_link(dve.scalar_tensor_tensor(pr[:, j:QH:2], sc, DH ** -0.5,
                                                        cbias[:, t, :, j:QH:2].rearrange("p n h -> p h n"),
                                                        ALU.mult, ALU.add))
                    mx = stat[:, 0:QH]
                    v_link(dve.tensor_reduce(mx, pr, AX.X, ALU.max))
                    dve.tensor_tensor(pr, pr, spread(mx, 2, CMP_N), ALU.subtract).then_inc(maxima_ready.sem, 1)
                    dve.wait_ge(probs_ready.sem, probs_ready.at(t + 1))
                    keep = cst[:, C_CMP + t * CMP_N:C_CMP + (t + 1) * CMP_N]
                    v_link(dve.tensor_tensor(pr, pr, spread(keep, 1, QH), ALU.mult))
                    v_link(dve.tensor_reduce(mx, pr, AX.X, ALU.add))
                    v_link(dve.tensor_scalar(mx, mx, 1e-30, None, ALU.max))
                    v_link(dve.reciprocal(mx, mx))
                    dve.tensor_tensor(pr, pr, spread(mx, 2, CMP_N), ALU.mult).then_inc(operand_ready.sem, 1)
                for t in range(TT):
                    dve.wait_ge(context_ready.sem, context_ready.at(t + 1))
                    g = gl[:, t, :].rearrange("p (h c) -> p h c", c=3)
                    dve.tensor_tensor(o[:, t, :].rearrange("p (h d) -> p h d", h=QH),
                                      bank(4 + 2 * t, 2).rearrange("p (h d) -> p h d", h=QH),
                                      spread(g[:, :, 0], 2, DH), ALU.mult)
                end(dve)

            scores_ready.close(TT)
            maxima_ready.close(TT)
            probs_ready.close(TT)
            operand_ready.close(TT)
            probs_turned.close(8)
            turned_copied.close(8)
            context_ready.close(TT)
            close_stage()

            units = []
            for st in range(2):
                units += [(1, (h, h + 2), (st,)) for g in range(0, QH, 4) for h in (g, g + 1)]
                units += [(0, (h, h + 2, h + 4, h + 6), (st,)) for g in range(0, QH, 8) for h in (g, g + 1)]

            def bias(u, unit, sc, dst, L):
                t, heads, _ = unit
                n = len(heads)
                yield (sc.rearrange("p (h s) -> p h s", h=n), dst.rearrange("p (h s) -> p h s", h=n),
                       table[:, heads[0]:heads[-1] + 1:2, S - L:S])

            tmp = region(c0, 2, 4 * DH)

            def finish(dve, u, unit, res, rec):
                t, heads, sets = unit
                n = len(heads)
                g = gl[:, t, :].rearrange("p (h c) -> p h c", c=3)[:, heads[0]:heads[-1] + 1:2, 1 + sets[0]]
                v_link(dve.tensor_tensor(rec, rec, g, ALU.mult))
                tv = tmp[:, u % 2, 0:n * DH].rearrange("p (h d) -> p h d", h=n)
                v_link(dve.tensor_tensor(tv, res.rearrange("p (h d) -> p h d", h=n), spread(rec, 2, DH), ALU.mult))
                nc.vector.nop().then_inc(context_read.sem, 1)
                ov = o[:, t, :].rearrange("p (h d) -> p h d", h=QH)[:, heads[0]:heads[-1] + 1:2]
                v_link(dve.tensor_tensor(ov, ov, tv, ALU.add))

            attention(units,
                      lambda h, st, t: q2[DH * (h % 2):DH * (h % 2) + DH, h // 2, t * P:(t + 1) * P],
                      lambda h, st: kd[DH * (h % 2):DH * (h % 2) + DH, st, h // PER_GROUP, :],
                      lambda st, kt, h: vv[:, st, kt, (h // PER_GROUP) * DH:(h // PER_GROUP + 1) * DH],
                      bias, DH ** -0.5, DH, (sbuf_s, sbuf_p, sbuf_t), finish)
            turn_rows(lambda t, j: o[:, t, j * P:(j + 1) * P], hT, KT)
            add_rows_product(hT, KT)

        ND = len(DILATIONS)
        d_k = region(0, ND, GROUPS, S).rearrange("p a g s -> p a g s")
        d_v = region(3072, ND, TT, S).rearrange("p a g s -> p a g s")
        d_q = region(4608, ND * KT, S)
        d_table = region(10752, ND, QH, S).rearrange("p n h s -> p n h s")
        d_rest = 10752 + ND * QH * S

        def shared_keys_stage():
            pairs = region(d_rest, ND, 2, S)
            n0, count = len(stream.freed), 2 * ND

            @block.tensor
            def _(pe):
                for n in range(count):
                    w = take_unit(pe, n0 + n)
                    mm = rows_product(pe, n, w, hT, S) if n % 2 else columns_product(pe, n, w, hT, (0, P))
                    mm.then_inc(bank_full.sem, 1)
                    release_unit(bank_full, n + 1)
                two_halves(pe, count, pairs, range(ND))
                end(pe)

            @block.scalar
            def _(act):
                begin(act)
                for n in range(ND):
                    src = bass.AP(table_dram.tensor, (1 + n) * TABLE_SKEW + P - 1, [[SPAN, P], [HEAD_SKEW, QH], [1, S]])
                    act.dma_start(d_table[:, n], src).then_inc(table_load.sem, 16)
                for n in range(count):
                    make_high(act, n0 + n + HIGH_SLOTS)
                    act.wait_ge(bank_full.sem, bank_full.at(n + 1))
                    dst = d_v[:, n // 2] if n % 2 else pairs[:, n // 2]
                    act.activation(dst.rearrange("p a s -> p (a s)"), bank(n % 4), ACT.Copy).then_inc(bank_free.sem, 1)
                act.wait_ge(bank_free.sem, bank_free.at(count))
                nc.scalar.nop().then_inc(inner_ready.sem, 1)
                for m in range(2 * ND):
                    n = count + m
                    i, gp = m // 2, m % 2
                    act.wait_ge(bank_full.sem, bank_full.at(n + 1))
                    act.activation(d_k[:, i, 2 * gp:2 * gp + 2, :], bank(n % 4).rearrange("p (j s) -> p j s", j=2),
                                   ACT.Copy).then_inc(bank_free.sem, 1)
                make_high(act, n0 + count + HIGH_SLOTS)
                end(act)

            @block.vector
            def _(dve):
                begin(dve)
                make_lows(dve, n0 + count)
                end(dve)

            bank_full.close(4 * ND)
            bank_free.close(4 * ND)
            inner_ready.close(1)
            close_stage()

        def dilated_attention_layer():
            n0, count = len(stream.freed), 4 * ND

            @block.tensor
            def _(pe):
                for n in range(count):
                    columns_product(pe, n, take_unit(pe, n0 + n), hT, (0, P)).then_inc(bank_full.sem, 1)
                    release_unit(bank_full, n + 1)
                end(pe)

            @block.scalar
            def _(act):
                begin(act)
                for n in range(count):
                    make_high(act, n0 + n + HIGH_SLOTS)
                    act.wait_ge(bank_full.sem, bank_full.at(n + 1))
                    act.activation(d_q[:, 2 * n:2 * n + 2, :].rearrange("p a s -> p (a s)"), bank(n % 4), ACT.Copy) \
                       .then_inc(bank_free.sem, 1)
                make_high(act, n0 + count + HIGH_SLOTS)
                end(act)

            @block.vector
            def _(dve):
                begin(dve)
                make_lows(dve, n0 + count)
                dve.wait_ge(table_load.sem, table_load.at(16 * ND))
                end(dve)

            bank_full.close(4 * ND)
            bank_free.close(4 * ND)
            table_load.close(16 * ND)
            close_stage()

            sbuf_s = region(d_rest, 2, 768)
            sbuf_p = region(d_rest + 1536, 2, 768)
            sbuf_t = region(d_rest + 3072, 2, 512)
            o = over("dilated_rows", at_h, 0, [TT, D], F32)
            oT = [over(f"dilated_columns{i}", at_work, i * KT * S, [KT, S]) for i in range(2)]
            sets = tuple(range(ND))
            units = [(t, (h,), sets) for h in range(QH) for t in (1, 0)]

            def bias(u, unit, sc, dst, L):
                t, heads, _ = unit
                yield (sc.rearrange("p (n s) -> p n s", n=ND), dst.rearrange("p (n s) -> p n s", n=ND),
                       d_table[:, :, heads[0], S - L:S])

            def finish(dve, u, unit, res, rec):
                t, heads, _ = unit
                h = heads[0]
                dve.tensor_scalar(o[:, t, h * DH:(h + 1) * DH], res, rec, None, ALU.mult).then_inc(context_read.sem, 1)

            attention(units,
                      lambda h, st, t: d_q[DH * (h % 2):DH * (h % 2) + DH, st * KT + h // 2, t * P:(t + 1) * P],
                      lambda h, st: d_k[DH * (h % 2):DH * (h % 2) + DH, st, h // PER_GROUP, :],
                      lambda st, kt, h: d_v[:, st, kt, (h // PER_GROUP) * DH:(h // PER_GROUP + 1) * DH],
                      bias, DH ** -0.5, DH, (sbuf_s, sbuf_p, sbuf_t), finish)
            turn_rows(lambda t, j: o[:, t, j * P:(j + 1) * P], oT, KT)
            add_rows_product(oT, KT)

        def output_stage():
            xn = region(0, TT, D)
            gain = region(2048, D)

            @block.scalar
            def _(act):
                begin(act)
                act.dma_start(gain, a["final_norm_2"].partition_broadcast(P)).then_inc(side_load.sem, 16)
                square_root(act, stat[:, 6:6 + TT], stat[:, 8:8 + TT], 1)
                for t in range(TT):
                    act.wait_ge(rows_scaled.sem, rows_scaled.at(t + 1))
                    act.dma_start(out[0, t * P:(t + 1) * P, :], xn[:, t, :]).then_inc(stored, 16)
                act.wait_ge(stored, 16 * TT)

            @block.vector
            def _(dve):
                begin(dve)
                inverse_root(dve, stat[:, 4:4 + TT], stat[:, 6:6 + TT], stat[:, 8:8 + TT], stat[:, 0:TT], 1.0 / D, 1)
                dve.wait_ge(side_load.sem, side_load.at(16))
                for t in range(TT):
                    dve.scalar_tensor_tensor(xn[:, t, :], x[:, t, :], stat[:, 4 + t:5 + t], gain, ALU.mult, ALU.mult) \
                       .then_inc(rows_scaled.sem, 1)

        def weight_stream():
            assert len(stream.freed) == len(stream.units) == stream.high

            @block.sync
            def _(sp):
                for n, (src, kt, cols, _) in enumerate(stream.units):
                    if n >= RAW_SLOTS:
                        sp.wait_ge(*stream.low[n - RAW_SLOTS])
                    sp.dma_start(part(raw, n, RAW_SLOTS).rearrange("p (k c) -> p k c", k=kt),
                                 src.rearrange("(k p) c -> p k c", p=P)).then_inc(raw_landed[n % RAW_SLOTS], 16)

            @block.gpsimd
            def _(pool):
                for n, unit in enumerate(stream.units):
                    if unit[3] == "P":
                        make_low(pool, n)

        def col(base):
            return lambda k: par[:, base + k:base + k + 1]

        setup_stage()
        for l in range(DEPTH):
            norm_stage(col(R_MISC(l) + M_MIX))
            mixer_rows_stage(l)
            mixer_columns_stage(l)
            mixer_turn_stage(l)
            gates_stage(l)
            sparse_attention_stage(l)
            stick_breaking_stage()
            branch_output_stage()
            add_rows_product(mT, KT)
            norm_stage(col(R_MISC(l) + M_FFN))
            ffn_up_stage(lambda k, j, l=l: par[:, R_FFC(l) + FT * k + j:R_FFC(l) + FT * k + j + 1])
            add_rows_product(fT, FT)
        for l in range(2):
            if l == 0:
                norm_stage(col(R_PART2 + M2_MIX))
                compressed_attention_layer()
            else:
                norm_stage(col(R_PART2 + M2_KV))
                shared_keys_stage()
                norm_stage(col(R_PART2 + M2_MIX + KT), d_rest)
                dilated_attention_layer()
            norm_stage(col(R_PART2 + M2_FFN + KT * l))
            ffn_up_stage(None)
            add_rows_product(fT, FT)
        output_stage()
        weight_stream()


_INS = ["x", "positions", "g_mix", "w_in", "b_gate", "g_qa", "g_ka", "g_kidx", "w_oa", "cb_conv_w", "cb_conv_b",
        "cb_ln_g", "cb_ln_b", "w_ob", "cc_conv_w", "w_oc", "w_od", "w_merge", "g_ffn", "w_ffn_gate", "w_ffn_up",
        "ffn_conv_w", "w_ffn_down", "rel_bias_2", "norm_mix_2", "norm_ffn_2", "a_w_in_2", "a_b_gate_2", "a_pe_k_2",
        "a_w1_k_2", "a_w2_k_2", "a_pe_v_2", "a_w1_v_2", "a_w2_v_2", "a_w_out_2", "kv_norm_2", "kv_w_2", "b_w_q_2",
        "b_w_out_2", "ffn_w_up_2", "ffn_w_down_2", "final_norm_2"]


def kernel(**inputs):
    import numpy as _np
    import concourse.bacc as _bacc
    from concourse import mybir as _mybir
    from concourse.bass_utils import run_bass_kernel_spmd as _run

    nc = _bacc.Bacc("TRN2", target_bir_lowering=False, num_devices=1)
    arrays, aps = {}, {}
    for name in _INS:
        v = _np.ascontiguousarray(inputs[name])
        arrays[f"in_{name}"] = v
        aps[name] = nc.dram_tensor(f"in_{name}", v.shape, _mybir.dt.from_np(v.dtype), kind="ExternalInput").ap()
    extra = []
    for name, v in (("shape_constants", shape_constants()), ("distance_tables", distance_tables())):
        arrays[f"in_{name}"] = v
        extra.append(nc.dram_tensor(f"in_{name}", v.shape, F32, kind="ExternalInput").ap())
    out = nc.dram_tensor("out_dram", [1, S, D], F32, kind="ExternalOutput").ap()
    two_part_transformer(nc, aps, extra[0], extra[1], out)
    r = _run(nc, [arrays], core_ids=[0])
    return r.results[0]["out_dram"]
```
